# Optimizing a Trainium2 kernel written in Bass

```python
import jax, jax.numpy as jnp
from jax import lax
import numpy as np
import math

D_MODEL = 1024
BATCH = 1
SEQ = 256
DEPTH = 2

HEAD_DIM = 64
A_HEADS = 8
B_HEADS = 8
M_HEADS = 4
M_HEAD_DIM = 128
BRANCH_WIDTH = 512
N_BRANCH = 3
MOBA_BLOCK = 256
MOBA_TOPK = 3
IDX_HEADS = 8
IDX_DIM = 64
IDX_TOPK_MAX = 256
N_MEM = 256
ROPE_THETA = 500000.0
ROT_FRACTION = 4
Q_BLOCK = 128
RMS_EPS = 1e-6
IN_WIDTHS = (
    BRANCH_WIDTH, BRANCH_WIDTH, BRANCH_WIDTH, BRANCH_WIDTH,
    BRANCH_WIDTH, BRANCH_WIDTH, BRANCH_WIDTH, BRANCH_WIDTH,
    IDX_HEADS * IDX_DIM, IDX_DIM, IDX_HEADS,
    BRANCH_WIDTH, BRANCH_WIDTH,
    N_BRANCH * D_MODEL,
)
IN_COLS = sum(IN_WIDTHS)


def rmsnorm(x, g):
    xf = x.astype(jnp.float32)
    y = xf * lax.rsqrt(jnp.mean(xf * xf, axis=-1, keepdims=True) + RMS_EPS)
    return (y * g.astype(jnp.float32)).astype(x.dtype)

def partial_rope(x, pos):
    d = x.shape[-1]
    rot = d // ROT_FRACTION
    half = rot // 2
    inv_freq = ROPE_THETA ** (-jnp.arange(half, dtype=jnp.float32) / half)
    ang = pos.astype(jnp.float32)[:, None] * inv_freq[None, :]
    cos = jnp.cos(ang)[:, None, :].astype(x.dtype)
    sin = jnp.sin(ang)[:, None, :].astype(x.dtype)
    x1 = x[..., :half]
    x2 = x[..., half:rot]
    return jnp.concatenate([x1 * cos - x2 * sin, x2 * cos + x1 * sin, x[..., rot:]], axis=-1)

def masked_softmax(s, mask):
    s = jnp.where(mask, s.astype(jnp.float32), -jnp.inf)
    return jax.nn.softmax(s, axis=-1)

def moba_attention(q, k, v):
    b, s, h, d = q.shape
    nb = -(-s // MOBA_BLOCK)
    pad = nb * MOBA_BLOCK - s
    padw = ((0, 0), (0, pad), (0, 0), (0, 0))
    kb = jnp.pad(k, padw).reshape(b, nb, MOBA_BLOCK, h, d).transpose(0, 3, 1, 2, 4)
    vb = jnp.pad(v, padw).reshape(b, nb, MOBA_BLOCK, h, d).transpose(0, 3, 1, 2, 4)
    kmean = jnp.mean(kb.astype(jnp.float32), axis=3).astype(q.dtype)
    kk = min(MOBA_TOPK, nb - 1)
    scale = d ** -0.5
    b_idx = jnp.arange(b)[:, None, None, None]
    h_idx = jnp.arange(h)[None, :, None, None]
    blk_ids = jnp.arange(nb)

    def one_block(qi):
        start = qi * Q_BLOCK
        own = start // MOBA_BLOCK
        qpos = start + jnp.arange(Q_BLOCK)
        qb = lax.dynamic_slice_in_dim(q, start, Q_BLOCK, axis=1).transpose(0, 2, 1, 3)
        k_own = lax.dynamic_index_in_dim(kb, own, axis=2, keepdims=False)
        v_own = lax.dynamic_index_in_dim(vb, own, axis=2, keepdims=False)
        kpos_own = own * MOBA_BLOCK + jnp.arange(MOBA_BLOCK)
        s_own = jnp.einsum('bhqd,bhkd->bhqk', qb, k_own) * scale
        m_own = jnp.broadcast_to(kpos_own[None, :] <= qpos[:, None], s_own.shape)
        if kk == 0:
            p = masked_softmax(s_own, m_own).astype(v.dtype)
            o = jnp.einsum('bhqk,bhkd->bhqd', p, v_own)
        else:
            gate = jnp.einsum('bhqd,bhnd->bhqn', qb, kmean).astype(jnp.float32)
            gate = jnp.where(blk_ids < own, gate, -jnp.inf)
            _, sel = lax.top_k(gate, kk)
            valid = sel < own
            kg = kb[b_idx, h_idx, sel]
            vg = vb[b_idx, h_idx, sel]
            s_past = jnp.einsum('bhqd,bhqjkd->bhqjk', qb, kg) * scale
            m_past = jnp.broadcast_to(valid[..., None], s_past.shape)
            n_past = kk * MOBA_BLOCK
            s_all = jnp.concatenate([s_past.reshape(b, h, Q_BLOCK, n_past), s_own], axis=-1)
            m_all = jnp.concatenate([m_past.reshape(b, h, Q_BLOCK, n_past), m_own], axis=-1)
            p = masked_softmax(s_all, m_all).astype(v.dtype)
            p_past = p[..., :n_past].reshape(b, h, Q_BLOCK, kk, MOBA_BLOCK)
            o = (jnp.einsum('bhqjk,bhqjkd->bhqd', p_past, vg)
                 + jnp.einsum('bhqk,bhkd->bhqd', p[..., n_past:], v_own))
        return o.transpose(0, 2, 1, 3)

    out = lax.map(one_block, jnp.arange(s // Q_BLOCK))
    return out.transpose(1, 0, 2, 3, 4).reshape(b, s, h, d)

def dsa_attention(q, k, v, qi, ki, wi):
    b, s, h, d = q.shape
    n_sel = min(IDX_TOPK_MAX, s // 4)
    scale = d ** -0.5
    kpos = jnp.arange(s)
    b_idx = jnp.arange(b)[:, None, None]

    def one_block(blk):
        start = blk * Q_BLOCK
        qpos = start + jnp.arange(Q_BLOCK)
        q_b = lax.dynamic_slice_in_dim(q, start, Q_BLOCK, axis=1)
        qi_b = lax.dynamic_slice_in_dim(qi, start, Q_BLOCK, axis=1)
        wi_b = lax.dynamic_slice_in_dim(wi, start, Q_BLOCK, axis=1)
        rel = jax.nn.relu(jnp.einsum('bqhd,bsd->bqhs', qi_b, ki))
        idx_score = jnp.einsum('bqhs,bqh->bqs', rel, wi_b).astype(jnp.float32)
        idx_score = jnp.where(kpos[None, :] <= qpos[:, None], idx_score, -jnp.inf)
        _, sel = lax.top_k(idx_score, n_sel)
        valid = sel <= qpos[None, :, None]
        kg = k[b_idx, sel]
        vg = v[b_idx, sel]
        sc = jnp.einsum('bqhd,bqnhd->bqhn', q_b, kg) * scale
        p = masked_softmax(sc, valid[:, :, None, :]).astype(v.dtype)
        return jnp.einsum('bqhn,bqnhd->bqhd', p, vg)

    out = lax.map(one_block, jnp.arange(s // Q_BLOCK))
    return out.transpose(1, 0, 2, 3, 4).reshape(b, s, h, d)

def memory_attention(qm, km, vm):
    sc = jnp.einsum('bshd,bmhd->bhsm', qm, km) * (qm.shape[-1] ** -0.5)
    p = jax.nn.softmax(sc.astype(jnp.float32), axis=-1).astype(vm.dtype)
    return jnp.einsum('bhsm,bmhd->bshd', p, vm)

def hybrid_layer(x, mem, pos, norm_g, w_in, mem_norm_g, w_mem_kv, w_branch, w_out):
    b, s, _ = x.shape
    h = rmsnorm(x, norm_g)
    proj = jnp.einsum('bsd,dc->bsc', h, w_in)
    offs = np.cumsum(IN_WIDTHS)[:-1].tolist()
    (a_q, a_k, a_v, a_g, b_q, b_k, b_v, b_g,
     i_q, i_k, i_w, m_q, m_g, mix) = jnp.split(proj, offs, axis=-1)

    qa = partial_rope(a_q.reshape(b, s, A_HEADS, HEAD_DIM), pos)
    ka = partial_rope(a_k.reshape(b, s, A_HEADS, HEAD_DIM), pos)
    va = a_v.reshape(b, s, A_HEADS, HEAD_DIM)
    ya = moba_attention(qa, ka, va).reshape(b, s, BRANCH_WIDTH) * jax.nn.silu(a_g)

    qb = partial_rope(b_q.reshape(b, s, B_HEADS, HEAD_DIM), pos)
    kb = partial_rope(b_k.reshape(b, s, B_HEADS, HEAD_DIM), pos)
    vb = b_v.reshape(b, s, B_HEADS, HEAD_DIM)
    qi = partial_rope(i_q.reshape(b, s, IDX_HEADS, IDX_DIM), pos) * (IDX_DIM ** -0.5)
    ki = partial_rope(i_k[:, :, None, :], pos)[:, :, 0, :]
    wi = i_w * (IDX_HEADS ** -0.5)
    yb = dsa_attention(qb, kb, vb, qi, ki, wi).reshape(b, s, BRANCH_WIDTH) * jax.nn.silu(b_g)

    mn = rmsnorm(mem, mem_norm_g)
    km, vm = jnp.split(jnp.einsum('bmd,dc->bmc', mn, w_mem_kv), 2, axis=-1)
    km = km.reshape(b, -1, M_HEADS, M_HEAD_DIM)
    vm = vm.reshape(b, -1, M_HEADS, M_HEAD_DIM)
    ym = memory_attention(m_q.reshape(b, s, M_HEADS, M_HEAD_DIM), km, vm)
    ym = ym.reshape(b, s, BRANCH_WIDTH) * jax.nn.silu(m_g)

    ys = jnp.stack([ya, yb, ym], axis=2)
    up = jnp.einsum('bsnw,nwd->bsnd', ys, w_branch)
    gates = jax.nn.sigmoid(mix.reshape(b, s, N_BRANCH, D_MODEL))
    merged = jnp.sum(gates * up, axis=2)
    return x + jnp.einsum('bsd,de->bse', merged, w_out)

def first_inputs(seed: int = 0) -> dict:
    key = jax.random.key(seed)
    ks = jax.random.split(key, 9)
    f32 = jnp.float32
    x = jax.random.normal(ks[0], (BATCH, SEQ, D_MODEL), f32)
    mem = jax.random.normal(ks[1], (BATCH, N_MEM, D_MODEL), f32)
    norm_g = 1.0 + 0.02 * jax.random.normal(ks[2], (DEPTH, D_MODEL), f32)
    w_in = jax.random.normal(ks[3], (DEPTH, D_MODEL, IN_COLS), f32) * (D_MODEL ** -0.5)
    mem_norm_g = 1.0 + 0.02 * jax.random.normal(ks[4], (DEPTH, D_MODEL), f32)
    w_mem_kv = jax.random.normal(ks[5], (DEPTH, D_MODEL, 2 * BRANCH_WIDTH), f32) * (D_MODEL ** -0.5)
    w_branch = jax.random.normal(ks[6], (DEPTH, N_BRANCH, BRANCH_WIDTH, D_MODEL), f32) * (BRANCH_WIDTH ** -0.5)
    w_out = jax.random.normal(ks[7], (DEPTH, D_MODEL, D_MODEL), f32) * (D_MODEL ** -0.5)
    final_g = 1.0 + 0.02 * jax.random.normal(ks[8], (D_MODEL,), f32)
    return {'x': x, 'mem': mem, 'norm_g': norm_g, 'w_in': w_in, 'mem_norm_g': mem_norm_g,
            'w_mem_kv': w_mem_kv, 'w_branch': w_branch, 'w_out': w_out, 'final_g': final_g}

def first_block(x, mem, norm_g, w_in, mem_norm_g, w_mem_kv, w_branch, w_out, final_g):
    pos = jnp.arange(x.shape[1], dtype=jnp.int32)
    for l in range(DEPTH):
        x = hybrid_layer(x, mem, pos, norm_g[l], w_in[l], mem_norm_g[l], w_mem_kv[l],
                         w_branch[l], w_out[l])
    return rmsnorm(x, final_g)


GRID_W = 64
CTX_LEN = 256
N_MIXERS = 3
N_MOD = 9
D_FF = 2816
MACARON_W = 0.5
NORM_EPS = 1e-6
NEG_INF = -1e9

DA_HEADS = 8
DA_HEAD_DIM = 64
DA_Q_BLOCK = 128
ROPE_BASE = 10000.0
ROPE_PAIRS = DA_HEAD_DIM // 4

NA_HEADS = 16
NA_HEAD_DIM = D_MODEL // NA_HEADS
NA_ROWS = 8
NA_COLS = 16

RW_HEAD = 64
RW_HEADS = D_MODEL // RW_HEAD
RW_DECAY_LORA = 64
RW_AAA_LORA = 64
RW_GATE_LORA = 160
RW_LN_EPS = 64e-5


def _rmsnorm(h, g):
    hf = h.astype(jnp.float32)
    hf = hf * lax.rsqrt(jnp.mean(hf * hf, axis=-1, keepdims=True) + NORM_EPS)
    return hf.astype(h.dtype) * g

def _modulate(h, shift, scale):
    return h * (1 + scale) + shift

def _ffn_sublayer(h, mod, g_pre, g_post, w_in, w_out):
    shift, scale, gate = mod
    u = _modulate(_rmsnorm(h, g_pre), shift, scale)
    a, b = jnp.split(u @ w_in, 2, axis=-1)
    y = (jax.nn.silu(a) * b) @ w_out
    return h + MACARON_W * gate * _rmsnorm(y, g_post)

def _axial_rope_tables(seq_len):
    t = jnp.arange(seq_len)
    pos = jnp.stack([t // GRID_W, t % GRID_W], axis=-1).astype(jnp.float32)
    freq = ROPE_BASE ** (-jnp.arange(ROPE_PAIRS, dtype=jnp.float32) / ROPE_PAIRS)
    ang = pos[:, :, None] * freq
    return jnp.cos(ang), jnp.sin(ang)

def _axial_rope(x, cos, sin):
    d = x.shape[-1]
    xr = x.reshape(x.shape[:-1] + (2, 2, d // 4))
    x1, x2 = xr[..., 0, :], xr[..., 1, :]
    bshape = (cos.shape[0],) + (1,) * (x.ndim - 3) + (2, d // 4)
    c = cos.reshape(bshape).astype(x.dtype)
    s = sin.reshape(bshape).astype(x.dtype)
    return jnp.stack([x1 * c - x2 * s, x2 * c + x1 * s], axis=-2).reshape(x.shape)

def _attend(q, k, v):
    s = jnp.einsum('bthd,bkhd->bhtk', q, k).astype(jnp.float32)
    p = jax.nn.softmax(s, axis=-1).astype(v.dtype)
    return jnp.einsum('bhtk,bkhd->bthd', p, v)

def _diff_attend(q, k, v, lam):
    s = jnp.einsum('bthjd,bkhjd->bhjtk', q, k).astype(jnp.float32)
    p = jax.nn.softmax(s, axis=-1)
    p = p[:, :, 0] - lam.astype(jnp.float32) * p[:, :, 1]
    return jnp.einsum('bhtk,bkhe->bthe', p.astype(v.dtype), v)

def _diff_attention(uc, ux, w_in, w_out, lam_vec, subln_g, lam_init, cos, sin, need_ctx):
    B, S, D = ux.shape
    H, d = DA_HEADS, DA_HEAD_DIM

    def proj(u):
        L = u.shape[1]
        q, k, v = jnp.split(u @ w_in, 3, axis=-1)
        return (q.reshape(B, L, H, 2, d) * d ** -0.5, k.reshape(B, L, H, 2, d), v.reshape(B, L, H, 2 * d))

    qc, kc, vc = proj(uc)
    qx, kx, vx = proj(ux)
    qx = _axial_rope(qx, cos, sin)
    kx = _axial_rope(kx, cos, sin)
    lam = (jnp.exp(jnp.sum(lam_vec[0] * lam_vec[1])) - jnp.exp(jnp.sum(lam_vec[2] * lam_vec[3]))
           + lam_init)
    k_all = jnp.concatenate([kc, kx], axis=1)
    v_all = jnp.concatenate([vc, vx], axis=1)
    nb = S // DA_Q_BLOCK
    qb = jnp.moveaxis(qx.reshape(B, nb, DA_Q_BLOCK, H, 2, d), 1, 0)
    ox = lax.map(lambda q: _diff_attend(q, k_all, v_all, lam), qb)
    ox = jnp.moveaxis(ox, 0, 1).reshape(B, S, H, 2 * d)

    def out(o):
        o = _rmsnorm(o, subln_g) * (1 - lam_init)
        return o.reshape(o.shape[0], o.shape[1], H * 2 * d) @ w_out

    yx = out(ox)
    yc = out(_diff_attend(qc, kc, vc, lam)) if need_ctx else None
    return yc, yx

def _neighbourhood_attention(uc, ux, w_in, w_out, rpb, need_ctx):
    B, S, D = ux.shape
    C = uc.shape[1]
    H, d = NA_HEADS, NA_HEAD_DIM
    rows = S // GRID_W
    kr = min(NA_ROWS, rows)

    def proj(u):
        L = u.shape[1]
        q, k, v = jnp.split(u @ w_in, 3, axis=-1)
        return q.reshape(B, L, H, d) * d ** -0.5, k.reshape(B, L, H, d), v.reshape(B, L, H, d)

    qc, kc, vc = proj(uc)
    qx, kx, vx = proj(ux)
    q_grid = qx.reshape(B, rows, GRID_W, H, d)
    k_grid = kx.reshape(B, rows, GRID_W, H, d)
    v_grid = vx.reshape(B, rows, GRID_W, H, d)
    col = jnp.arange(GRID_W)
    col_start = jnp.clip(col - NA_COLS // 2, 0, GRID_W - NA_COLS)
    col_in = (col[None, :] >= col_start[:, None]) & (col[None, :] < col_start[:, None] + NA_COLS)
    col_off = jnp.clip(col[None, :] - col[:, None] + NA_COLS - 1, 0, 2 * NA_COLS - 2)
    col_bias = jnp.where(col_in, rpb[:, :, col_off].astype(jnp.float32), NEG_INF)

    def row_block(r):
        rs = jnp.clip(r - kr // 2, 0, rows - kr)
        q = lax.dynamic_index_in_dim(q_grid, r, axis=1, keepdims=False)
        kb = lax.dynamic_slice_in_dim(k_grid, rs, kr, axis=1)
        vb = lax.dynamic_slice_in_dim(v_grid, rs, kr, axis=1)
        bias = jnp.swapaxes(col_bias[:, rs + jnp.arange(kr) - r + NA_ROWS - 1], 1, 2)
        s_lat = jnp.einsum('bqhd,brkhd->bhqrk', q, kb).astype(jnp.float32) + bias
        s_ctx = jnp.einsum('bqhd,bchd->bhqc', q, kc).astype(jnp.float32)
        s = jnp.concatenate([s_ctx, s_lat.reshape(B, H, GRID_W, kr * GRID_W)], axis=-1)
        p = jax.nn.softmax(s, axis=-1).astype(vx.dtype)
        p_ctx = p[..., :C]
        p_lat = p[..., C:].reshape(B, H, GRID_W, kr, GRID_W)
        return (jnp.einsum('bhqc,bchd->bqhd', p_ctx, vc)
                + jnp.einsum('bhqrk,brkhd->bqhd', p_lat, vb))

    ox = lax.map(row_block, jnp.arange(rows))
    yx = jnp.moveaxis(ox, 0, 1).reshape(B, S, D) @ w_out
    yc = _attend(qc, kc, vc).reshape(B, C, D) @ w_out if need_ctx else None
    return yc, yx

def _rwkv7_prep(u, mu, w_in, w0, w1, w2, a0, a1, a2, g1, g2, k_k, k_a):
    B, L, D = u.shape
    H, N = RW_HEADS, RW_HEAD
    f32 = jnp.float32
    zero = jnp.zeros_like(u[:, :1])
    xx = 0.5 * (jnp.concatenate([zero, u[:, :-1]], axis=1) + jnp.concatenate([u[:, 1:], zero], axis=1)) - u
    xr, xw, xk, xv, xa, xg = [u + xx * mu[j] for j in range(6)]
    w_r, w_k, w_v = jnp.split(w_in, 3, axis=1)
    r = xr @ w_r
    k = xk @ w_k
    v = xv @ w_v
    lora_w = jnp.einsum('zblr,zrd->zbld', jnp.tanh(jnp.einsum('bld,zdr->zblr', xw, w1)), w2)
    w_log = -jax.nn.softplus(-(w0[:, None, None, :] + lora_w).astype(f32)) - 0.5
    decay = jnp.exp(-jnp.exp(w_log))
    a = jax.nn.sigmoid(a0[:, None, None, :]
                       + jnp.einsum('zblr,zrd->zbld', jnp.einsum('bld,zdr->zblr', xa, a1), a2))
    g = jax.nn.sigmoid(xg @ g1) @ g2
    kk = (k * k_k).reshape(B, L, H, N).astype(f32)
    kk = kk / jnp.maximum(jnp.linalg.norm(kk, axis=-1, keepdims=True), 1e-12)
    kd = k[None] * (1 + (a - 1) * k_a)

    def heads(t):
        return t.reshape(t.shape[:-1] + (H, N)).astype(f32)

    def two(t):
        return jnp.broadcast_to(t, (2,) + t.shape)

    def orient(t):
        t = jnp.stack([t[0], jnp.flip(t[1], axis=1)])
        return jnp.moveaxis(t, 2, 0)

    scan_in = (orient(two(heads(r))), orient(heads(decay)), orient(heads(kd)),
               orient(two(heads(v))), orient(two(-kk)), orient(kk[None] * heads(a)))
    return scan_in, (r, kd, v, g)

def _wkv7_scan(state0, r, w, k, v, a, b):
    def step(S, inp):
        rt, wt, kt, vt, at, bt = inp
        sa = jnp.einsum('zbhvk,zbhk->zbhv', S, at)
        S = S * wt[..., None, :] + sa[..., :, None] * bt[..., None, :] + vt[..., :, None] * kt[..., None, :]
        return S, jnp.einsum('zbhvk,zbhk->zbhv', S, rt)
    return lax.scan(step, state0, (r, w, k, v, a, b))

def _rwkv7_readout(y, r, kd, v, g, r_k, ln_g, ln_b, w_out):
    B, L, D = r.shape
    H, N = RW_HEADS, RW_HEAD
    y = jnp.moveaxis(y, 0, 2)
    y = y[0] + jnp.flip(y[1], axis=1)
    mean = jnp.mean(y, axis=-1, keepdims=True)
    var = jnp.mean(jnp.square(y - mean), axis=-1, keepdims=True)
    y = ((y - mean) * lax.rsqrt(var + RW_LN_EPS)).reshape(B, L, D).astype(r.dtype) * ln_g + ln_b
    rh = r.reshape(B, L, H, N)
    kh = (kd[0] + kd[1]).reshape(B, L, H, N)
    bonus = jnp.sum(rh * kh * r_k, axis=-1, keepdims=True) * v.reshape(B, L, H, N)
    return ((y + bonus.reshape(B, L, D)) * g) @ w_out

def _rwkv7_mixer(uc, ux, mu, w_in, w_out, w0, w1, w2, a0, a1, a2, g1, g2, k_k, k_a, r_k,
                 ln_g, ln_b, need_ctx):
    B = ux.shape[0]
    in_c, aux_c = _rwkv7_prep(uc, mu, w_in, w0, w1, w2, a0, a1, a2, g1, g2, k_k, k_a)
    in_x, aux_x = _rwkv7_prep(ux, mu, w_in, w0, w1, w2, a0, a1, a2, g1, g2, k_k, k_a)
    s0 = jnp.zeros((2, B, RW_HEADS, RW_HEAD, RW_HEAD), jnp.float32)
    s_ctx, y_c = _wkv7_scan(s0, *in_c)
    _, y_x = _wkv7_scan(s_ctx, *in_x)
    yx = _rwkv7_readout(y_x, *aux_x, r_k, ln_g, ln_b, w_out)
    yc = _rwkv7_readout(y_c, *aux_c, r_k, ln_g, ln_b, w_out) if need_ctx else None
    return yc, yx

def second_inputs(seed: int = 0) -> dict:
    key = jax.random.key(seed)
    ks = iter(jax.random.split(key, 48))
    f32 = jnp.float32
    D, F = D_MODEL, D_FF
    n_a, n_b, n_c = [len(range(m, DEPTH, N_MIXERS)) for m in range(N_MIXERS)]

    def nrm(shape, scale):
        return jax.random.normal(next(ks), shape, f32) * scale

    def gain(shape):
        return 1.0 + nrm(shape, 0.05)

    return {
        'x': nrm((BATCH, SEQ, D), 1.0),
        'c': nrm((BATCH, D), 1.0),
        'ctx': nrm((BATCH, CTX_LEN, D), 1.0),
        'c_ctx': nrm((D,), 1.0),
        'ada_w': nrm((DEPTH, D, N_MOD * D), 0.5 * D ** -0.5),
        'ada_b': nrm((DEPTH, N_MOD * D), 0.02),
        'norm_g': gain((DEPTH, 6, D)),
        'ffn_w_in': nrm((DEPTH, 2, D, 2 * F), D ** -0.5),
        'ffn_w_out': nrm((DEPTH, 2, F, D), F ** -0.5),
        'da_w_in': nrm((n_a, D, 3 * D), D ** -0.5),
        'da_w_out': nrm((n_a, D, D), D ** -0.5),
        'da_lambda': nrm((n_a, 4, DA_HEAD_DIM), 0.1),
        'da_subln_g': gain((n_a, 2 * DA_HEAD_DIM)),
        'na_w_in': nrm((n_b, D, 3 * D), D ** -0.5),
        'na_w_out': nrm((n_b, D, D), D ** -0.5),
        'na_rpb': nrm((n_b, NA_HEADS, 2 * NA_ROWS - 1, 2 * NA_COLS - 1), 0.2),
        'rw_mu': jax.random.uniform(next(ks), (n_c, 6, D), f32),
        'rw_w_in': nrm((n_c, D, 3 * D), D ** -0.5),
        'rw_w_out': nrm((n_c, D, D), D ** -0.5),
        'rw_w0': jax.random.uniform(next(ks), (n_c, 2, D), f32, -6.0, -1.0),
        'rw_w1': nrm((n_c, 2, D, RW_DECAY_LORA), D ** -0.5),
        'rw_w2': nrm((n_c, 2, RW_DECAY_LORA, D), 0.1 * RW_DECAY_LORA ** -0.5),
        'rw_a0': nrm((n_c, 2, D), 0.1),
        'rw_a1': nrm((n_c, 2, D, RW_AAA_LORA), D ** -0.5),
        'rw_a2': nrm((n_c, 2, RW_AAA_LORA, D), RW_AAA_LORA ** -0.5),
        'rw_g1': nrm((n_c, D, RW_GATE_LORA), D ** -0.5),
        'rw_g2': nrm((n_c, RW_GATE_LORA, D), RW_GATE_LORA ** -0.5),
        'rw_k_k': 0.85 + nrm((n_c, D), 0.05),
        'rw_k_a': gain((n_c, D)),
        'rw_r_k': nrm((n_c, RW_HEADS, RW_HEAD), 0.1),
        'rw_ln_g': gain((n_c, D)),
        'rw_ln_b': nrm((n_c, D), 0.02),
    }

def second_block(x, c, ctx, c_ctx, ada_w, ada_b, norm_g, ffn_w_in, ffn_w_out,
              da_w_in, da_w_out, da_lambda, da_subln_g,
              na_w_in, na_w_out, na_rpb,
              rw_mu, rw_w_in, rw_w_out, rw_w0, rw_w1, rw_w2, rw_a0, rw_a1, rw_a2,
              rw_g1, rw_g2, rw_k_k, rw_k_a, rw_r_k, rw_ln_g, rw_ln_b):
    B, S, D = x.shape
    cos, sin = _axial_rope_tables(S)
    hx, hc = x, ctx
    silu_c, silu_cc = jax.nn.silu(c), jax.nn.silu(c_ctx)
    for i in range(DEPTH):
        last = i == DEPTH - 1
        kind, slot = i % N_MIXERS, i // N_MIXERS
        g = norm_g[i]
        mx = (silu_c @ ada_w[i] + ada_b[i]).reshape(B, N_MOD, 1, D)
        mc = (silu_cc @ ada_w[i] + ada_b[i]).reshape(N_MOD, D)

        hx = _ffn_sublayer(hx, (mx[:, 0], mx[:, 1], mx[:, 2]), g[0], g[1], ffn_w_in[i, 0], ffn_w_out[i, 0])
        hc = _ffn_sublayer(hc, (mc[0], mc[1], mc[2]), g[0], g[1], ffn_w_in[i, 0], ffn_w_out[i, 0])

        ux = _modulate(_rmsnorm(hx, g[2]), mx[:, 3], mx[:, 4])
        uc = _modulate(_rmsnorm(hc, g[2]), mc[3], mc[4])
        if kind == 0:
            lam_init = 0.8 - 0.6 * math.exp(-0.3 * i)
            yc, yx = _diff_attention(uc, ux, da_w_in[slot], da_w_out[slot], da_lambda[slot],
                                     da_subln_g[slot], lam_init, cos, sin, not last)
        elif kind == 1:
            yc, yx = _neighbourhood_attention(uc, ux, na_w_in[slot], na_w_out[slot], na_rpb[slot], not last)
        else:
            yc, yx = _rwkv7_mixer(uc, ux, rw_mu[slot], rw_w_in[slot], rw_w_out[slot],
                                  rw_w0[slot], rw_w1[slot], rw_w2[slot],
                                  rw_a0[slot], rw_a1[slot], rw_a2[slot],
                                  rw_g1[slot], rw_g2[slot], rw_k_k[slot], rw_k_a[slot],
                                  rw_r_k[slot], rw_ln_g[slot], rw_ln_b[slot], not last)
        hx = hx + mx[:, 5] * _rmsnorm(yx, g[3])

        hx = _ffn_sublayer(hx, (mx[:, 6], mx[:, 7], mx[:, 8]), g[4], g[5], ffn_w_in[i, 1], ffn_w_out[i, 1])
        if not last:
            hc = hc + mc[5] * _rmsnorm(yc, g[3])
            hc = _ffn_sublayer(hc, (mc[6], mc[7], mc[8]), g[4], g[5], ffn_w_in[i, 1], ffn_w_out[i, 1])
    return hx


def setup_inputs(seed=0):
    out = dict(first_inputs(seed))
    for name, value in second_inputs(seed + 1).items():
        if name != "x":
            out[name + "_2"] = value
    return out


def reference(
    x, mem, norm_g, w_in, mem_norm_g, w_mem_kv, w_branch, w_out, final_g, c_2, ctx_2, c_ctx_2,
    ada_w_2, ada_b_2, norm_g_2, ffn_w_in_2, ffn_w_out_2, da_w_in_2, da_w_out_2, da_lambda_2,
    da_subln_g_2, na_w_in_2, na_w_out_2, na_rpb_2, rw_mu_2, rw_w_in_2, rw_w_out_2, rw_w0_2,
    rw_w1_2, rw_w2_2, rw_a0_2, rw_a1_2, rw_a2_2, rw_g1_2, rw_g2_2, rw_k_k_2, rw_k_a_2, rw_r_k_2,
    rw_ln_g_2, rw_ln_b_2,
):
    x = first_block(
        x, mem, norm_g, w_in, mem_norm_g, w_mem_kv, w_branch, w_out, final_g,
    )
    return second_block(
        x, c_2, ctx_2, c_ctx_2, ada_w_2, ada_b_2, norm_g_2, ffn_w_in_2, ffn_w_out_2, da_w_in_2,
        da_w_out_2, da_lambda_2, da_subln_g_2, na_w_in_2, na_w_out_2, na_rpb_2, rw_mu_2,
        rw_w_in_2, rw_w_out_2, rw_w0_2, rw_w1_2, rw_w2_2, rw_a0_2, rw_a1_2, rw_a2_2, rw_g1_2,
        rw_g2_2, rw_k_k_2, rw_k_a_2, rw_r_k_2, rw_ln_g_2, rw_ln_b_2,
    )


_drawn_inputs = setup_inputs


def setup_inputs(seed=0):
    import zlib

    import numpy as np

    out = dict(_drawn_inputs(seed))
    spreads = {}
    factors = {'norm_g': 4.289,
     'mem_norm_g': 8.0,
     'final_g': 9.056,
     'da_lambda_2': 2.938,
     'da_subln_g_2': 79.098,
     'na_rpb_2': 20.541,
     'ada_b_2': 3.6,
     'norm_g_2': 3.804}
    for name, (base, spread) in spreads.items():
        noise = np.random.default_rng([zlib.crc32(name.encode()), seed]).standard_normal(out[name].shape)
        drawn = base * np.exp(spread * noise) if base else spread * noise
        out[name] = __import__('jax').numpy.asarray(drawn.astype(out[name].dtype))
    for name, factor in factors.items():
        out[name] = (out[name] * factor).astype(out[name].dtype)
    return out
```

```python
import math
from contextlib import ExitStack

import numpy as np
import concourse.bass as bass
from concourse import mybir

F32 = mybir.dt.float32
F32R = mybir.dt.float32r
ACT = mybir.ActivationFunctionType
ALU = mybir.AluOpType
AX = mybir.AxisListType

P = 128
D = 1024
KT = D // P
TX = 256
TT = 2 * TX
DEPTH = 2
BW = 512
NH1 = 8
HD = 64
TOPK = 64
D_FF = 2816
FH = D_FF // P // 2
EPS = 1e-6
NEG = -1e30
TAKEN = -3e38
SLAB = KT * 256
SLAB_OUT = FH * 256
SLAB_MIX = (KT + 4) * P
LAM_INIT = 0.8 - 0.6 * math.exp(-0.3 * 0)

V_NG = 0
V_MG = V_NG + DEPTH * KT
V_FG = V_MG + DEPTH * KT
V_G2 = V_FG + KT
V_AB = V_G2 + DEPTH * 6 * KT * 2
V_SG = V_AB + DEPTH * 9 * KT * 2
V_C = V_SG + 1
V_LM = V_C + 2 * KT
NV = V_LM + 4 * HD
C_ID = 0
C_R1 = C_ID + P
C_R2 = C_R1 + 2 * TX
C_CM = C_R2 + 2 * TX
C_WM = C_CM + 2 * P
NC = C_WM + HD


class Stage:

    def __init__(self, kind, counts, last, slabs=(), src=None, T=TT, apply=None, l=0, sub=0,
                 mod=False, steps=(), which=None, units=(), groups=1, half=0):
        self.kind, self.counts, self.last, self.slabs = kind, counts, last, slabs
        self.src, self.T, self.apply, self.l, self.sub, self.mod = src, T, apply, l, sub, mod
        self.steps, self.which, self.units, self.groups = steps, which, units, groups
        self.half = half


def norm(src, T, apply, **par):
    counts = dict(sq_ready=KT, sum_ready=KT, mean_ready=1, sqrt_ready=1, rms_ready=1, scaled=KT)
    last = dict(pe="mean_ready", act="sqrt_ready", dve="rms_ready")
    if apply == "split":
        counts |= dict(u_hi_ready=KT, u_lo_ready=KT)
        last |= dict(act="u_hi_ready", dve="u_lo_ready")
    else:
        counts |= dict(x_ready=KT)
        last |= dict(dve="x_ready")
    return Stage("norm", counts, last, src=src, T=T, apply=apply, **par)


def proj(steps):
    act = sum(s[0] in ("copy", "silu", "scale", "nat", "y") for s in steps)
    rope = sum(s[0] in ("rope1", "rope2", "index") for s in steps)
    counts = dict(slab_done=len(steps), taken_act=act, taken_dve=len(steps) - act, out_dve=rope)
    last = dict(pe="slab_done")
    if act:
        last["act"] = "taken_act"
    if act < len(steps):
        last["dve"] = "out_dve" if rope else "taken_dve"
    return Stage("proj", counts, last, [SLAB] * len(steps), steps=steps)


def attn(which, units, groups):
    n = len(units)
    counts = dict(s_ready=n, negmax_ready=n, p_ready=n, p_normed=n, pt_ready=n, pt_copied=n,
                  o_ready=n, o_taken=groups, y_hi_ready=1, y_lo_ready=1)
    return Stage("attn", counts, dict(pe="o_ready", act="y_hi_ready", dve="y_lo_ready"),
                 which=which, units=units, groups=groups)


def ffn(l, sub, T):
    out = [norm("X", T, "split", l=l, sub=sub, mod=True)]
    for half in range(2):
        out.append(Stage("ffn_in", dict(slab_done=FH, silu_ready=FH, h_ready=FH, g_hi_ready=FH,
                                        g_lo_ready=FH),
                         dict(pe="slab_done", act="g_hi_ready", dve="g_lo_ready"),
                         [SLAB] * FH, T=T, half=half))
        ev = "taken_act" if half == 0 else "taken_dve"
        out.append(Stage("ffn_out", {"slab_done": 4, ev: 4},
                         {"pe": "slab_done", ("act" if half == 0 else "dve"): ev},
                         [SLAB_OUT] * 4, T=T, half=half))
    out.append(norm("Y", T, "resid", l=l, sub=sub))
    return out


def make_plan():
    plan = [Stage("setup", dict(setup_act=2, setup_dve=4), dict(act="setup_act", dve="setup_dve"))]
    for l in range(DEPTH):
        plan.append(norm("X", TT, "split", l=l, sub=0, mod=False))
        qkvg = [("rope1", "q", 2 * i, 0, TX) for i in range(2)]
        qkvg += [("rope1", "k", 2 * i, 0, TX) for i in range(2)]
        qkvg += [("nat", "v", i, 0, TX) for i in range(2)]
        qkvg += [("silu", "g", 2 * i, 0, TX) for i in range(2)]
        au = [(h, i, 0) for h in range(NH1) for i in range(2)]
        plan.append(proj(qkvg))
        plan.append(attn("a", au, 4))
        plan.append(proj([("rope1", "iq", 0, 0, TX), ("rope1", "iq", 2, 0, TX),
                          ("index", "ik", 0, 0, TX)]))
        plan.append(Stage("index", dict(is_ready=16, relu_ready=16, acc_ready=16, topk_ready=2),
                          dict(pe="is_ready", act="relu_ready", dve="topk_ready")))
        plan.append(proj(qkvg))
        plan.append(attn("b", au, 4))
        plan.append(proj([("copy", "k", 0, TX, TX), ("copy", "k", 2, TX, TX),
                          ("nat", "v", 0, TX, TX), ("nat", "v", 1, TX, TX),
                          ("copy", "q", 0, 0, TX), ("copy", "q", 2, 0, TX),
                          ("silu", "g", 0, 0, TX), ("silu", "g", 2, 0, TX)]))
        plan.append(attn("m", [(h, i, 0) for h in range(4) for i in range(2)], 4))
        plan.append(Stage("mix", dict(slab_done=24, gate_ready=24, up_taken=24, merged=24,
                                      m_hi_ready=1, m_lo_ready=1),
                          dict(pe="slab_done", act="m_hi_ready", dve="m_lo_ready"),
                          [SLAB_MIX] * 24))
        plan.append(proj([("add_x", "X", 2 * i, 0, TX) for i in range(4)]))
    plan.append(norm("X", TX, "plain", l=0, sub=0))
    plan.append(Stage("ada", dict(slab_done=72, mod_copied=2, mod_ready=28, c_ready=1, c_hi_ready=1,
                                  c_lo_ready=1),
                      dict(pe="slab_done", act="mod_copied", dve="mod_ready"), [SLAB] * 72))
    for l in range(DEPTH):
        plan += ffn(l, 0, TT)
        plan.append(norm("X", TT, "split", l=l, sub=1, mod=True))
        T = TT if l == 0 else TX
        q = "rope2" if l == 0 else "scale"
        k = "rope2" if l == 0 else "copy"
        plan.append(proj([(q, "Q", 2 * i, 0, T) for i in range(4)] +
                         [(k, "K", 2 * i, 0, TT) for i in range(4)] +
                         [("nat", "V", i, 0, TT) for i in range(4)]))
        if l == 0:
            n = 32
            plan.append(Stage("diff", dict(s_ready=n, negmax_ready=n, p_ready=n, p_normed=n,
                                           pt_ready=n, pt_copied=n, o_ready=n, o_taken=n,
                                           o_sq_ready=n, o_sqrt_ready=1, o_scaled=n, ot_ready=8,
                                           og_ready=8, y_hi_ready=8, y_lo_ready=8),
                              dict(pe="ot_ready", act="y_hi_ready", dve="y_lo_ready"),
                              units=[(h, t) for h in range(8) for t in range(4)]))
        else:
            plan.append(attn("n", [(h, i, 0) for h in range(16) for i in range(2)], 8))
        plan.append(proj([("y", "Y", 2 * i, 0, T) for i in range(4)]))
        plan.append(norm("Y", T, "resid", l=l, sub=1))
        plan += ffn(l, 2, T)
    at, last, sizes = {}, {}, []
    for n, st in enumerate(plan):
        st.at, st.before, st.s0 = dict(at), dict(last), len(sizes)
        sizes += st.slabs
        for name, count in st.counts.items():
            at[name] = at.get(name, 0) + count
        for name in st.counts:
            st.at.setdefault(name, 0)
        for engine, name in st.last.items():
            last[engine] = (name, at[name])
    return plan, at, last, sizes


def build(nc, x_in, mem_in, ctx_in, vec_in, cst_in, bias_in, w16, w22, w12, out):
    plan, totals, finals, sizes = make_plan()
    ns = len(sizes)

    with ExitStack() as ctx:
        base = 16512

        def sb(name, shape, dt, at):
            return nc.alloc_sbuf_tensor_at(name, [P] + shape, dt, offset=base + at)

        kb = 1024
        raw = [sb(f"raw{u}", [SLAB_OUT], F32, 11 * kb * u) for u in range(2)]
        wh = [sb(f"w_hi{u}", [SLAB_OUT], F32R, 22 * kb + 11 * kb * u) for u in range(2)]
        wl = [sb(f"w_lo{u}", [SLAB_OUT], F32R, 44 * kb + 11 * kb * u) for u in range(2)]
        u_hi = sb("u_hi", [KT, TT], F32R, 66 * kb)
        u_lo = sb("u_lo", [KT, TT], F32R, 82 * kb)
        X = sb("X", [KT, TT], F32, 98 * kb)
        YO = 114 * kb
        Y = sb("Y", [KT, TT], F32, YO)
        q1, k1, g1 = [sb(f"{n}1", [4, TX], F32, YO + 4 * kb * i) for i, n in enumerate("qkg")]
        v1 = sb("v1", [2, BW], F32, YO + 12 * kb)
        merged = sb("merged", [KT, TX], F32, YO)
        Q = sb("Q", [KT, TT], F32, YO)
        qn = sb("qn", [KT, TX], F32, YO)
        on = sb("on", [32, P], F32, YO)
        GO = 130 * kb
        g_hi = sb("g_hi", [FH, TT], F32R, GO)
        g_lo = sb("g_lo", [FH, TT], F32R, GO + 22 * kb)
        y_hi = sb("y_hi", [12, TX], F32R, GO)
        y_lo = sb("y_lo", [12, TX], F32R, GO + 22 * kb)
        iq = sb("iq", [4, TX], F32, GO + 12 * kb)
        ik = sb("ik", [TX], F32, GO + 16 * kb)
        sel_bias = sb("sel_bias", [2, TX], F32, GO + 17 * kb)
        idx_acc = sb("idx_acc", [2, TX], F32, GO + 19 * kb)
        K = sb("K", [KT, TT], F32, GO)
        V = sb("V", [4, D], F32, GO + 16 * kb)
        na_bias = sb("na_bias", [2, TX], F32, GO + 32 * kb)
        SO = 174 * kb
        sq = sb("sq", [2, TT], F32, SO)
        sqsum = sb("sqsum", [TT], F32, SO + 4 * kb)
        rms_root = sb("rms_root", [TT], F32, SO + 6 * kb)
        rms = sb("rms", [TT], F32, SO + 8 * kb)
        scaled = sb("scaled", [2, TT], F32, SO + 10 * kb)
        silu = sb("silu", [2, TT], F32, SO)
        h_f32 = sb("h_f32", [2, TT], F32, SO + 4 * kb)
        shuf = sb("shuf", [2, TX], F32, SO)
        sig = sb("sig", [2, TX], F32, SO)
        upg = sb("upg", [2, TX], F32, SO + 2 * kb)
        relu = sb("relu", [2, TX], F32, SO)
        s_sb = sb("s_sb", [2, TT], F32, SO)
        p_sb = sb("p_sb", [2, TT], F32, SO + 4 * kb)
        pt_sb = sb("pt_sb", [2, TT], F32, SO + 12 * kb)
        p2_sb = sb("p2_sb", [2, 2, TT], F32, SO)
        og = sb("og", [2, TT], F32, SO)
        osq = sb("osq", [P], F32, SO + 8 * kb)
        CO = 190 * kb
        cst = sb("cst", [NC], F32, CO)
        CO += 4 * NC
        vec = sb("vec", [NV], F32, CO)
        CO += -(-4 * NV // 32) * 32
        ones = sb("ones", [P], F32, CO)
        mod = sb("mod", [DEPTH, 9, KT, 2], F32, CO + 512)
        CO += 512 + 4 * DEPTH * 9 * KT * 2
        gs = sb("gs", [DEPTH, 3, KT, 2], F32, CO)
        gg = sb("gg", [DEPTH, 3, KT, 2], F32, CO + 4 * DEPTH * 3 * KT * 2)
        CO += 8 * DEPTH * 3 * KT * 2
        mod_raw = sb("mod_raw", [9 * KT, 4], F32, SO)
        c_f32 = sb("c_f32", [KT, 2], F32, CO)
        c_split = sb("c_split", [KT, 4], F32R, CO + 64)
        CO += 64 + 128
        wi = sb("wi", [2, NH1], F32, CO)
        top8 = sb("top8", [8], F32, CO + 64)
        eps = sb("eps", [1], F32, CO + 96)
        lam = sb("lam", [8], F32, CO + 128)
        mx = sb("mx", [2, 2], F32, CO + 160)
        nm = sb("nm", [2, 2], F32, CO + 192)
        rs = sb("rs", [2, 2], F32, CO + 224)
        ri = sb("ri", [2, 2], F32, CO + 256)
        rw = sb("rw", [2], F32, CO + 288)
        sub_g = sb("sub_g", [1], F32, CO + 320)
        ssq = sb("ssq", [32], F32, CO + 352)
        sroot = sb("sroot", [32], F32, CO + 480)
        srec = sb("srec", [32], F32, CO + 608)
        lam_tmp = sb("lam_tmp", [2, HD], F32, CO + 736)
        CO += 736 + 512
        assert base + CO <= 229368, CO

        PA = ctx.enter_context(nc.psum_tensor("PA", [P, 4, 512], F32))
        PB = ctx.enter_context(nc.psum_tensor("PB", [P, 4, 512], F32))

        ident = cst[:, C_ID:C_ID + P]
        dest = dict(q=q1, k=k1, g=g1, v=v1, iq=iq, ik=ik, Q=Q, K=K, V=V, Y=Y, X=X)

        names = set(totals) | {"raw_full0", "raw_full1", "w_hi_ready", "w_split", "chain",
                               "ones_ready", "consts_in", "x_in", "mem_in", "ctx_in", "bias_in0",
                               "bias_in1", "stored", "bias_ready"}
        sem = {n: ctx.enter_context(nc.semaphore(n)) for n in sorted(names)}
        raw_full = [sem["raw_full0"], sem["raw_full1"]]
        block = ctx.enter_context(nc.Block())

        def before(st, engine):
            name, value = st.before.get(engine, ("ones_ready", 2))
            return sem[name], value

        def keys(w, qt):
            return (qt + 1) * P if w in "ab" else TX if w == "m" else TT

        class Chain:

            n = 0

            def up(self):
                self.n += 1
                return 1

        @block.sync
        def _(sp):
            sp.dma_start(X[:, :, 0:TX], x_in).then_inc(sem["x_in"], 16)
            sp.dma_start(X[:, :, TX:TT], mem_in).then_inc(sem["mem_in"], 16)
            src = {SLAB: w16, SLAB_OUT: w22, SLAB_MIX: w12}
            used = {SLAB: 0, SLAB_OUT: 0, SLAB_MIX: 0}
            s = 0
            while s < ns:
                size, n = sizes[s], 1
                while s + n < ns and sizes[s + n] == size:
                    n += 1
                pairs = (n - 2) // 2 if s == 0 else n // 2

                def load(s, half, index):
                    if not isinstance(s, int) or s >= 2:
                        sp.wait_ge(sem["w_split"], s - 1)
                    sp.dma_start(raw[half][:, 0:size],
                                 src[size][bass.ds(index, 1), :, :].rearrange("a p n -> p (a n)"))\
                      .then_inc(raw_full[half], 16)

                first = used[size]
                done = 0
                if s == 0:
                    load(0, 0, first)
                    load(1, 1, first + 1)
                    done = 2
                if pairs > 1:
                    with sp.Fori(0, pairs) as i:
                        for p in range(2):
                            load(i * 2 + (s + done + p), (s + done + p) % 2,
                                 i * 2 + (first + done + p))
                    done += 2 * pairs
                for p in range(done, n):
                    load(s + p, (s + p) % 2, first + p)
                used[size] += n
                s += n
            name, value = finals["dve"]
            sp.wait_ge(sem[name], value)
            sp.dma_start(out, X[:, :, 0:TX]).then_inc(sem["stored"], 16)
            sp.wait_ge(sem["stored"], 16)

        @block.tensor
        def _(pe):
            def mm3(psum, u, wcol, hi, lo, first, last):
                whi, wlo = wh[u][:, wcol:wcol + P], wl[u][:, wcol:wcol + P]
                pe.matmul(psum, whi, hi, start=first, stop=False)
                pe.matmul(psum, whi, lo, start=False, stop=False)
                return pe.matmul(psum, wlo, hi, start=False, stop=last)

            def nat3(psum, u, c0, c1, k, hi, lo, first, last):
                whi, wlo = wh[u][:, k * 256 + c0:k * 256 + c1], wl[u][:, k * 256 + c0:k * 256 + c1]
                pe.matmul(psum, hi, whi, start=first, stop=False)
                pe.matmul(psum, lo, whi, start=False, stop=False)
                return pe.matmul(psum, hi, wlo, start=False, stop=last)

            def pe_norm(st):
                T = st.T
                pe.wait_ge(*before(st, "act"))
                pe.wait_ge(*before(st, "dve"))
                pe.wait_ge(sem["sum_ready"], st.at["sum_ready"] + KT)
                pe.matmul(PB[:, 3, 0:T], ones[:, :], sqsum[:, 0:T], start=True, stop=True)\
                  .then_inc(sem["mean_ready"], 1)

            def pe_proj(st):
                pe.wait_ge(*before(st, "act"))
                pe.wait_ge(*before(st, "dve"))
                act = dve = 0
                taken = []
                for i, (how, to, tile, t0, T) in enumerate(st.steps):
                    s = st.s0 + i
                    u, ps = s % 2, i % 2
                    if i >= 2:
                        pe.wait_ge(sem[taken[i - 2][0]], st.at[taken[i - 2][0]] + taken[i - 2][1])
                    pe.wait_ge(sem["w_split"], s + 1)
                    if how == "nat":
                        for t in range(T // P):
                            po = PA[:, 2 * ps + t // 2, (t % 2) * 256:(t % 2) * 256 + 256]
                            tok = slice(t0 + t * P, t0 + t * P + P)
                            for k in range(KT):
                                mm = nat3(po, u, 0, 256, k, u_hi[:, k, tok], u_lo[:, k, tok],
                                          k == 0, k == KT - 1)
                    elif how == "index":
                        for k in range(KT):
                            mm3(PA[:, 2 * ps, 0:TX], u, k * 256, u_hi[:, k, 0:TX],
                                u_lo[:, k, 0:TX], k == 0, k == KT - 1)
                        for t in range(2):
                            po = PA[:, 2 * ps, TX + 8 * t:TX + 8 * t + 8]
                            tok = slice(t * P, t * P + P)
                            for k in range(KT):
                                mm = nat3(po, u, P, P + NH1, k, u_hi[:, k, tok],
                                          u_lo[:, k, tok], k == 0, k == KT - 1)
                    else:
                        for c in range(2):
                            po = PA[:, 2 * ps, c * TX:c * TX + TX] if T == TX else \
                                PA[:, 2 * ps + c, 0:T]
                            for k in range(KT):
                                mm = mm3(po, u, k * 256 + c * P, u_hi[:, k, t0:t0 + T],
                                         u_lo[:, k, t0:t0 + T], k == 0, k == KT - 1)
                    mm.then_inc(sem["slab_done"], 1)
                    if how in ("copy", "silu", "scale", "nat", "y"):
                        act += 1
                        taken.append(("taken_act", act))
                    else:
                        dve += 1
                        taken.append(("taken_dve", dve))

            def pe_ffn_in(st):
                T = st.T
                pe.wait_ge(*before(st, "act"))
                pe.wait_ge(*before(st, "dve"))

                def step(i, p):
                    s = st.s0 + p
                    u, ps = s % 2, p % 2
                    if not isinstance(i, int) or i + p >= 2:
                        pe.wait_ge(sem["h_ready"], st.at["h_ready"] + (i + (p - 1)))
                    pe.wait_ge(sem["w_split"], i + (s + 1))
                    for c in range(2):
                        for k in range(KT):
                            mm = mm3(PA[:, 2 * ps + c, 0:T], u, k * 256 + c * P, u_hi[:, k, 0:T],
                                     u_lo[:, k, 0:T], k == 0, k == KT - 1)
                    mm.then_inc(sem["slab_done"], 1)

                step(0, 0)
                step(0, 1)
                with pe.Fori(0, (FH - 3) // 2) as i:
                    step(i * 2, 2)
                    step(i * 2, 3)
                step(0, FH - 1)

            def pe_ffn_out(st):
                T = st.T
                pe.wait_ge(*before(st, "act"))
                pe.wait_ge(*before(st, "dve"))
                ev = "taken_act" if st.half == 0 else "taken_dve"

                def step(i, p):
                    s = st.s0 + p
                    u, ps = s % 2, p % 2
                    if not isinstance(i, int) or i + p >= 2:
                        pe.wait_ge(sem[ev], st.at[ev] + (i + (p - 1)))
                    pe.wait_ge(sem["w_split"], i + (s + 1))
                    for c in range(2):
                        for k in range(FH):
                            mm = mm3(PB[:, 2 * ps + c, 0:T], u, k * 256 + c * P, g_hi[:, k, 0:T],
                                     g_lo[:, k, 0:T], k == 0, k == FH - 1)
                    mm.then_inc(sem["slab_done"], 1)

                for p in range(4):
                    step(0, p)

            def pe_attn(st):
                pe.wait_ge(*before(st, "act"))
                pe.wait_ge(*before(st, "dve"))
                n = len(st.units)
                w = st.which
                for i in range(n + 2):
                    if i < n:
                        h, qt, _ = st.units[i]
                        if i >= 2:
                            pe.wait_ge(sem["p_ready"], st.at["p_ready"] + i - 1)
                        mm = scores(w, h, qt, PA[:, i % 2, :])
                        mm.then_inc(sem["s_ready"], 1)
                    if 1 <= i <= n:
                        j = i - 1
                        pe.wait_ge(sem["p_normed"], st.at["p_normed"] + j + 1)
                        if j >= 2:
                            pe.wait_ge(sem["pt_copied"], st.at["pt_copied"] + j - 1)
                        for b in range(keys(w, st.units[j][1]) // P):
                            mm = pe.transpose(PB[:, 2 + j % 2, b * P:b * P + P],
                                              p_sb[:, j % 2, b * P:b * P + P], ident)
                        mm.then_inc(sem["pt_ready"], 1)
                    if i >= 2:
                        j = i - 2
                        h, qt, _ = st.units[j]
                        g = j // (n // st.groups)
                        if g >= 2 and j % (n // st.groups) == 0:
                            pe.wait_ge(sem["o_taken"], st.at["o_taken"] + g - 1)
                        pe.wait_ge(sem["pt_copied"], st.at["pt_copied"] + j + 1)
                        nb = keys(w, qt) // P
                        for b in range(nb):
                            if w in "ab":
                                p0, vt = HD * (h % 2), v1[:, b, h * HD:h * HD + HD]
                            elif w == "m":
                                p0, vt = 0, v1[:, b, h * P:h * P + P]
                            else:
                                p0, vt = HD * (h % 2), V[:, b, h * HD:h * HD + HD]
                            m = P if w == "m" else HD
                            mm = pe.matmul(PB[p0:p0 + m, g % 2, qt * P:qt * P + P], vt,
                                           pt_sb[:, j % 2, b * P:b * P + P],
                                           start=(b == 0), stop=(b == nb - 1))
                        mm.then_inc(sem["o_ready"], 1)

            def scores(w, h, qt, bank):
                nk = keys(w, qt)
                if w == "m":
                    return pe.matmul(bank[:, 0:nk], q1[:, h, qt * P:qt * P + P], k1[:, h, 0:nk],
                                     start=True, stop=True)
                p0 = HD * (h % 2)
                q_, k_ = (q1, k1) if w in "ab" else (qn, K)
                return pe.matmul(bank[:, 0:nk], q_[p0:p0 + HD, h // 2, qt * P:qt * P + P],
                                 k_[p0:p0 + HD, h // 2, 0:nk], start=True, stop=True)

            def pe_index(st):
                pe.wait_ge(*before(st, "act"))
                pe.wait_ge(*before(st, "dve"))
                for j in range(16):
                    qt, h = j // 8, j % 8
                    p0, nk = HD * (h % 2), (qt + 1) * P
                    if j >= 4:
                        pe.wait_ge(sem["relu_ready"], st.at["relu_ready"] + j - 3)
                    pe.matmul(PA[:, j % 4, 0:nk], iq[p0:p0 + HD, h // 2, qt * P:qt * P + P],
                              ik[p0:p0 + HD, 0:nk], start=True, stop=True)\
                      .then_inc(sem["is_ready"], 1)

            def pe_mix(st):
                pe.wait_ge(*before(st, "act"))
                pe.wait_ge(*before(st, "dve"))

                def step(b, i, p):
                    s = st.s0 + 8 * b + p
                    u, ps = s % 2, p % 2
                    if b or p >= 2:
                        pe.wait_ge(sem["up_taken"], st.at["up_taken"] + (i + (8 * b + p - 1)))
                    pe.wait_ge(sem["w_split"], i + (s + 1))
                    for k in range(KT):
                        mm3(PA[:, 2 * ps, 0:TX], u, k * P, u_hi[:, k, 0:TX], u_lo[:, k, 0:TX],
                            k == 0, k == KT - 1)
                    for k in range(4):
                        mm = mm3(PA[:, 2 * ps + 1, 0:TX], u, (KT + k) * P, y_hi[:, 4 * b + k, :],
                                 y_lo[:, 4 * b + k, :], k == 0, k == 3)
                    mm.then_inc(sem["slab_done"], 1)

                for b in range(3):
                    step(b, 0, 0)
                    step(b, 0, 1)
                    with pe.Fori(0, 3) as i:
                        step(b, i * 2, 2)
                        step(b, i * 2, 3)

            def pe_ada(st):
                pe.wait_ge(*before(st, "act"))
                pe.wait_ge(*before(st, "dve"))
                pe.wait_ge(sem["c_lo_ready"], st.at["c_lo_ready"] + 1)
                for l in range(DEPTH):
                    with pe.Fori(0, 18) as i:
                        for p in range(2):
                            s = st.s0 + 36 * l + p
                            pe.wait_ge(sem["w_split"], i * 2 + (s + 1))
                            for c in range(2):
                                po = PA[:, l, bass.ds(i * 16 + (8 * p + 4 * c), 4)]
                                for k in range(KT):
                                    w0 = k * 256 + c * P
                                    pe.matmul(po, wh[s % 2][:, w0:w0 + P], c_split[:, k, :],
                                              start=(k == 0), stop=False)
                                    mm = pe.matmul(po, wl[s % 2][:, w0:w0 + P], c_split[:, k, :],
                                                   start=False, stop=(k == KT - 1))
                            mm.then_inc(sem["slab_done"], 1)

            def pe_diff(st):
                pe.wait_ge(*before(st, "act"))
                pe.wait_ge(*before(st, "dve"))
                n = len(st.units)
                for i in range(n + 2):
                    if i < n:
                        h, t = st.units[i]
                        k0 = 0 if t < 2 else TX
                        if i >= 2:
                            pe.wait_ge(sem["p_ready"], st.at["p_ready"] + i - 1)
                        for j in range(2):
                            p0 = HD * j
                            mm = pe.matmul(PA[:, 2 * (i % 2) + j, 0:TT - k0],
                                           Q[p0:p0 + HD, h, t * P:t * P + P],
                                           K[p0:p0 + HD, h, k0:TT], start=True, stop=True)
                        mm.then_inc(sem["s_ready"], 1)
                    if 1 <= i <= n:
                        j = i - 1
                        pe.wait_ge(sem["p_normed"], st.at["p_normed"] + j + 1)
                        if j >= 2:
                            pe.wait_ge(sem["pt_copied"], st.at["pt_copied"] + j - 1)
                        for b in range(4 if st.units[j][1] < 2 else 2):
                            mm = pe.transpose(PB[:, 2 + j % 2, b * P:b * P + P],
                                              p2_sb[:, j % 2, 0, b * P:b * P + P], ident)
                        mm.then_inc(sem["pt_ready"], 1)
                    if i >= 2:
                        j = i - 2
                        h, t = st.units[j]
                        if j >= 2:
                            pe.wait_ge(sem["o_taken"], st.at["o_taken"] + j - 1)
                        pe.wait_ge(sem["pt_copied"], st.at["pt_copied"] + j + 1)
                        nb, b0 = (4, 0) if t < 2 else (2, 2)
                        for b in range(nb):
                            mm = pe.matmul(PB[:, j % 2, 0:P], pt_sb[:, j % 2, b * P:b * P + P],
                                           V[:, b0 + b, h * P:h * P + P],
                                           start=(b == 0), stop=(b == nb - 1))
                        mm.then_inc(sem["o_ready"], 1)
                for h in range(8):
                    pe.wait_ge(sem["o_scaled"], st.at["o_scaled"] + (4 * h + 4))
                    if h >= 4:
                        pe.wait_ge(sem["og_ready"], st.at["og_ready"] + h - 3)
                    for t in range(4):
                        mm = pe.transpose(PA[:, h % 4, t * P:t * P + P], on[:, 4 * h + t, :], ident)
                    mm.then_inc(sem["ot_ready"], 1)

            run = dict(norm=pe_norm, proj=pe_proj, ffn_in=pe_ffn_in, ffn_out=pe_ffn_out,
                       attn=pe_attn, index=pe_index, mix=pe_mix, ada=pe_ada, diff=pe_diff)
            pe.wait_ge(sem["consts_in"], 32)
            for st in plan:
                if st.kind in run:
                    run[st.kind](st)

        @block.scalar
        def _(act):
            def feed(s, i=0):
                if s >= ns:
                    return
                u = s % 2
                half = i if isinstance(i, int) else None
                act.wait_ge(raw_full[u], (feed_pair * 16 if half is None else 0) +
                            16 * (s // 2 + 1))
                if s >= 2:
                    act.wait_ge(sem["slab_done"], i + (s - 1))
                act.activation(wh[u][:, 0:sizes[s]], raw[u][:, 0:sizes[s]], ACT.Copy)\
                   .then_inc(sem["w_hi_ready"], 1)

            feed_pair = 0

            def act_norm(st):
                src = X if st.src == "X" else Y
                T = st.T
                act.wait_ge(*before(st, "pe"))
                act.wait_ge(*before(st, "act"))
                act.wait_ge(*before(st, "dve"))
                for k in range(KT):
                    if k >= 2:
                        act.wait_ge(sem["sum_ready"], st.at["sum_ready"] + k - 1)
                    act.activation(sq[:, k % 2, 0:T], src[:, k, 0:T], ACT.Square)\
                       .then_inc(sem["sq_ready"], 1)
                act.wait_ge(sem["mean_ready"], st.at["mean_ready"] + 1)
                act.activation(rms_root[:, 0:T], PB[:, 3, 0:T], ACT.Sqrt, bias=eps[:, 0:1])\
                   .then_inc(sem["sqrt_ready"], 1)
                if st.apply == "split":
                    for k in range(KT):
                        act.wait_ge(sem["scaled"], st.at["scaled"] + k + 1)
                        for v in range(T // TX):
                            tok = slice(v * TX, v * TX + TX)
                            if st.mod:
                                ins = act.activation(u_hi[:, k, tok], scaled[:, k % 2, tok],
                                                     ACT.Identity,
                                                     bias=mod[:, st.l, 3 * st.sub, k, v:v + 1])
                            else:
                                ins = act.activation(u_hi[:, k, tok], scaled[:, k % 2, tok],
                                                     ACT.Copy)
                        ins.then_inc(sem["u_hi_ready"], 1)

            def act_proj(st):
                act.wait_ge(*before(st, "pe"))
                act.wait_ge(*before(st, "act"))
                act.wait_ge(*before(st, "dve"))
                for i, (how, to, tile, t0, T) in enumerate(st.steps):
                    s, ps = st.s0 + i, i % 2
                    feed(s + 2)
                    if how not in ("copy", "silu", "scale", "nat", "y"):
                        continue
                    act.wait_ge(sem["slab_done"], st.at["slab_done"] + i + 1)
                    if how == "nat":
                        nt = T // P
                        src = PA[:, 2 * ps:2 * ps + nt // 2, :]\
                            .rearrange("p b (t c) -> p (b t) c", c=256)
                        dst = dest[to][:, 0:nt, tile * 256:tile * 256 + 256]
                    elif T == TX:
                        src = PA[:, 2 * ps, :].rearrange("p (c t) -> p c t", t=TX)
                        full = qn if to == "Q" else dest[to]
                        dst = full[:, tile:tile + 2, 0:TX]
                    else:
                        src = PA[:, 2 * ps:2 * ps + 2, :]
                        dst = dest[to][:, tile:tile + 2, 0:TT]
                    if how == "silu":
                        ins = act.activation(dst, src, ACT.Silu)
                    elif how == "scale":
                        ins = act.activation(dst, src, ACT.Copy, scale=HD ** -0.5)
                    else:
                        ins = act.activation(dst, src, ACT.Copy)
                    ins.then_inc(sem["taken_act"], 1)

            def act_ffn_in(st):
                nonlocal feed_pair
                T = st.T
                act.wait_ge(*before(st, "pe"))
                act.wait_ge(*before(st, "act"))
                act.wait_ge(*before(st, "dve"))

                def step(i, p):
                    ps = p % 2
                    act.wait_ge(sem["slab_done"], st.at["slab_done"] + (i + (p + 1)))
                    act.activation(silu[:, ps, 0:T], PA[:, 2 * ps, 0:T], ACT.Silu)\
                       .then_inc(sem["silu_ready"], 1)
                    feed(st.s0 + p + 2, i)
                    act.wait_ge(sem["h_ready"], st.at["h_ready"] + (i + (p + 1)))
                    act.activation(g_hi[:, p if isinstance(i, int) else bass.ds(i + p, 1), 0:T],
                                   h_f32[:, ps, 0:T], ACT.Copy).then_inc(sem["g_hi_ready"], 1)

                with act.Fori(0, (FH - 3) // 2) as i:
                    feed_pair = i
                    step(i * 2, 0)
                    step(i * 2, 1)
                for p in range(FH - 3, FH):
                    step(0, p)

            def act_ffn_out(st):
                T = st.T
                act.wait_ge(*before(st, "pe"))
                act.wait_ge(*before(st, "act"))
                act.wait_ge(*before(st, "dve"))
                for p in range(4):
                    ps = p % 2
                    feed(st.s0 + p + 2)
                    if st.half == 0:
                        act.wait_ge(sem["slab_done"], st.at["slab_done"] + p + 1)
                        act.activation(Y[:, 2 * p:2 * p + 2, 0:T], PB[:, 2 * ps:2 * ps + 2, 0:T],
                                       ACT.Copy).then_inc(sem["taken_act"], 1)

            def act_attn(st):
                w, n = st.which, len(st.units)
                scale = dict(a=HD ** -0.5, b=HD ** -0.5, m=P ** -0.5, n=1.0)[w]
                act.wait_ge(*before(st, "pe"))
                act.wait_ge(*before(st, "act"))
                act.wait_ge(*before(st, "dve"))
                for i in range(n + 1):
                    if i < n:
                        nk = keys(w, st.units[i][1])
                        act.wait_ge(sem["negmax_ready"], st.at["negmax_ready"] + i + 1)
                        if i >= 2:
                            act.wait_ge(sem["pt_ready"], st.at["pt_ready"] + i - 1)
                        if w == "m":
                            src = PA[:, i % 2, 0:nk]
                        else:
                            src = s_sb[:, i % 2, 0:nk]
                        act.activation(p_sb[:, i % 2, 0:nk], src, ACT.Exp, scale=scale,
                                       bias=nm[:, i % 2, 0:1], accum_out=rs[:, i % 2, 0:1])\
                           .then_inc(sem["p_ready"], 1)
                    if i >= 1:
                        j = i - 1
                        nk = keys(w, st.units[j][1])
                        act.wait_ge(sem["pt_ready"], st.at["pt_ready"] + j + 1)
                        if j >= 2:
                            act.wait_ge(sem["o_ready"], st.at["o_ready"] + j - 1)
                        act.activation(pt_sb[:, j % 2, 0:nk], PB[:, 2 + j % 2, 0:nk], ACT.Copy)\
                           .then_inc(sem["pt_copied"], 1)
                act.wait_ge(sem["o_taken"], st.at["o_taken"] + st.groups)
                if w == "n":
                    act.activation(u_hi[:, :, 0:TX], qn[:, :, :], ACT.Copy)\
                       .then_inc(sem["y_hi_ready"], 1)
                else:
                    b = 4 * "abm".index(w)
                    act.activation(y_hi[:, b:b + 4, :], q1[:, :, :], ACT.Copy)\
                       .then_inc(sem["y_hi_ready"], 1)

            def act_index(st):
                act.wait_ge(*before(st, "pe"))
                act.wait_ge(*before(st, "act"))
                act.wait_ge(*before(st, "dve"))
                for j in range(16):
                    nk = (j // 8 + 1) * P
                    act.wait_ge(sem["is_ready"], st.at["is_ready"] + j + 1)
                    if j >= 2:
                        act.wait_ge(sem["acc_ready"], st.at["acc_ready"] + j - 1)
                    act.activation(relu[:, j % 2, 0:nk], PA[:, j % 4, 0:nk], ACT.Relu,
                                   scale=HD ** -0.5).then_inc(sem["relu_ready"], 1)

            def act_mix(st):
                nonlocal feed_pair
                act.wait_ge(*before(st, "pe"))
                act.wait_ge(*before(st, "act"))
                act.wait_ge(*before(st, "dve"))

                def step(i, p):
                    ps = p % 2
                    feed(st.s0 + p + 2, i)
                    act.wait_ge(sem["slab_done"], st.at["slab_done"] + (i + (p + 1)))
                    if not isinstance(i, int) or p >= 2:
                        act.wait_ge(sem["up_taken"], st.at["up_taken"] + (i + (p - 1)))
                    act.activation(sig[:, ps, :], PA[:, 2 * ps, 0:TX], ACT.Sigmoid)\
                       .then_inc(sem["gate_ready"], 1)

                step(0, 0)
                step(0, 1)
                with act.Fori(0, 10) as i:
                    feed_pair = i
                    step(i * 2, 2)
                    step(i * 2, 3)
                step(0, 22)
                step(0, 23)
                act.wait_ge(sem["merged"], st.at["merged"] + 24)
                act.activation(u_hi[:, :, 0:TX], merged[:, :, :], ACT.Copy)\
                   .then_inc(sem["m_hi_ready"], 1)

            def act_ada(st):
                nonlocal feed_pair
                act.wait_ge(*before(st, "pe"))
                act.wait_ge(*before(st, "act"))
                act.wait_ge(*before(st, "dve"))
                act.dma_start(X[:, :, TX:TT], ctx_in).then_inc(sem["ctx_in"], 16)
                act.activation(c_f32[:, :, :], vec[:, V_C:V_C + 2 * KT]
                               .rearrange("p (k v) -> p k v", v=2), ACT.Silu)\
                   .then_inc(sem["c_ready"], 1)
                act.wait_ge(sem["c_ready"], st.at["c_ready"] + 1)
                act.activation(c_split[:, :, 0:2], c_f32[:, :, :], ACT.Copy)\
                   .then_inc(sem["c_hi_ready"], 1)
                with act.Fori(0, 35) as i:
                    feed_pair = i
                    feed(st.s0 + 2, i * 2)
                    feed(st.s0 + 3, i * 2)
                feed(st.s0 + 72)
                feed(st.s0 + 73)
                for l in range(DEPTH):
                    act.wait_ge(sem["slab_done"], st.at["slab_done"] + (36 * (l + 1)))
                    if l:
                        act.wait_ge(sem["mod_ready"], st.at["mod_ready"] + 1)
                    act.activation(mod_raw[:, :, :], PA[:, l, 0:9 * KT * 4]
                                   .rearrange("p (m v) -> p m v", v=4), ACT.Copy)\
                       .then_inc(sem["mod_copied"], 1)
                act.wait_ge(sem["ctx_in"], 16)

            def act_diff(st):
                n = len(st.units)
                act.wait_ge(*before(st, "pe"))
                act.wait_ge(*before(st, "act"))
                act.wait_ge(*before(st, "dve"))
                for i in range(n + 3):
                    if i < n:
                        nk = TT if st.units[i][1] < 2 else TX
                        act.wait_ge(sem["negmax_ready"], st.at["negmax_ready"] + i + 1)
                        if i >= 2:
                            act.wait_ge(sem["pt_ready"], st.at["pt_ready"] + i - 1)
                        for j in range(2):
                            ins = act.activation(p2_sb[:, i % 2, j, 0:nk],
                                                 PA[:, 2 * (i % 2) + j, 0:nk], ACT.Exp,
                                                 scale=HD ** -0.5, bias=nm[:, i % 2, j:j + 1],
                                                 accum_out=rs[:, i % 2, j:j + 1])
                        ins.then_inc(sem["p_ready"], 1)
                    if 1 <= i <= n:
                        j = i - 1
                        nk = TT if st.units[j][1] < 2 else TX
                        act.wait_ge(sem["pt_ready"], st.at["pt_ready"] + j + 1)
                        if j >= 2:
                            act.wait_ge(sem["o_ready"], st.at["o_ready"] + j - 1)
                        act.activation(pt_sb[:, j % 2, 0:nk], PB[:, 2 + j % 2, 0:nk], ACT.Copy)\
                           .then_inc(sem["pt_copied"], 1)
                    if i >= 3:
                        j = i - 3
                        act.wait_ge(sem["o_taken"], st.at["o_taken"] + j + 1)
                        if j >= 1:
                            act.wait_ge(sem["o_sq_ready"], st.at["o_sq_ready"] + j)
                        act.activation(osq[:, :], on[:, j, :], ACT.Square,
                                       accum_out=ssq[:, j:j + 1]).then_inc(sem["o_sq_ready"], 1)
                act.wait_ge(sem["o_sq_ready"], st.at["o_sq_ready"] + n)
                act.activation(sroot[:, :], ssq[:, :], ACT.Sqrt, scale=1.0 / P, bias=eps[:, 0:1])\
                   .then_inc(sem["o_sqrt_ready"], 1)
                for h in range(8):
                    act.wait_ge(sem["og_ready"], st.at["og_ready"] + h + 1)
                    act.activation(u_hi[:, h, :], og[:, h % 2, :], ACT.Copy)\
                       .then_inc(sem["y_hi_ready"], 1)

            st = plan[0]
            act.dma_start(cst[:, :], cst_in).then_inc(sem["consts_in"], 16)
            act.dma_start(vec[:, :], vec_in).then_inc(sem["consts_in"], 16)
            feed(0)
            feed(1)
            act.wait_ge(sem["setup_dve"], st.at["setup_dve"] + 2)
            act.activation(lam[:, 2:3], lam[:, 0:1], ACT.Exp).then_inc(sem["setup_act"], 1)
            act.activation(lam[:, 3:4], lam[:, 1:2], ACT.Exp).then_inc(sem["setup_act"], 1)
            act.wait_ge(sem["consts_in"], 32)
            act.wait_ge(sem["x_in"], 16)
            act.wait_ge(sem["mem_in"], 16)
            run = dict(norm=act_norm, proj=act_proj, ffn_in=act_ffn_in, ffn_out=act_ffn_out,
                       attn=act_attn, index=act_index, mix=act_mix, ada=act_ada, diff=act_diff)
            for st in plan[1:]:
                run[st.kind](st)

        @block.vector
        def _(dve):
            chain = Chain()

            def feed(s, i=0):
                if s >= ns:
                    return
                u, n = s % 2, sizes[s]
                dve.wait_ge(sem["w_hi_ready"], i + (s + 1))
                dve.tensor_tensor(wl[u][:, 0:n], raw[u][:, 0:n], wh[u][:, 0:n].bitcast(F32),
                                  ALU.subtract).then_inc(sem["w_split"], 1)

            def dve_norm(st):
                src = X if st.src == "X" else Y
                T, l, sub = st.T, st.l, st.sub
                nv = T // TX
                dve.wait_ge(*before(st, "pe"))
                dve.wait_ge(*before(st, "act"))
                dve.wait_ge(*before(st, "dve"))
                for k in range(KT):
                    dve.wait_ge(sem["sq_ready"], st.at["sq_ready"] + k + 1)
                    if k == 0:
                        ins = dve.tensor_copy(sqsum[:, 0:T], sq[:, 0, 0:T])
                    else:
                        dve.wait_ge(sem["sum_ready"], st.at["sum_ready"] + k)
                        ins = dve.tensor_tensor(sqsum[:, 0:T], sqsum[:, 0:T], sq[:, k % 2, 0:T],
                                                ALU.add)
                    ins.then_inc(sem["sum_ready"], 1)
                dve.wait_ge(sem["sqrt_ready"], st.at["sqrt_ready"] + 1)
                dve.reciprocal(rms[:, 0:T], rms_root[:, 0:T]).then_inc(sem["rms_ready"], 1)
                dve.wait_ge(sem["rms_ready"], st.at["rms_ready"] + 1)

                def gain(k, v):
                    if st.apply == "resid":
                        return gg[:, l, sub, k, v:v + 1]
                    if st.apply == "plain":
                        return vec[:, V_FG + k:V_FG + k + 1]
                    if st.mod:
                        return gs[:, l, sub, k, v:v + 1]
                    c = (V_NG, V_MG)[v] + l * KT + k
                    return vec[:, c:c + 1]

                def scale(k):
                    if k >= 2:
                        dve.wait_ge(sem["u_lo_ready" if st.apply == "split" else "x_ready"], st.at["u_lo_ready" if st.apply == "split" else "x_ready"] + k - 1)
                    for v in range(nv):
                        tok = slice(v * TX, v * TX + TX)
                        ins = dve.scalar_tensor_tensor(out=scaled[:, k % 2, tok],
                                                       in0=src[:, k, tok], scalar=gain(k, v),
                                                       in1=rms[:, tok], op0=ALU.mult,
                                                       op1=ALU.mult)
                    ins.then_inc(sem["scaled"], 1)

                def finish(k):
                    dve.wait_ge(sem["scaled"], st.at["scaled"] + k + 1)
                    if st.apply == "resid":
                        ins = dve.tensor_tensor(X[:, k, 0:T], X[:, k, 0:T], scaled[:, k % 2, 0:T],
                                                ALU.add)
                    elif st.apply == "plain":
                        ins = dve.tensor_copy(X[:, k, 0:T], scaled[:, k % 2, 0:T])
                    else:
                        dve.wait_ge(sem["u_hi_ready"], st.at["u_hi_ready"] + k + 1)
                        if not st.mod:
                            ins = dve.tensor_tensor(u_lo[:, k, 0:T], scaled[:, k % 2, 0:T],
                                                    u_hi[:, k, 0:T].bitcast(F32), ALU.subtract)
                        else:
                            for v in range(nv):
                                tok = slice(v * TX, v * TX + TX)
                                ins = dve.scalar_tensor_tensor(
                                    out=u_lo[:, k, tok], in0=scaled[:, k % 2, tok],
                                    scalar=mod[:, l, 3 * sub, k, v:v + 1],
                                    in1=u_hi[:, k, tok].bitcast(F32), op0=ALU.add,
                                    op1=ALU.subtract)
                        ins.then_inc(sem["u_lo_ready"], 1)
                        return
                    ins.then_inc(sem["x_ready"], 1)

                scale(0)
                for k in range(1, KT):
                    scale(k)
                    finish(k - 1)
                finish(KT - 1)

            def rope(src, dst, sh, table, mask, shape, taken):
                cos = cst[:, table:table + TX]
                sin = cst[:, table + TX:table + 2 * TX]
                if len(shape) == 3:
                    cos, sin = cos[:, None, :].broadcast_to(shape), sin[:, None, :].broadcast_to(shape)
                dve.stream_shuffle(sh, src, mask).then_inc(sem["chain"], chain.up())
                dve.tensor_tensor(dst, src, cos, ALU.mult).then_inc(taken, 1)
                dve.wait_ge(sem["chain"], chain.n)
                dve.tensor_tensor(sh, sh, sin, ALU.mult).then_inc(sem["chain"], chain.up())
                dve.wait_ge(sem["chain"], chain.n)
                return dve.tensor_tensor(dst, dst, sh, ALU.add)

            def dve_proj(st):
                dve.wait_ge(*before(st, "pe"))
                dve.wait_ge(*before(st, "act"))
                dve.wait_ge(*before(st, "dve"))
                mask1 = [(p + 8) % 16 if p < 16 else p for p in range(32)]
                mask2 = [(p + 16) % 32 for p in range(32)]
                done = 0
                for i, (how, to, tile, t0, T) in enumerate(st.steps):
                    s, ps = st.s0 + i, i % 2
                    feed(s + 2)
                    if how in ("copy", "silu", "scale", "nat", "y"):
                        continue
                    dve.wait_ge(sem["slab_done"], st.at["slab_done"] + i + 1)
                    if done:
                        dve.wait_ge(sem["out_dve"], st.at["out_dve"] + done)
                    two = PA[:, 2 * ps, :].rearrange("p (c t) -> p c t", t=TX)
                    if how == "rope1":
                        ins = rope(two, dest[to][:, tile:tile + 2, :], shuf[:, :, :], C_R1, mask1,
                                   (P, 2, TX), sem["taken_dve"])
                    elif how == "rope2":
                        dve.tensor_copy(dest[to][:, tile:tile + 2, TX:TT],
                                                  PA[:, 2 * ps:2 * ps + 2, TX:TT]).then_inc(sem["chain"], chain.up())
                        ins = rope(PA[:, 2 * ps:2 * ps + 2, 0:TX], dest[to][:, tile:tile + 2, 0:TX],
                                   shuf[:, :, :], C_R2, mask2, (P, 2, TX), sem["taken_dve"])
                    elif how == "index":
                        dve.tensor_scalar(
                            wi[:, :, :], PA[:, 2 * ps, TX:TX + 2 * NH1]
                            .rearrange("p (t h) -> p t h", h=NH1), NH1 ** -0.5, None, ALU.mult).then_inc(sem["chain"], chain.up())
                        ins = rope(PA[:, 2 * ps, 0:TX], ik[:, :], shuf[:, 0, :], C_R1, mask1,
                                   (P, TX), sem["taken_dve"])
                    else:
                        x = X[:, tile:tile + 2, 0:TX]
                        dve.tensor_tensor(x, x, two, ALU.add).then_inc(sem["taken_dve"], 1)
                        continue
                    ins.then_inc(sem["out_dve"], 1)
                    done += 1

            def dve_ffn_in(st):
                T = st.T
                dve.wait_ge(*before(st, "pe"))
                dve.wait_ge(*before(st, "act"))
                dve.wait_ge(*before(st, "dve"))

                def step(i, p):
                    ps = p % 2
                    dve.wait_ge(sem["silu_ready"], st.at["silu_ready"] + (i + (p + 1)))
                    dve.tensor_tensor(h_f32[:, ps, 0:T], silu[:, ps, 0:T], PA[:, 2 * ps + 1, 0:T],
                                      ALU.mult).then_inc(sem["h_ready"], 1)
                    feed(st.s0 + p + 2, i)
                    dve.wait_ge(sem["g_hi_ready"], st.at["g_hi_ready"] + (i + (p + 1)))
                    at = p if isinstance(i, int) else bass.ds(i + p, 1)
                    dve.tensor_tensor(g_lo[:, at, 0:T], h_f32[:, ps, 0:T],
                                      g_hi[:, at, 0:T].bitcast(F32), ALU.subtract)\
                       .then_inc(sem["g_lo_ready"], 1)

                with dve.Fori(0, (FH - 3) // 2) as i:
                    step(i * 2, 0)
                    step(i * 2, 1)
                for p in range(FH - 3, FH):
                    step(0, p)

            def dve_ffn_out(st):
                T = st.T
                dve.wait_ge(*before(st, "pe"))
                dve.wait_ge(*before(st, "act"))
                dve.wait_ge(*before(st, "dve"))
                for p in range(4):
                    ps = p % 2
                    feed(st.s0 + p + 2)
                    if st.half == 1:
                        dve.wait_ge(sem["slab_done"], st.at["slab_done"] + p + 1)
                        y = Y[:, 2 * p:2 * p + 2, 0:T]
                        dve.tensor_tensor(y, y, PB[:, 2 * ps:2 * ps + 2, 0:T], ALU.add)\
                           .then_inc(sem["taken_dve"], 1)

            def dve_attn(st):
                w, n = st.which, len(st.units)
                per = n // st.groups
                dve.wait_ge(*before(st, "pe"))
                dve.wait_ge(*before(st, "act"))
                dve.wait_ge(*before(st, "dve"))
                scale = dict(a=HD ** -0.5, b=HD ** -0.5, m=P ** -0.5, n=1.0)[w]

                def soft(i):
                    h, qt, _ = st.units[i]
                    nk, sl = keys(w, qt), i % 2
                    dve.wait_ge(sem["s_ready"], st.at["s_ready"] + i + 1)
                    if i >= 2:
                        dve.wait_ge(sem["p_ready"], st.at["p_ready"] + i - 1)
                    if w == "m":
                        dve.tensor_reduce(mx[:, sl, 0:1], PA[:, sl, 0:nk], AX.X, ALU.max).then_inc(sem["chain"], chain.up())
                        dve.wait_ge(sem["chain"], chain.n)
                    elif w == "n":
                        dve.wait_ge(sem["bias_ready"], i + 1)
                        dve.tensor_tensor_reduce(s_sb[:, sl, 0:TX], PA[:, sl, 0:TX],
                                                 na_bias[:, sl, :], 1.0, NEG, ALU.add, ALU.max,
                                                 mx[:, sl, 0:1])
                        dve.tensor_scalar(s_sb[:, sl, TX:TT], PA[:, sl, TX:TT], 1.0,
                                                    None, ALU.mult).then_inc(sem["chain"], chain.up())
                        dve.wait_ge(sem["chain"], chain.n)
                        dve.tensor_reduce(mx[:, sl, 1:2], s_sb[:, sl, TX:TT], AX.X,
                                                    ALU.max).then_inc(sem["chain"], chain.up())
                        dve.wait_ge(sem["chain"], chain.n)
                        dve.tensor_tensor(mx[:, sl, 0:1], mx[:, sl, 0:1],
                                                    mx[:, sl, 1:2], ALU.max).then_inc(sem["chain"], chain.up())
                        dve.wait_ge(sem["chain"], chain.n)
                    else:
                        m = cst[:, C_CM + (P if qt == 0 else 0):C_CM + 2 * P] if w == "a" else \
                            sel_bias[:, qt, 0:nk]
                        dve.tensor_tensor_reduce(s_sb[:, sl, 0:nk], PA[:, sl, 0:nk], m,
                                                           1.0, 4 * NEG, ALU.add, ALU.max,
                                                           mx[:, sl, 0:1]).then_inc(sem["chain"], chain.up())
                        dve.wait_ge(sem["chain"], chain.n)
                    dve.tensor_scalar(nm[:, sl, 0:1], mx[:, sl, 0:1], -scale, None, ALU.mult)\
                       .then_inc(sem["negmax_ready"], 1)

                def normalise(j):
                    nk, sl = keys(w, st.units[j][1]), j % 2
                    dve.wait_ge(sem["p_ready"], st.at["p_ready"] + j + 1)
                    dve.reciprocal(ri[:, sl, 0:1], rs[:, sl, 0:1]).then_inc(sem["chain"], chain.up())
                    dve.wait_ge(sem["chain"], chain.n)
                    dve.tensor_scalar(p_sb[:, sl, 0:nk], p_sb[:, sl, 0:nk], ri[:, sl, 0:1], None,
                                      ALU.mult).then_inc(sem["p_normed"], 1)

                def take(g):
                    dve.wait_ge(sem["o_ready"], st.at["o_ready"] + (per * (g + 1)))
                    o = PB[:, g % 2, 0:TX]
                    if w == "n":
                        ins = dve.tensor_copy(qn[:, g, :], o)
                    else:
                        ins = dve.tensor_tensor(q1[:, g, :], g1[:, g, :], o, ALU.mult)
                    ins.then_inc(sem["o_taken"], 1)

                for i in range(n + 3):
                    if i < n:
                        soft(i)
                    if 1 <= i <= n:
                        normalise(i - 1)
                    if i >= 3 and (i - 3) % per == per - 1:
                        take((i - 3) // per)
                dve.wait_ge(sem["y_hi_ready"], st.at["y_hi_ready"] + 1)
                if w == "n":
                    hi, lo, src = u_hi[:, :, 0:TX], u_lo[:, :, 0:TX], qn[:, :, :]
                else:
                    b = 4 * "abm".index(w)
                    hi, lo, src = y_hi[:, b:b + 4, :], y_lo[:, b:b + 4, :], q1[:, :, :]
                dve.tensor_tensor(lo, src, hi.bitcast(F32), ALU.subtract)\
                   .then_inc(sem["y_lo_ready"], 1)

            def dve_index(st):
                dve.wait_ge(*before(st, "pe"))
                dve.wait_ge(*before(st, "act"))
                dve.wait_ge(*before(st, "dve"))
                for j in range(16):
                    qt, h = j // 8, j % 8
                    nk = (qt + 1) * P
                    acc, r, wgt = idx_acc[:, qt, 0:nk], relu[:, j % 2, 0:nk], wi[:, qt, h:h + 1]
                    dve.wait_ge(sem["relu_ready"], st.at["relu_ready"] + j + 1)
                    if h == 0:
                        ins = dve.tensor_scalar(acc, r, wgt, 0.0, ALU.mult, ALU.add)
                    else:
                        dve.wait_ge(sem["acc_ready"], st.at["acc_ready"] + j)
                        ins = dve.scalar_tensor_tensor(out=acc, in0=r, scalar=wgt, in1=acc,
                                                       op0=ALU.mult, op1=ALU.add)
                    ins.then_inc(sem["acc_ready"], 1)
                for qt in range(2):
                    nk = (qt + 1) * P
                    acc = idx_acc[:, qt, 0:nk]
                    causal = cst[:, C_CM + (P if qt == 0 else 0):C_CM + 2 * P]
                    dve.wait_ge(sem["acc_ready"], st.at["acc_ready"] + (8 * (qt + 1)))
                    dve.tensor_tensor(acc, acc, causal, ALU.add).then_inc(sem["chain"], chain.up())
                    for _ in range(TOPK // 8):
                        dve.wait_ge(sem["chain"], chain.n)
                        dve.max(top8[:, :], acc).then_inc(sem["chain"], chain.up())
                        dve.wait_ge(sem["chain"], chain.n)
                        dve.match_replace(acc, top8[:, :], acc, TAKEN).then_inc(sem["chain"], chain.up())
                    dve.wait_ge(sem["chain"], chain.n)
                    sel = sel_bias[:, qt, 0:nk]
                    dve.tensor_scalar(sel, acc, TAKEN, NEG, ALU.is_gt, ALU.mult).then_inc(sem["chain"], chain.up())
                    dve.wait_ge(sem["chain"], chain.n)
                    dve.tensor_tensor(sel, sel, causal, ALU.add).then_inc(sem["topk_ready"], 1)

            def dve_mix(st):
                dve.wait_ge(*before(st, "pe"))
                dve.wait_ge(*before(st, "act"))
                dve.wait_ge(*before(st, "dve"))

                def step(b, i, p):
                    ps, n = p % 2, 8 * b + p
                    feed(st.s0 + n + 2, i)
                    dve.wait_ge(sem["gate_ready"], st.at["gate_ready"] + (i + (n + 1)))
                    at = p if isinstance(i, int) else bass.ds(i + p, 1)
                    if b == 0:
                        dve.tensor_tensor(upg[:, ps, :], sig[:, ps, :], PA[:, 2 * ps + 1, 0:TX],
                                          ALU.mult).then_inc(sem["up_taken"], 1)
                        dve.wait_ge(sem["up_taken"], st.at["up_taken"] + (i + (n + 1)))
                        dve.tensor_copy(merged[:, at, :], upg[:, ps, :]).then_inc(sem["merged"], 1)
                    else:
                        dve.tensor_tensor(upg[:, ps, :], sig[:, ps, :], PA[:, 2 * ps + 1, 0:TX],
                                          ALU.mult).then_inc(sem["up_taken"], 1)
                        dve.wait_ge(sem["up_taken"], st.at["up_taken"] + (i + (n + 1)))
                        dve.tensor_tensor(merged[:, at, :], merged[:, at, :], upg[:, ps, :],
                                          ALU.add).then_inc(sem["merged"], 1)

                for b in range(3):
                    with dve.Fori(0, 3) as i:
                        step(b, i * 2, 0)
                        step(b, i * 2, 1)
                    step(b, 0, 6)
                    step(b, 0, 7)
                dve.wait_ge(sem["m_hi_ready"], st.at["m_hi_ready"] + 1)
                dve.tensor_tensor(u_lo[:, :, 0:TX], merged[:, :, :], u_hi[:, :, 0:TX].bitcast(F32),
                                  ALU.subtract).then_inc(sem["m_lo_ready"], 1)

            def dve_ada(st):
                dve.wait_ge(*before(st, "pe"))
                dve.wait_ge(*before(st, "act"))
                dve.wait_ge(*before(st, "dve"))
                dve.wait_ge(sem["c_hi_ready"], st.at["c_hi_ready"] + 1)
                dve.tensor_tensor(c_split[:, :, 2:4], c_f32[:, :, :],
                                  c_split[:, :, 0:2].bitcast(F32), ALU.subtract)\
                   .then_inc(sem["c_lo_ready"], 1)
                with dve.Fori(0, 35) as i:
                    feed(st.s0 + 2, i * 2)
                    feed(st.s0 + 3, i * 2)
                feed(st.s0 + 72)
                feed(st.s0 + 73)
                done = 0
                for l in range(DEPTH):
                    m = mod[:, l, :, :, :].rearrange("p m k v -> p (m k) v")
                    dve.wait_ge(sem["mod_copied"], st.at["mod_copied"] + l + 1)
                    ins = dve.tensor_tensor(m, mod_raw[:, :, 0:2], mod_raw[:, :, 2:4], ALU.add)
                    ins.then_inc(sem["mod_ready"], 1)
                    done += 1
                    dve.wait_ge(sem["mod_ready"], st.at["mod_ready"] + done)
                    ab = vec[:, V_AB + l * 9 * KT * 2:V_AB + (l + 1) * 9 * KT * 2]\
                        .rearrange("p (m v) -> p m v", v=2)
                    dve.tensor_tensor(m, m, ab, ALU.add).then_inc(sem["mod_ready"], 1)
                    done += 1
                    dve.wait_ge(sem["mod_ready"], st.at["mod_ready"] + done)
                    for sub in range(3):
                        g = [vec[:, V_G2 + (l * 6 + 2 * sub + e) * KT * 2:
                                 V_G2 + (l * 6 + 2 * sub + e + 1) * KT * 2]
                             .rearrange("p (k v) -> p k v", v=2) for e in range(2)]
                        t = gs[:, l, sub, :, :]
                        dve.tensor_scalar(t, mod[:, l, 3 * sub + 1, :, :], 1.0, None, ALU.add)\
                           .then_inc(sem["mod_ready"], 1)
                        r = gg[:, l, sub, :, :]
                        dve.tensor_scalar(r, mod[:, l, 3 * sub + 2, :, :],
                                          1.0 if sub == 1 else 0.5, None, ALU.mult)\
                           .then_inc(sem["mod_ready"], 1)
                        done += 2
                        dve.wait_ge(sem["mod_ready"], st.at["mod_ready"] + done)
                        dve.tensor_tensor(t, t, g[0], ALU.mult).then_inc(sem["mod_ready"], 1)
                        dve.tensor_tensor(r, r, g[1], ALU.mult).then_inc(sem["mod_ready"], 1)
                        done += 2
                dve.wait_ge(sem["ctx_in"], 16)

            def dve_diff(st):
                n = len(st.units)
                dve.wait_ge(*before(st, "pe"))
                dve.wait_ge(*before(st, "act"))
                dve.wait_ge(*before(st, "dve"))

                def soft(i):
                    nk, sl = (TT if st.units[i][1] < 2 else TX), i % 2
                    dve.wait_ge(sem["s_ready"], st.at["s_ready"] + i + 1)
                    if i >= 2:
                        dve.wait_ge(sem["p_ready"], st.at["p_ready"] + i - 1)
                    dve.tensor_reduce(mx[:, sl, :], PA[:, 2 * sl:2 * sl + 2, 0:nk], AX.X,
                                                ALU.max).then_inc(sem["chain"], chain.up())
                    dve.wait_ge(sem["chain"], chain.n)
                    dve.tensor_scalar(nm[:, sl, :], mx[:, sl, :], -HD ** -0.5, None, ALU.mult)\
                       .then_inc(sem["negmax_ready"], 1)

                def normalise(j):
                    nk, sl = (TT if st.units[j][1] < 2 else TX), j % 2
                    p_1, p_2 = p2_sb[:, sl, 0, 0:nk], p2_sb[:, sl, 1, 0:nk]
                    dve.wait_ge(sem["p_ready"], st.at["p_ready"] + j + 1)
                    dve.reciprocal(ri[:, sl, :], rs[:, sl, :]).then_inc(sem["chain"], chain.up())
                    dve.wait_ge(sem["chain"], chain.n)
                    dve.tensor_scalar(rw[:, sl:sl + 1], ri[:, sl, 1:2], lam[:, 5:6],
                                                None, ALU.mult).then_inc(sem["chain"], chain.up())
                    dve.tensor_scalar(p_1, p_1, ri[:, sl, 0:1], None, ALU.mult).then_inc(sem["chain"], chain.up())
                    dve.wait_ge(sem["chain"], chain.n)
                    dve.scalar_tensor_tensor(out=p_1, in0=p_2, scalar=rw[:, sl:sl + 1], in1=p_1,
                                             op0=ALU.mult, op1=ALU.add)\
                       .then_inc(sem["p_normed"], 1)

                for i in range(n + 3):
                    if i < n:
                        soft(i)
                    if 1 <= i <= n:
                        normalise(i - 1)
                    if i >= 3:
                        j = i - 3
                        dve.wait_ge(sem["o_ready"], st.at["o_ready"] + j + 1)
                        dve.tensor_copy(on[:, j, :], PB[:, j % 2, 0:P]).then_inc(sem["o_taken"], 1)
                dve.wait_ge(sem["o_sqrt_ready"], st.at["o_sqrt_ready"] + 1)
                dve.reciprocal(srec[:, :], sroot[:, :]).then_inc(sem["chain"], chain.up())
                dve.wait_ge(sem["chain"], chain.n)
                for j in range(n):
                    dve.tensor_scalar(on[:, j, :], on[:, j, :], srec[:, j:j + 1], None, ALU.mult)\
                       .then_inc(sem["o_scaled"], 1)
                for h in range(8):
                    dve.wait_ge(sem["ot_ready"], st.at["ot_ready"] + h + 1)
                    dve.tensor_scalar(og[:, h % 2, :], PA[:, h % 4, :], sub_g[:, 0:1], None,
                                      ALU.mult).then_inc(sem["og_ready"], 1)
                    dve.wait_ge(sem["y_hi_ready"], st.at["y_hi_ready"] + h + 1)
                    dve.tensor_tensor(u_lo[:, h, :], og[:, h % 2, :], u_hi[:, h, :].bitcast(F32),
                                      ALU.subtract).then_inc(sem["y_lo_ready"], 1)

            st = plan[0]
            dve.memset(ones[:, :], 1.0 / D).then_inc(sem["ones_ready"], 1)
            dve.memset(eps[:, :], EPS).then_inc(sem["ones_ready"], 1)
            dve.wait_ge(sem["consts_in"], 32)
            for e in range(2):
                a = V_LM + 2 * e * HD
                dve.tensor_tensor_reduce(lam_tmp[:, e, :], vec[:, a:a + HD],
                                         vec[:, a + HD:a + 2 * HD], 1.0, 0.0, ALU.mult, ALU.add,
                                         lam[:, e:e + 1]).then_inc(sem["setup_dve"], 1)
            feed(0)
            feed(1)
            dve.wait_ge(sem["setup_act"], st.at["setup_act"] + 2)
            dve.tensor_tensor(lam[:, 4:5], lam[:, 3:4], lam[:, 2:3], ALU.subtract)\
               .then_inc(sem["setup_dve"], 1)
            dve.tensor_scalar(sub_g[:, :], vec[:, V_SG:V_SG + 1], 1.0 - LAM_INIT, None, ALU.mult)
            dve.wait_ge(sem["setup_dve"], st.at["setup_dve"] + 3)
            dve.tensor_scalar(lam[:, 5:6], lam[:, 4:5], -LAM_INIT, None, ALU.add)\
               .then_inc(sem["setup_dve"], 1)
            dve.wait_ge(sem["x_in"], 16)
            dve.wait_ge(sem["mem_in"], 16)
            run = dict(norm=dve_norm, proj=dve_proj, ffn_in=dve_ffn_in, ffn_out=dve_ffn_out,
                       attn=dve_attn, index=dve_index, mix=dve_mix, ada=dve_ada, diff=dve_diff)
            for st in plan[1:]:
                run[st.kind](st)

        @block.gpsimd
        def _(pool):
            st = [s for s in plan if s.kind == "attn" and s.which == "n"][0]
            pool.wait_ge(*before(st, "pe"))
            pool.wait_ge(*before(st, "act"))
            pool.wait_ge(*before(st, "dve"))
            for i, (h, qt, _) in enumerate(st.units):
                if i >= 2:
                    pool.wait_ge(sem["negmax_ready"], st.at["negmax_ready"] + i - 1)
                pool.dma_start(na_bias[:, i % 2, :], bias_in[:, h, qt, :])\
                    .then_inc(sem[f"bias_in{i % 2}"], 16)
                pool.wait_ge(sem[f"bias_in{i % 2}"], 16 * (i // 2 + 1))
                rows = na_bias[:, i % 2, :].rearrange("p (r c) -> p r c", c=HD)
                window = cst[:, C_WM:C_WM + HD][:, None, :].broadcast_to((P, 4, HD))
                pool.tensor_tensor(rows, rows, window, ALU.add).then_inc(sem["bias_ready"], 1)


def pack(w, nk=KT):
    n = w.shape[1] // 256
    return w.reshape(nk, P, n, 256).transpose(2, 1, 0, 3).reshape(n, P, nk * 256)


def pack_ffn_in(w):
    n = D_FF // P
    return w.reshape(KT, P, 2, n, P).transpose(3, 1, 0, 2, 4).reshape(n, P, SLAB)


def pack_mix(w_mix, w_up):
    a = w_mix.reshape(KT, P, KT, P).transpose(2, 1, 0, 3)
    b = w_up.reshape(4, P, KT, P).transpose(2, 1, 0, 3)
    return np.concatenate([a, b], axis=2).reshape(KT, P, SLAB_MIX)


def lay_out(a):
    s16, s22, s12 = [], [], []
    for l in range(DEPTH):
        w = a["w_in"][l]
        col = lambda i, n=1: w[:, i * BW:(i + n) * BW]
        s16 += [pack(col(0)), pack(col(1)), pack(col(2)), pack(col(3)), pack(col(8))]
        small = np.zeros((D, 256), np.float32)
        o = 9 * BW
        small[:, 0:HD] = w[:, o:o + HD]
        small[:, HD:P] = w[:, o:o + HD]
        small[:, P:P + NH1] = w[:, o + HD:o + HD + NH1]
        s16.append(pack(small))
        s16 += [pack(col(4)), pack(col(5)), pack(col(6)), pack(col(7))]
        o += HD + NH1
        s16 += [pack(a["w_mem_kv"][l]), pack(w[:, o:o + 2 * BW])]
        o += 2 * BW
        for b in range(3):
            s12.append(pack_mix(w[:, o + b * D:o + (b + 1) * D], a["w_branch"][l, b]))
        s16.append(pack(a["w_out"][l]))
    for l in range(DEPTH):
        s16.append(pack(a["ada_w_2"][l]))
    for l in range(DEPTH):
        for f in range(2):
            s16.append(pack_ffn_in(a["ffn_w_in_2"][l, f]))
            w = a["ffn_w_out_2"][l, f]
            s22 += [pack(w[0:FH * P], FH), pack(w[FH * P:], FH)]
            if f == 0:
                m = ("da", "na")[l]
                s16 += [pack(a[f"{m}_w_in_2"][0]), pack(a[f"{m}_w_out_2"][0])]
    cols = lambda v: v.reshape(-1, P).T
    two = lambda v: np.repeat(cols(v), 2, axis=1)
    vec = np.concatenate([
        cols(a["norm_g"]), cols(a["mem_norm_g"]), cols(a["final_g"]), two(a["norm_g_2"]),
        two(a["ada_b_2"]), cols(a["da_subln_g_2"]),
        np.stack([cols(a["c_2"]), cols(a["c_ctx_2"])], axis=2).reshape(P, 2 * KT),
        np.broadcast_to(a["da_lambda_2"].reshape(1, -1), (P, 4 * HD))], axis=1)
    rpb = np.zeros((16, 15, 127), np.float32)
    rpb[:, :, 48:79] = a["na_rpb_2"][0]
    bias = np.empty((P, 16, 2, 4, HD), np.float32)
    for p in range(P):
        for i in range(2):
            r, c = 2 * i + p // HD, p % HD
            bias[p, :, i] = rpb[:, 7 - r:11 - r, 63 - c:127 - c]
    tr = lambda t: t.reshape(TX, KT, P).transpose(2, 1, 0)
    return dict(x=tr(a["x"]), mem=tr(a["mem"]), ctx=tr(a["ctx_2"]), vec=vec, cst=constants(),
                bias=bias.reshape(P, 16, 2, TX), w16=np.concatenate(s16), w22=np.concatenate(s22),
                w12=np.concatenate(s12))


def constants():
    t = np.arange(TX, dtype=np.float32)
    c = np.zeros((P, NC), np.float32)
    c[:, C_ID:C_ID + P] = np.eye(P)
    f1 = (np.float32(500000.0) ** (-np.arange(8, dtype=np.float32) / np.float32(8)))
    f1 = f1.astype(np.float32)
    f2 = (np.float32(10000.0) ** (-np.arange(16, dtype=np.float32) / np.float32(16)))
    f2 = f2.astype(np.float32)
    for p in range(P):
        d = p % HD
        cos, sin = np.ones(TX), np.zeros(TX)
        if d < 16:
            ang = (t * f1[d % 8]).astype(np.float32)
            cos, sin = np.cos(ang), np.sin(ang) * (-1 if d < 8 else 1)
        c[p, C_R1:C_R1 + TX], c[p, C_R1 + TX:C_R1 + 2 * TX] = cos, sin
        pos = (np.arange(TX) // 64 if d < 32 else np.arange(TX) % 64).astype(np.float32)
        ang = (pos * f2[d % 16]).astype(np.float32)
        c[p, C_R2:C_R2 + TX] = np.cos(ang)
        c[p, C_R2 + TX:C_R2 + 2 * TX] = np.sin(ang) * (-1 if d % 32 < 16 else 1)
        c[p, C_CM + P:C_CM + 2 * P] = np.where(np.arange(P) <= p, 0.0, NEG)
        start = min(max(d - 8, 0), HD - 16)
        k = np.arange(HD)
        c[p, C_WM:C_WM + HD] = np.where((k >= start) & (k < start + 16), 0.0, -1e9)
    return c


def kernel(**inputs):
    import concourse.bacc as bacc
    from concourse.bass_utils import run_bass_kernel_spmd

    a = {k: np.asarray(v) for k, v in inputs.items() if not k.startswith("rw_")}
    laid = {k: np.ascontiguousarray(v) for k, v in lay_out(a).items()}
    nc = bacc.Bacc("TRN2", target_bir_lowering=False, num_devices=1)
    args = {k: nc.dram_tensor(f"in_{k}", v.shape, F32, kind="ExternalInput").ap()
            for k, v in laid.items()}
    out = nc.dram_tensor("out", (P, KT, TX), F32, kind="ExternalOutput").ap()
    build(nc, args["x"], args["mem"], args["ctx"], args["vec"], args["cst"], args["bias"],
          args["w16"], args["w22"], args["w12"], out)
    r = run_bass_kernel_spmd(nc, [{f"in_{k}": v for k, v in laid.items()}], core_ids=[0])
    got = r.results[0]["out"]
    return np.ascontiguousarray(got.transpose(2, 1, 0)).reshape(1, TX, D)
```

```python
import math
from contextlib import ExitStack

import numpy as np
import concourse.bass as bass
from concourse import mybir

F32 = mybir.dt.float32
F32R = mybir.dt.float32r
ACT = mybir.ActivationFunctionType
ALU = mybir.AluOpType
AX = mybir.AxisListType

P = 128
D = 1024
KT = D // P
TX = 256
TT = 2 * TX
DEPTH = 2
BW = 512
NH1 = 8
HD = 64
TOPK = 64
D_FF = 2816
FH = D_FF // P // 2
EPS = 1e-6
NP = 3
NSQ = 4
NEG = -1e30
TAKEN = -3e38
SLAB = KT * 256
SLAB_OUT = FH * 256
SLAB_MIX = (KT + 4) * P
LAM_INIT = 0.8 - 0.6 * math.exp(-0.3 * 0)

V_NG = 0
V_MG = V_NG + DEPTH * KT
V_FG = V_MG + DEPTH * KT
V_G2 = V_FG + KT
V_AB = V_G2 + DEPTH * 6 * KT * 2
V_SG = V_AB + DEPTH * 9 * KT * 2
V_C = V_SG + 1
V_LM = V_C + 2 * KT
NV = V_LM + 4 * HD
C_ID = 0
C_R1 = C_ID + P
C_R2 = C_R1 + 2 * TX
C_CM = C_R2 + 2 * TX
C_WM = C_CM + 2 * P
C_TU = C_WM + HD
NC = C_TU + 4 * 12
AB = 12
AN = 3 * DEPTH
AR = 6
AH = 4


class Stage:

    def __init__(self, kind, counts, last, slabs=(), src=None, T=TT, apply=None, l=0, sub=0,
                 mod=False, steps=(), which=None, units=(), groups=1, half=0, stat=None,
                 more=False):
        self.kind, self.counts, self.last, self.slabs = kind, counts, last, slabs
        self.src, self.T, self.apply, self.l, self.sub, self.mod = src, T, apply, l, sub, mod
        self.steps, self.which, self.units, self.groups = steps, which, units, groups
        self.half, self.stat, self.more, self.late = half, stat, more, False


def norm(apply, T, stat, more=True, **par):
    counts = dict(sqrt_ready=1, rms_ready=1, r_ready=1, scaled=KT)
    last = dict(pe="r_ready", act="sqrt_ready", dve="rms_ready")
    if stat == "own":
        counts |= dict(sq_ready=KT, stat_used=KT)
    if apply == "split":
        counts |= dict(u_hi_ready=KT, u_lo_ready=KT)
        last |= dict(act="u_hi_ready", dve="u_lo_ready")
    else:
        counts |= dict(x_ready=KT)
        last |= dict(dve="x_ready")
    if apply == "resid":
        counts |= dict(sq_ready=KT * more, stat_used=1 + KT * more)
        if more:
            last |= dict(pe="stat_used", act="sq_ready")
    return Stage("norm", counts, last, T=T, apply=apply, stat=stat, more=more, **par)


def out_y(kind, T, slabs, src, **par):
    counts = dict(slab_done=4, tile_done=4, sq_ready=KT, sum_ready=KT - 2)
    if kind == "ffn_out":
        counts |= dict(y_ready=KT)
    return Stage(kind, counts, dict(pe="slab_done", act="sq_ready", dve="sum_ready"), slabs,
                 T=T, src=src, **par)


def proj(steps):
    act = sum(s[0] in ("copy", "silu", "scale", "nat") for s in steps)
    rope = sum(s[0] in ("rope1", "rope2", "index") for s in steps)
    counts = dict(slab_done=len(steps), taken_act=act, taken_dve=len(steps) - act, out_dve=rope)
    last = dict(pe="slab_done")
    if act:
        last["act"] = "taken_act"
    if act < len(steps):
        last["dve"] = "out_dve" if rope else "taken_dve"
    return Stage("proj", counts, last, [SLAB] * len(steps), steps=steps)


def attn(which, heads):
    if which in "ab":
        units = [[(h, 0, 0, P), (h, 1, P, TX)] for h in range(heads)]
    elif which == "m":
        units = [[(h, 0, 0, TX), (h, 1, TX, TX)] for h in range(heads)]
    else:
        units = [[(h, i, 0, TT)] for h in range(heads) for i in range(2)]
    n, groups = len(units), heads if which == "m" else heads // 2
    counts = dict(s_ready=n, negmax_ready=n, p_ready=n, p_normed=n, pt_ready=n, pt_copied=n,
                  o_ready=n, o_taken=groups, y_hi_ready=1, y_lo_ready=1)
    return Stage("attn", counts, dict(pe="o_ready", act="y_hi_ready", dve="y_lo_ready"),
                 which=which, units=units, groups=groups)


def ffn(l, sub, T, stat, more=True):
    out = [norm("split", T, stat, l=l, sub=sub, mod=True)]
    for half in range(2):
        out.append(Stage("ffn_in", dict(slab_done=FH, silu_ready=FH, h_ready=FH, g_hi_ready=FH,
                                        g_lo_ready=FH),
                         dict(pe="slab_done", act="g_hi_ready", dve="g_lo_ready"),
                         [SLAB] * FH, T=T, half=half))
        if half == 0:
            out.append(Stage("ffn_out", dict(slab_done=4, tile_done=4, taken_act=4),
                             dict(pe="slab_done", act="taken_act"), [SLAB_OUT] * 4, T=T, half=0))
        else:
            out.append(out_y("ffn_out", T, [SLAB_OUT] * 4, "g", half=1))
    out.append(norm("resid", T, "PA3", more=more, l=l, sub=sub))
    return out


def make_plan():
    plan = [Stage("setup", dict(setup_act=2, setup_dve=4), dict(act="setup_act", dve="setup_dve"))]
    for l in range(DEPTH):
        plan.append(norm("split", TT, "own", l=l))
        qkvg = [("rope1", "q", 2 * i, 0, TX) for i in range(2)]
        qkvg += [("rope1", "k", 2 * i, 0, TX) for i in range(2)]
        qkvg += [("nat", "v", i, 0, TX) for i in range(2)]
        qkvg += [("silu", "g", 2 * i, 0, TX) for i in range(2)]
        plan.append(proj(qkvg))
        plan.append(attn("a", NH1))
        plan.append(proj([("rope1", "iq", 0, 0, TX), ("rope1", "iq", 2, 0, TX),
                          ("index", "ik", 0, 0, TX)]))
        plan.append(Stage("index", dict(is_ready=16, relu_ready=16, acc_ready=16, topk_ready=2),
                          dict(pe="is_ready", act="relu_ready", dve="topk_ready")))
        plan.append(proj(qkvg))
        plan.append(attn("b", NH1))
        plan.append(proj([("copy", "k", 0, TX, TX), ("copy", "k", 2, TX, TX),
                          ("nat", "v", 0, TX, TX), ("nat", "v", 1, TX, TX),
                          ("copy", "q", 0, 0, TX), ("copy", "q", 2, 0, TX),
                          ("silu", "g", 0, 0, TX), ("silu", "g", 2, 0, TX)]))
        plan.append(attn("m", 4))
        plan.append(Stage("mix", dict(slab_done=24, gate_ready=24, up_taken=24, merged=24,
                                      m_hi_ready=1, m_lo_ready=1),
                          dict(pe="slab_done", act="m_hi_ready", dve="m_lo_ready"),
                          [SLAB_MIX] * 24))
        plan.append(proj([("add_x", "X", 2 * i, 0, TX) for i in range(4)]))
    plan.append(norm("plain", TX, "own"))
    plan.append(Stage("ada", dict(ada_hi_ready=AB * AN, ada_split=AB * AN, ada_used=AB * AN,
                                  rows_copied=AN, rows_moved=48 * AN, turned=AN,
                                  mod_ready=AN + 4, c_ready=1, c_hi_ready=1),
                      dict(pe="turned", act="rows_copied", dve="mod_ready")))
    for l in range(DEPTH):
        plan += ffn(l, 0, TT, "own" if l == 0 else "PB2")
        plan.append(norm("split", TT, "PB2", l=l, sub=1, mod=True))
        T = TT if l == 0 else TX
        q = "rope2" if l == 0 else "scale"
        k = "rope2" if l == 0 else "copy"
        plan.append(proj([(q, "Q", 2 * i, 0, T) for i in range(4)] +
                         [(k, "K", 2 * i, 0, TT) for i in range(4)] +
                         [("nat", "V", i, 0, TT) for i in range(4)]))
        if l == 0:
            n = 32
            plan.append(Stage("diff", dict(s_ready=n, negmax_ready=n, p_ready=n, p_normed=n,
                                           pt_ready=n, pt_copied=n, o_ready=n, o_taken=n,
                                           o_sq_ready=n, o_sqrt_ready=1, o_scaled=n, ot_ready=8,
                                           og_ready=8, y_hi_ready=8, y_lo_ready=8),
                              dict(pe="ot_ready", act="y_hi_ready", dve="y_lo_ready"),
                              units=[(h, t) for h in range(8) for t in range(4)]))
        else:
            plan.append(attn("n", 16))
        plan.append(out_y("proj_y", T, [SLAB] * 4, "u"))
        plan.append(norm("resid", T, "PB3", l=l, sub=1))
        plan += ffn(l, 2, T, "PB2", more=l + 1 < DEPTH)
    for n, st in enumerate(plan):
        if st.apply == "resid" and st.more:
            plan[n + 2].late = True
    at, last, sizes = {}, {}, []
    for n, st in enumerate(plan):
        st.at, st.before, st.s0 = dict(at), dict(last), len(sizes)
        sizes += st.slabs
        for name, count in st.counts.items():
            at[name] = at.get(name, 0) + count
        for name in st.counts:
            st.at.setdefault(name, 0)
        for engine, name in st.last.items():
            last[engine] = (name, at[name])
    return plan, at, last, sizes


def build(nc, x_in, mem_in, ctx_in, vec_in, cst_in, bias_in, w16, w22, w12, w_ada, out):
    plan, totals, finals, sizes = make_plan()
    ns = len(sizes)

    with ExitStack() as ctx:
        base = 16512

        def sb(name, shape, dt, at):
            return nc.alloc_sbuf_tensor_at(name, [P] + shape, dt, offset=base + at)

        kb = 1024
        raw = [sb(f"raw{u}", [SLAB_OUT], F32, 11 * kb * u) for u in range(2)]
        wh = [sb(f"w_hi{u}", [SLAB_OUT], F32R, 22 * kb + 11 * kb * u) for u in range(2)]
        wl = [sb(f"w_lo{u}", [SLAB_OUT], F32R, 44 * kb + 11 * kb * u) for u in range(2)]
        u_hi = sb("u_hi", [KT, TT], F32R, 66 * kb)
        u_lo = sb("u_lo", [KT, TT], F32R, 82 * kb)
        X = sb("X", [KT, TT], F32, 98 * kb)
        YO = 114 * kb
        Y = sb("Y", [KT, TT], F32, YO)
        q1, k1, g1 = [sb(f"{n}1", [4, TX], F32, YO + 4 * kb * i) for i, n in enumerate("qkg")]
        v1 = sb("v1", [2, BW], F32, YO + 12 * kb)
        merged = sb("merged", [KT, TX], F32, YO)
        Q = sb("Q", [KT, TT], F32, YO)
        qn = sb("qn", [KT, TX], F32, YO)
        on = sb("on", [32, P], F32, YO)
        GO = 130 * kb
        g_hi = sb("g_hi", [FH, TT], F32R, GO)
        g_lo = sb("g_lo", [FH, TT], F32R, GO + 22 * kb)
        y_hi = sb("y_hi", [12, TX], F32R, GO)
        y_lo = sb("y_lo", [12, TX], F32R, GO + 22 * kb)
        iq = sb("iq", [4, TX], F32, GO + 12 * kb)
        ik = sb("ik", [TX], F32, GO + 16 * kb)
        sel_bias = sb("sel_bias", [2, TX], F32, GO + 17 * kb)
        idx_acc = sb("idx_acc", [2, TX], F32, GO + 19 * kb)
        K = sb("K", [KT, TT], F32, GO)
        V = sb("V", [4, D], F32, GO + 16 * kb)
        na_bias = sb("na_bias", [2, TT], F32, GO + 32 * kb)
        ada_raw = [sb(f"ada_raw{u}", [SLAB], F32, YO + 8 * kb * u) for u in range(AR)]
        ada_lo = [sb(f"ada_lo{u}", [SLAB], F32R, YO + 8 * kb * u) for u in range(AR)]
        ada_hi = [sb(f"ada_hi{u}", [SLAB], F32R, 66 * kb + 8 * kb * u) for u in range(AH)]
        ada_rows = sb("ada_rows", [4 * 256], F32, YO + 50 * kb)
        ada_turn = sb("ada_turn", [P], F32, YO + 54 * kb)
        c_f32 = sb("c_f32", [KT, 160], F32, 174 * kb)
        c_split = sb("c_split", [KT, 160], F32R, 182 * kb)
        SO = 174 * kb
        sq = sb("sq", [NSQ, TT], F32, SO)
        sqsum = sb("sqsum", [TT], F32, SO + 8 * kb)
        rms_root = sb("rms_root", [P], F32, SO + 10 * kb)
        rms = sb("rms", [P], F32, SO + 10 * kb + 512)
        scaled = sb("scaled", [2, TT], F32, SO + 11 * kb)
        silu = sb("silu", [2, TT], F32, SO)
        h_f32 = sb("h_f32", [2, TT], F32, SO + 4 * kb)
        shuf = sb("shuf", [2, TX], F32, SO)
        sig = sb("sig", [2, TX], F32, SO)
        upg = sb("upg", [2, TX], F32, SO + 2 * kb)
        relu = sb("relu", [2, TX], F32, SO)
        s_sb = sb("s_sb", [NP, TT], F32, SO)
        p_sb = sb("p_sb", [NP, TT], F32, SO + 6 * kb)
        pt_sb = sb("pt_sb", [2, TT], F32, SO + 12 * kb)
        p2_sb = sb("p2_sb", [NP, 2, TT], F32, SO)
        og = sb("og", [2, TT], F32, SO)
        CO = 190 * kb
        cst = sb("cst", [NC], F32, CO)
        CO += 4 * NC
        vec = sb("vec", [NV], F32, CO)
        CO += -(-4 * NV // 32) * 32
        ones = sb("ones", [P], F32, CO)
        spread = sb("spread", [4, P], F32, CO + 512)
        CO += 2048
        mod = sb("mod", [DEPTH, 9, KT, 2], F32, CO + 512)
        CO += 512 + 4 * DEPTH * 9 * KT * 2
        gs = sb("gs", [DEPTH, 3, KT, 2], F32, CO)
        gg = sb("gg", [DEPTH, 3, KT, 2], F32, CO + 4 * DEPTH * 3 * KT * 2)
        CO += 8 * DEPTH * 3 * KT * 2
        wi = sb("wi", [2, NH1], F32, CO)
        top8 = sb("top8", [8], F32, CO + 64)
        eps = sb("eps", [2], F32, CO + 96)
        lam = sb("lam", [8], F32, CO + 128)
        mx = sb("mx", [NP, 2], F32, CO + 160)
        nm = sb("nm", [NP, 2], F32, CO + 192)
        rs = sb("rs", [NP, 2], F32, CO + 224)
        ri = sb("ri", [4, 2], F32, CO + 256)
        rw = sb("rw", [NP], F32, CO + 288)
        sub_g = sb("sub_g", [1], F32, CO + 320)
        ssq = sb("ssq", [32], F32, CO + 352)
        sroot = sb("sroot", [32], F32, CO + 480)
        srec = sb("srec", [32], F32, CO + 608)
        lam_tmp = sb("lam_tmp", [2, HD], F32, CO + 736)
        r2 = sb("r2", [NP], F32, CO + 736 + 512 + 512)
        osq = sb("osq", [P], F32, CO + 736 + 512)
        CO += 736 + 1024 + 32
        assert base + CO <= 229368, CO

        PA = ctx.enter_context(nc.psum_tensor("PA", [P, 4, 512], F32))
        PB = ctx.enter_context(nc.psum_tensor("PB", [P, 4, 512], F32))

        ident = cst[:, C_ID:C_ID + P]
        dest = dict(q=q1, k=k1, g=g1, v=v1, iq=iq, ik=ik, Q=Q, K=K, V=V, Y=Y, X=X)

        names = set(totals) | {"raw_full0", "raw_full1", "w_hi_ready", "w_split", "chain",
                               "ones_ready", "consts_in", "x_in", "mem_in", "ctx_in", "bias_in0",
                               "bias_in1", "no_bias", "c_zero", "stored", "bias_ready"}
        names |= {f"ada_full{u}" for u in range(AR)}
        sem = {n: ctx.enter_context(nc.semaphore(n)) for n in sorted(names)}
        raw_full = [sem["raw_full0"], sem["raw_full1"]]
        block = ctx.enter_context(nc.Block())

        def before(st, engine):
            name, value = st.before.get(engine, ("ones_ready", 8))
            return sem[name], value

        def stat_bank(st):
            return PB[:, 2, :] if st.stat in ("own", "PB2") else \
                PA[:, 3, :] if st.stat == "PA3" else PB[:, 3, :]

        def width(unit):
            return sum(nk for _, _, _, nk in unit)

        class Chain:

            n = 0

            def up(self):
                self.n += 1
                return 1

        @block.sync
        def _(sp):
            sp.dma_start(X[:, :, 0:TX], x_in).then_inc(sem["x_in"], 16)
            sp.dma_start(X[:, :, TX:TT], mem_in).then_inc(sem["mem_in"], 16)
            src = {SLAB: w16, SLAB_OUT: w22, SLAB_MIX: w12}
            used = {SLAB: 0, SLAB_OUT: 0, SLAB_MIX: 0}
            ada = [st for st in plan if st.kind == "ada"][0]
            out_proj = plan[plan.index(ada) - 2]

            def load_ada():
                for engine in ("pe", "act", "dve"):
                    sp.wait_ge(*before(out_proj, engine))
                for j in range(AR):
                    sp.dma_start(ada_raw[j][:, :], w_ada[j, :, :])\
                      .then_inc(sem[f"ada_full{j}"], 16)
                with sp.Fori(0, AB * AN // AR - 1) as i:
                    for u in range(AR):
                        sp.wait_ge(sem["ada_used"], i * AR + (u + 1))
                        sp.dma_start(ada_raw[u][:, :], w_ada[bass.ds(i * AR + (AR + u), 1), :, :]
                                     .rearrange("a p n -> p (a n)"))\
                          .then_inc(sem[f"ada_full{u}"], 16)

            s = 0
            while s < ns:
                if s == ada.s0 + 2:
                    load_ada()
                size, n = sizes[s], 1
                while s + n < ns and sizes[s + n] == size and s + n != ada.s0 + 2:
                    n += 1
                pairs = (n - 2) // 2 if s == 0 else n // 2

                def load(s, half, index):
                    if not isinstance(s, int) or s >= 2:
                        sp.wait_ge(sem["w_split"], s - 1)
                    sp.dma_start(raw[half][:, 0:size],
                                 src[size][bass.ds(index, 1), :, :].rearrange("a p n -> p (a n)"))\
                      .then_inc(raw_full[half], 16)

                first = used[size]
                done = 0
                if s == 0:
                    load(0, 0, first)
                    load(1, 1, first + 1)
                    done = 2
                if pairs > 1:
                    with sp.Fori(0, pairs) as i:
                        for p in range(2):
                            load(i * 2 + (s + done + p), (s + done + p) % 2,
                                 i * 2 + (first + done + p))
                    done += 2 * pairs
                for p in range(done, n):
                    load(s + p, (s + p) % 2, first + p)
                used[size] += n
                s += n
            name, value = finals["dve"]
            sp.wait_ge(sem[name], value)
            sp.dma_start(out, X[:, :, 0:TX]).then_inc(sem["stored"], 16)
            sp.wait_ge(sem["stored"], 16)

        @block.tensor
        def _(pe):
            def mm3(psum, u, wcol, hi, lo, first, last):
                whi, wlo = wh[u][:, wcol:wcol + P], wl[u][:, wcol:wcol + P]
                pe.matmul(psum, whi, hi, start=first, stop=False)
                pe.matmul(psum, whi, lo, start=False, stop=False)
                return pe.matmul(psum, wlo, hi, start=False, stop=last)

            def nat3(psum, u, c0, c1, k, hi, lo, first, last):
                whi, wlo = wh[u][:, k * 256 + c0:k * 256 + c1], wl[u][:, k * 256 + c0:k * 256 + c1]
                pe.matmul(psum, hi, whi, start=first, stop=False)
                pe.matmul(psum, lo, whi, start=False, stop=False)
                return pe.matmul(psum, hi, wlo, start=False, stop=last)

            def add_squares(bank, tile, T, first, last):
                for t in range(T // P):
                    mm = pe.matmul(bank[32 * t:32 * t + 32, 0:P], ones[:, 0:32],
                                   tile[:, t * P:t * P + P], start=first, stop=last)
                return mm

            def pe_norm(st):
                T = st.T
                bank = stat_bank(st)
                pe.wait_ge(*before(st, "act"))
                pe.wait_ge(*before(st, "dve"))
                if st.stat == "own":
                    for k in range(KT):
                        pe.wait_ge(sem["sq_ready"], st.at["sq_ready"] + k + 1)
                        add_squares(bank, sq[:, k % NSQ, :], T, k == 0, k == KT - 1)\
                            .then_inc(sem["stat_used"], 1)
                if st.apply == "resid":
                    pe.wait_ge(sem["sum_ready"], st.at["sum_ready"])
                    add_squares(bank, sqsum, T, True, False)
                    pe.wait_ge(sem["sq_ready"], st.at["sq_ready"])
                    add_squares(bank, sq[:, (KT - 1) % NSQ, :], T, False, True)\
                        .then_inc(sem["stat_used"], 1)
                pe.wait_ge(sem["rms_ready"], st.at["rms_ready"] + 1)
                for t in range(T // P):
                    mm = pe.matmul(bank[:, t * P:t * P + P], spread[0:T // 4, t, :],
                                   rms[0:T // 4, :], start=True, stop=True)
                mm.then_inc(sem["r_ready"], 1)
                if st.apply == "resid" and st.more:
                    for k in range(KT):
                        pe.wait_ge(sem["sq_ready"], st.at["sq_ready"] + k + 1)
                        add_squares(PB[:, 2, :], sq[:, k % NSQ, :], T, k == 0, k == KT - 1)\
                            .then_inc(sem["stat_used"], 1)

            def operand(st):
                if st.before["dve"][0] == "u_lo_ready":
                    return True
                prev = plan[plan.index(st) - 1]
                if prev.kind == "attn" and prev.which != "n":
                    pe.wait_ge(sem["o_taken"], st.at["o_taken"])
                    pe.wait_ge(sem["p_ready"], st.at["p_ready"])
                    pe.wait_ge(sem["pt_copied"], st.at["pt_copied"])
                    return False
                pe.wait_ge(*before(st, "act"))
                pe.wait_ge(*before(st, "dve"))
                return False

            def first_slab(st, out, t0, T):
                pe.wait_ge(sem["w_split"], st.s0 + 1)
                for k in range(KT):
                    pe.wait_ge(sem["u_lo_ready"], st.at["u_lo_ready"] - KT + k + 1)
                    for c in range(2):
                        mm = mm3(out[c], st.s0 % 2, k * 256 + c * P, u_hi[:, k, t0:t0 + T],
                                 u_lo[:, k, t0:t0 + T], k == 0, k == KT - 1)
                mm.then_inc(sem["slab_done"], 1)

            def pe_proj(st):
                by_tile = operand(st)
                act = dve = 0
                taken = []
                for i, (how, to, tile, t0, T) in enumerate(st.steps):
                    s = st.s0 + i
                    u, ps = s % 2, i % 2
                    if i == 0 and by_tile:
                        first_slab(st, [PA[:, c, 0:T] for c in range(2)], t0, T)
                        taken.append(("taken_dve", 1) if how.startswith("rope") else
                                     ("taken_act", 1))
                        act, dve = (0, 1) if how.startswith("rope") else (1, 0)
                        continue
                    if i >= 2:
                        pe.wait_ge(sem[taken[i - 2][0]], st.at[taken[i - 2][0]] + taken[i - 2][1])
                    pe.wait_ge(sem["w_split"], s + 1)
                    if how == "nat":
                        for t in range(T // P):
                            po = PA[:, 2 * ps + t // 2, (t % 2) * 256:(t % 2) * 256 + 256]
                            tok = slice(t0 + t * P, t0 + t * P + P)
                            for k in range(KT):
                                mm = nat3(po, u, 0, 256, k, u_hi[:, k, tok], u_lo[:, k, tok],
                                          k == 0, k == KT - 1)
                    elif how == "index":
                        for k in range(KT):
                            mm3(PA[:, 2 * ps, 0:TX], u, k * 256, u_hi[:, k, 0:TX],
                                u_lo[:, k, 0:TX], k == 0, k == KT - 1)
                        for t in range(2):
                            po = PA[:, 2 * ps, TX + 8 * t:TX + 8 * t + 8]
                            tok = slice(t * P, t * P + P)
                            for k in range(KT):
                                mm = nat3(po, u, P, P + NH1, k, u_hi[:, k, tok],
                                          u_lo[:, k, tok], k == 0, k == KT - 1)
                    else:
                        for c in range(2):
                            po = PA[:, 2 * ps + c, 0:T]
                            for k in range(KT):
                                mm = mm3(po, u, k * 256 + c * P, u_hi[:, k, t0:t0 + T],
                                         u_lo[:, k, t0:t0 + T], k == 0, k == KT - 1)
                    mm.then_inc(sem["slab_done"], 1)
                    if how in ("copy", "silu", "scale", "nat"):
                        act += 1
                        taken.append(("taken_act", act))
                    else:
                        dve += 1
                        taken.append(("taken_dve", dve))

            def pe_ffn_in(st):
                T = st.T
                by_tile = operand(st)

                def step(i, p):
                    s = st.s0 + p
                    u, ps = s % 2, p % 2
                    if not isinstance(i, int) or i + p >= 2:
                        pe.wait_ge(sem["h_ready"], st.at["h_ready"] + (i + (p - 1)))
                    pe.wait_ge(sem["w_split"], i + (s + 1))
                    for c in range(2):
                        for k in range(KT):
                            mm = mm3(PA[:, 2 * ps + c, 0:T], u, k * 256 + c * P, u_hi[:, k, 0:T],
                                     u_lo[:, k, 0:T], k == 0, k == KT - 1)
                    mm.then_inc(sem["slab_done"], 1)

                if by_tile:
                    first_slab(st, [PA[:, c, 0:T] for c in range(2)], 0, T)
                else:
                    step(0, 0)
                step(0, 1)
                with pe.Fori(0, (FH - 3) // 2) as i:
                    step(i * 2, 2)
                    step(i * 2, 3)
                step(0, FH - 1)

            def pe_out(st):
                T = st.T
                pe.wait_ge(*before(st, "act"))
                pe.wait_ge(*before(st, "dve"))
                ffn = st.kind == "ffn_out"
                nk, hi, lo, bank = (FH, g_hi, g_lo, PB) if ffn else (KT, u_hi, u_lo, PA)
                for p in range(4):
                    s = st.s0 + p
                    u, ps = s % 2, p % 2
                    if p >= 2:
                        if not ffn:
                            pe.wait_ge(sem["sq_ready"], st.at["sq_ready"] + 2 * (p - 1))
                        elif st.half == 0:
                            pe.wait_ge(sem["taken_act"], st.at["taken_act"] + p - 1)
                        else:
                            pe.wait_ge(sem["y_ready"], st.at["y_ready"] + 2 * (p - 1))
                    pe.wait_ge(sem["w_split"], s + 1)
                    for c in range(2):
                        for k in range(nk):
                            mm = mm3(bank[:, 2 * ps + c, 0:T], u, k * 256 + c * P, hi[:, k, 0:T],
                                     lo[:, k, 0:T], k == 0, k == nk - 1)
                        mm.then_inc(sem[("tile_done", "slab_done")[c]], 1)

            def pe_attn(st):
                pe.wait_ge(*before(st, "act"))
                pe.wait_ge(*before(st, "dve"))
                n, w = len(st.units), st.which
                per = n // st.groups
                for i in range(n + 3):
                    if i < n:
                        if i >= 4:
                            pe.wait_ge(sem["p_ready"], st.at["p_ready"] + i - 3)
                        for h, qt, off, nk in st.units[i]:
                            mm = scores(w, h, qt, PA[:, i % 4, off:off + nk], nk)
                        mm.then_inc(sem["s_ready"], 1)
                    if 2 <= i < n + 2:
                        j = i - 2
                        pe.wait_ge(sem["p_normed"], st.at["p_normed"] + j + 1)
                        if j >= 2:
                            pe.wait_ge(sem["pt_copied"], st.at["pt_copied"] + j - 1)
                        for b in range(width(st.units[j]) // P):
                            mm = pe.transpose(PB[:, 2 + j % 2, b * P:b * P + P],
                                              p_sb[:, j % NP, b * P:b * P + P], ident)
                        mm.then_inc(sem["pt_ready"], 1)
                    if i >= 3:
                        j = i - 3
                        g = j // per
                        if g >= 2 and j % per == 0:
                            pe.wait_ge(sem["o_taken"], st.at["o_taken"] + g - 1)
                        pe.wait_ge(sem["pt_copied"], st.at["pt_copied"] + j + 1)
                        for h, qt, off, nk in st.units[j]:
                            m = P if w == "m" else HD
                            p0 = 0 if w == "m" else HD * (h % 2)
                            values = V if w == "n" else v1
                            for b in range(nk // P):
                                mm = pe.matmul(PB[p0:p0 + m, g % 2, qt * P:qt * P + P],
                                               values[:, b, h * m:h * m + m],
                                               pt_sb[:, j % 2, off + b * P:off + b * P + P],
                                               start=(b == 0), stop=(b == nk // P - 1))
                        mm.then_inc(sem["o_ready"], 1)

            def scores(w, h, qt, bank, nk):
                if w == "m":
                    return pe.matmul(bank, q1[:, h, qt * P:qt * P + P], k1[:, h, 0:nk],
                                     start=True, stop=True)
                p0 = HD * (h % 2)
                q_, k_ = (q1, k1) if w in "ab" else (qn, K)
                return pe.matmul(bank, q_[p0:p0 + HD, h // 2, qt * P:qt * P + P],
                                 k_[p0:p0 + HD, h // 2, 0:nk], start=True, stop=True)

            def pe_index(st):
                pe.wait_ge(*before(st, "act"))
                pe.wait_ge(*before(st, "dve"))
                for j in range(16):
                    qt, h = j // 8, j % 8
                    p0, nk = HD * (h % 2), (qt + 1) * P
                    if j >= 4:
                        pe.wait_ge(sem["relu_ready"], st.at["relu_ready"] + j - 3)
                    pe.matmul(PA[:, j % 4, 0:nk], iq[p0:p0 + HD, h // 2, qt * P:qt * P + P],
                              ik[p0:p0 + HD, 0:nk], start=True, stop=True)\
                      .then_inc(sem["is_ready"], 1)

            def pe_mix(st):
                pe.wait_ge(*before(st, "act"))
                pe.wait_ge(*before(st, "dve"))

                def step(b, i, p):
                    s = st.s0 + 8 * b + p
                    u, ps = s % 2, p % 2
                    if b or p >= 2:
                        pe.wait_ge(sem["up_taken"], st.at["up_taken"] + (i + (8 * b + p - 1)))
                    pe.wait_ge(sem["w_split"], i + (s + 1))
                    for k in range(KT):
                        mm3(PA[:, 2 * ps, 0:TX], u, k * P, u_hi[:, k, 0:TX], u_lo[:, k, 0:TX],
                            k == 0, k == KT - 1)
                    for k in range(4):
                        mm = mm3(PA[:, 2 * ps + 1, 0:TX], u, (KT + k) * P, y_hi[:, 4 * b + k, :],
                                 y_lo[:, 4 * b + k, :], k == 0, k == 3)
                    mm.then_inc(sem["slab_done"], 1)

                for b in range(3):
                    step(b, 0, 0)
                    step(b, 0, 1)
                    with pe.Fori(0, 3) as i:
                        step(b, i * 2, 2)
                        step(b, i * 2, 3)

            def pe_ada(st):
                pe.wait_ge(*before(st, "act"))
                pe.wait_ge(*before(st, "dve"))
                pe.wait_ge(sem["mod_ready"], 1)

                def slabs(i, j0, j1):
                    for j in range(j0, j1):
                        g, e = j // 3, j % 3
                        po = PA[0:96, g // 2, 256 * (g % 2):256 * (g % 2) + 256]
                        pe.wait_ge(sem["ada_split"], i + (j + 1))
                        for k in range(KT):
                            w = slice(k * 256, k * 256 + 256)
                            c = c_split[:, k, 64 - 32 * e:160 - 32 * e]
                            pe.matmul(po, c, ada_hi[j % AH][:, w],
                                      start=(e == 0 and k == 0), stop=False)
                            mm = pe.matmul(po, c, ada_lo[j % AR][:, w], start=False,
                                           stop=(e == 2 and k == KT - 1))
                        mm.then_inc(sem["ada_used"], 1)

                def turn(i):
                    pe.wait_ge(sem["rows_moved"], i * 48 + 48)
                    pe.wait_ge(sem["mod_ready"], i + 1)
                    pe.matmul(PA[:, 3, 0:4 * AB], ada_turn[0:8 * AB, :],
                              cst[0:8 * AB, C_TU:C_TU + 4 * AB], start=True, stop=True)\
                      .then_inc(sem["turned"], 1)

                slabs(0, 0, AB)
                with pe.Fori(0, AN - 1) as i:
                    pe.wait_ge(sem["rows_copied"], i + 1)
                    slabs(i * AB + AB, 0, 8)
                    turn(i)
                    slabs(i * AB + AB, 8, AB)
                turn(AN - 1)

            def pe_diff(st):
                pe.wait_ge(*before(st, "act"))
                pe.wait_ge(*before(st, "dve"))
                n = len(st.units)
                for i in range(n + 3):
                    if i < n:
                        h, t = st.units[i]
                        k0 = 0 if t < 2 else TX
                        if i >= 2:
                            pe.wait_ge(sem["p_ready"], st.at["p_ready"] + i - 1)
                        for j in range(2):
                            p0 = HD * j
                            mm = pe.matmul(PA[:, 2 * (i % 2) + j, 0:TT - k0],
                                           Q[p0:p0 + HD, h, t * P:t * P + P],
                                           K[p0:p0 + HD, h, k0:TT], start=True, stop=True)
                        mm.then_inc(sem["s_ready"], 1)
                    if 2 <= i < n + 2:
                        j = i - 2
                        pe.wait_ge(sem["p_normed"], st.at["p_normed"] + j + 1)
                        if j >= 2:
                            pe.wait_ge(sem["pt_copied"], st.at["pt_copied"] + j - 1)
                        for b in range(4 if st.units[j][1] < 2 else 2):
                            mm = pe.transpose(PB[:, 2 + j % 2, b * P:b * P + P],
                                              p2_sb[:, j % NP, 0, b * P:b * P + P], ident)
                        mm.then_inc(sem["pt_ready"], 1)
                    if i >= 3:
                        j = i - 3
                        h, t = st.units[j]
                        if j >= 2:
                            pe.wait_ge(sem["o_taken"], st.at["o_taken"] + j - 1)
                        pe.wait_ge(sem["pt_copied"], st.at["pt_copied"] + j + 1)
                        nb, b0 = (4, 0) if t < 2 else (2, 2)
                        for b in range(nb):
                            mm = pe.matmul(PB[:, j % 2, 0:P], pt_sb[:, j % 2, b * P:b * P + P],
                                           V[:, b0 + b, h * P:h * P + P],
                                           start=(b == 0), stop=(b == nb - 1))
                        mm.then_inc(sem["o_ready"], 1)
                for h in range(8):
                    pe.wait_ge(sem["o_scaled"], st.at["o_scaled"] + (4 * h + 4))
                    if h >= 4:
                        pe.wait_ge(sem["og_ready"], st.at["og_ready"] + h - 3)
                    for t in range(4):
                        mm = pe.transpose(PA[:, h % 4, t * P:t * P + P], on[:, 4 * h + t, :], ident)
                    mm.then_inc(sem["ot_ready"], 1)

            run = dict(norm=pe_norm, proj=pe_proj, ffn_in=pe_ffn_in, ffn_out=pe_out, proj_y=pe_out,
                       attn=pe_attn, index=pe_index, mix=pe_mix, ada=pe_ada, diff=pe_diff)
            pe.wait_ge(sem["consts_in"], 32)
            for st in plan:
                if st.kind in run:
                    run[st.kind](st)

        @block.scalar
        def _(act):
            def feed(s, i=0):
                if s >= ns:
                    return
                u = s % 2
                half = i if isinstance(i, int) else None
                act.wait_ge(raw_full[u], (feed_pair * 16 if half is None else 0) +
                            16 * (s // 2 + 1))
                if s >= 2:
                    act.wait_ge(sem["slab_done"], i + (s - 1))
                act.activation(wh[u][:, 0:sizes[s]], raw[u][:, 0:sizes[s]], ACT.Copy)\
                   .then_inc(sem["w_hi_ready"], 1)

            feed_pair = 0

            def act_norm(st):
                T = st.T
                act.wait_ge(*before(st, "pe"))
                act.wait_ge(*before(st, "act"))
                act.wait_ge(*before(st, "dve"))
                if st.stat == "own":
                    for k in range(KT):
                        if k >= NSQ:
                            act.wait_ge(sem["stat_used"], st.at["stat_used"] + k - NSQ + 1)
                        act.activation(sq[:, k % NSQ, 0:T], X[:, k, 0:T], ACT.Square)\
                           .then_inc(sem["sq_ready"], 1)
                rows = T // P * 32
                stat = KT if st.stat == "own" else 1 if st.apply == "resid" else 0
                act.wait_ge(sem["stat_used"], st.at["stat_used"] + stat)
                act.activation(rms_root[0:rows, :], stat_bank(st)[0:rows, 0:P], ACT.Sqrt,
                               scale=1.0 / D, bias=eps[0:rows, 1:2])\
                   .then_inc(sem["sqrt_ready"], 1)
                if st.apply == "resid" and st.more:
                    for k in range(KT):
                        act.wait_ge(sem["x_ready"], st.at["x_ready"] + k + 1)
                        if k >= NSQ:
                            act.wait_ge(sem["stat_used"], st.at["stat_used"] + k - NSQ + 2)
                        act.activation(sq[:, k % NSQ, 0:T], X[:, k, 0:T], ACT.Square)\
                           .then_inc(sem["sq_ready"], 1)
                if st.apply == "split":
                    for k in range(KT):
                        act.wait_ge(sem["scaled"], st.at["scaled"] + k + 1)
                        for v in range(T // TX):
                            tok = slice(v * TX, v * TX + TX)
                            if st.mod:
                                ins = act.activation(u_hi[:, k, tok], scaled[:, k % 2, tok],
                                                     ACT.Identity,
                                                     bias=mod[:, st.l, 3 * st.sub, k, v:v + 1])
                            else:
                                ins = act.activation(u_hi[:, k, tok], scaled[:, k % 2, tok],
                                                     ACT.Copy)
                        ins.then_inc(sem["u_hi_ready"], 1)

            def act_proj(st):
                act.wait_ge(*before(st, "pe"))
                act.wait_ge(*before(st, "act"))
                act.wait_ge(*before(st, "dve"))
                if st.late:
                    feed(st.s0 + 1)
                for i, (how, to, tile, t0, T) in enumerate(st.steps):
                    s, ps = st.s0 + i, i % 2
                    feed(s + 2)
                    if how not in ("copy", "silu", "scale", "nat"):
                        continue
                    act.wait_ge(sem["slab_done"], st.at["slab_done"] + i + 1)
                    if how == "nat":
                        nt = T // P
                        src = PA[:, 2 * ps:2 * ps + nt // 2, :]\
                            .rearrange("p b (t c) -> p (b t) c", c=256)
                        dst = dest[to][:, 0:nt, tile * 256:tile * 256 + 256]
                    elif T == TX:
                        src = PA[:, 2 * ps:2 * ps + 2, 0:TX]
                        full = qn if to == "Q" else dest[to]
                        dst = full[:, tile:tile + 2, 0:TX]
                    else:
                        src = PA[:, 2 * ps:2 * ps + 2, :]
                        dst = dest[to][:, tile:tile + 2, 0:TT]
                    if how == "silu":
                        ins = act.activation(dst, src, ACT.Silu)
                    elif how == "scale":
                        ins = act.activation(dst, src, ACT.Copy, scale=HD ** -0.5)
                    else:
                        ins = act.activation(dst, src, ACT.Copy)
                    ins.then_inc(sem["taken_act"], 1)

            def act_ffn_in(st):
                nonlocal feed_pair
                T = st.T
                act.wait_ge(*before(st, "pe"))
                act.wait_ge(*before(st, "act"))
                act.wait_ge(*before(st, "dve"))

                if st.late:
                    feed(st.s0 + 1)

                def step(i, p):
                    ps = p % 2
                    act.wait_ge(sem["slab_done"], st.at["slab_done"] + (i + (p + 1)))
                    act.activation(silu[:, ps, 0:T], PA[:, 2 * ps, 0:T], ACT.Silu)\
                       .then_inc(sem["silu_ready"], 1)
                    feed(st.s0 + p + 2, i)
                    act.wait_ge(sem["h_ready"], st.at["h_ready"] + (i + (p + 1)))
                    act.activation(g_hi[:, p if isinstance(i, int) else bass.ds(i + p, 1), 0:T],
                                   h_f32[:, ps, 0:T], ACT.Copy).then_inc(sem["g_hi_ready"], 1)

                with act.Fori(0, (FH - 3) // 2) as i:
                    feed_pair = i
                    step(i * 2, 0)
                    step(i * 2, 1)
                for p in range(FH - 3, FH):
                    step(0, p)

            def act_ffn_out(st):
                T = st.T
                act.wait_ge(*before(st, "pe"))
                act.wait_ge(*before(st, "act"))
                act.wait_ge(*before(st, "dve"))
                if st.half == 0:
                    for p in range(4):
                        ps = p % 2
                        feed(st.s0 + p + 2)
                        act.wait_ge(sem["slab_done"], st.at["slab_done"] + p + 1)
                        act.activation(Y[:, 2 * p:2 * p + 2, 0:T], PB[:, 2 * ps:2 * ps + 2, 0:T],
                                       ACT.Copy).then_inc(sem["taken_act"], 1)
                    return

                def square(m):
                    act.wait_ge(sem["y_ready"], st.at["y_ready"] + m + 1)
                    if m > NSQ:
                        act.wait_ge(sem["sum_ready"], st.at["sum_ready"] + m - NSQ)
                    to = sqsum[:, 0:T] if m == 0 else sq[:, m % NSQ, 0:T]
                    act.activation(to, Y[:, m, 0:T], ACT.Square).then_inc(sem["sq_ready"], 1)

                for p in range(4):
                    square(2 * p)
                    if p < 3:
                        feed(st.s0 + p + 2)
                    square(2 * p + 1)

            def act_proj_y(st):
                T = st.T
                act.wait_ge(*before(st, "pe"))
                act.wait_ge(*before(st, "act"))
                act.wait_ge(*before(st, "dve"))

                def take(m):
                    bank = PA[:, m % 4, 0:T]
                    act.wait_ge(sem[("tile_done", "slab_done")[m % 2]],
                                st.at[("tile_done", "slab_done")[m % 2]] + m // 2 + 1)
                    if m > NSQ:
                        act.wait_ge(sem["sum_ready"], st.at["sum_ready"] + m - NSQ)
                    to = sqsum[:, 0:T] if m == 0 else sq[:, m % NSQ, 0:T]
                    act.activation(Y[:, m, 0:T], bank, ACT.Copy)
                    act.activation(to, bank, ACT.Square).then_inc(sem["sq_ready"], 1)

                for p in range(4):
                    take(2 * p)
                    if p < 3:
                        feed(st.s0 + p + 2)
                    take(2 * p + 1)

            def act_attn(st):
                w, n = st.which, len(st.units)
                scale = dict(a=HD ** -0.5, b=HD ** -0.5, m=P ** -0.5, n=1.0)[w]
                act.wait_ge(*before(st, "pe"))
                act.wait_ge(*before(st, "act"))
                act.wait_ge(*before(st, "dve"))
                for i in range(n + 2):
                    if i < n:
                        act.wait_ge(sem["negmax_ready"], st.at["negmax_ready"] + i + 1)
                        if i >= NP:
                            act.wait_ge(sem["pt_ready"], st.at["pt_ready"] + i - NP + 1)
                        for e, (_, _, off, nk) in enumerate(st.units[i]):
                            src = PA[:, i % 4, off:off + nk] if w == "m" else \
                                s_sb[:, i % NP, off:off + nk]
                            ins = act.activation(p_sb[:, i % NP, off:off + nk], src, ACT.Exp,
                                                 scale=scale, bias=nm[:, i % NP, e:e + 1],
                                                 accum_out=rs[:, i % NP, e:e + 1])
                        ins.then_inc(sem["p_ready"], 1)
                    if i >= 2:
                        j = i - 2
                        nk = width(st.units[j])
                        act.wait_ge(sem["pt_ready"], st.at["pt_ready"] + j + 1)
                        if j >= 2:
                            act.wait_ge(sem["o_ready"], st.at["o_ready"] + j - 1)
                        act.activation(pt_sb[:, j % 2, 0:nk], PB[:, 2 + j % 2, 0:nk], ACT.Copy)\
                           .then_inc(sem["pt_copied"], 1)
                act.wait_ge(sem["o_taken"], st.at["o_taken"] + st.groups)
                if w == "n":
                    act.activation(u_hi[:, :, 0:TX], qn[:, :, :], ACT.Copy)\
                       .then_inc(sem["y_hi_ready"], 1)
                else:
                    b = 4 * "abm".index(w)
                    act.activation(y_hi[:, b:b + 4, :], q1[:, :, :], ACT.Copy)\
                       .then_inc(sem["y_hi_ready"], 1)

            def act_index(st):
                act.wait_ge(*before(st, "pe"))
                act.wait_ge(*before(st, "act"))
                act.wait_ge(*before(st, "dve"))
                for j in range(16):
                    nk = (j // 8 + 1) * P
                    act.wait_ge(sem["is_ready"], st.at["is_ready"] + j + 1)
                    if j >= 2:
                        act.wait_ge(sem["acc_ready"], st.at["acc_ready"] + j - 1)
                    act.activation(relu[:, j % 2, 0:nk], PA[:, j % 4, 0:nk], ACT.Relu,
                                   scale=HD ** -0.5).then_inc(sem["relu_ready"], 1)

            def act_mix(st):
                nonlocal feed_pair
                act.wait_ge(*before(st, "pe"))
                act.wait_ge(*before(st, "act"))
                act.wait_ge(*before(st, "dve"))

                def step(i, p):
                    ps = p % 2
                    feed(st.s0 + p + 2, i)
                    act.wait_ge(sem["slab_done"], st.at["slab_done"] + (i + (p + 1)))
                    if not isinstance(i, int) or p >= 2:
                        act.wait_ge(sem["up_taken"], st.at["up_taken"] + (i + (p - 1)))
                    act.activation(sig[:, ps, :], PA[:, 2 * ps, 0:TX], ACT.Sigmoid)\
                       .then_inc(sem["gate_ready"], 1)

                step(0, 0)
                step(0, 1)
                with act.Fori(0, 10) as i:
                    feed_pair = i
                    step(i * 2, 2)
                    step(i * 2, 3)
                step(0, 22)
                step(0, 23)
                act.wait_ge(sem["merged"], st.at["merged"] + 24)
                act.activation(u_hi[:, :, 0:TX], merged[:, :, :], ACT.Copy)\
                   .then_inc(sem["m_hi_ready"], 1)

            def act_ada(st):
                act.wait_ge(*before(st, "pe"))
                act.wait_ge(*before(st, "act"))
                act.wait_ge(*before(st, "dve"))
                act.dma_start(X[:, :, TX:TT], ctx_in).then_inc(sem["ctx_in"], 16)
                act.wait_ge(sem["c_zero"], 1)
                act.activation(c_f32[:, :, 64:66], vec[:, V_C:V_C + 2 * KT]
                               .rearrange("p (k v) -> p k v", v=2), ACT.Silu)\
                   .then_inc(sem["c_ready"], 1)
                act.wait_ge(sem["c_ready"], st.at["c_ready"] + 1)
                act.activation(c_split[:, :, :], c_f32[:, :, :], ACT.Copy)\
                   .then_inc(sem["c_hi_ready"], 1)

                def slabs(b, j0, j1, first):
                    for j in range(j0, j1):
                        act.wait_ge(sem[f"ada_full{j % AR}"], b * 32 + 16 * (j // AR + 1))
                        if not first or j >= AH:
                            act.wait_ge(sem["ada_used"], b * AB + (j + 1 - AH))
                        act.activation(ada_hi[j % AH][:, :], ada_raw[j % AR][:, :], ACT.Copy)\
                           .then_inc(sem["ada_hi_ready"], 1)

                def rows(b):
                    act.wait_ge(sem["ada_used"], b * AB + AB)
                    act.wait_ge(sem["mod_ready"], b + 1)
                    act.activation(ada_rows[0:96, :], PA[0:96, 0:2, :]
                                   .rearrange("p b c -> p (b c)"), ACT.Copy)\
                       .then_inc(sem["rows_copied"], 1)
                    act.wait_ge(sem["rows_copied"], b + 1)
                    for e in range(3):
                        act.dma_start(ada_turn[32 * e:32 * e + 32, :],
                                      ada_rows[32 * e:32 * e + 4, :])\
                           .then_inc(sem["rows_moved"], 16)

                slabs(0, 0, AB, True)
                with act.Fori(0, AN - 1) as i:
                    slabs(i + 1, 0, 2, False)
                    rows(i)
                    slabs(i + 1, 2, AB, False)
                rows(AN - 1)
                act.wait_ge(sem["ctx_in"], 16)

            def act_diff(st):
                n = len(st.units)
                act.wait_ge(*before(st, "pe"))
                act.wait_ge(*before(st, "act"))
                act.wait_ge(*before(st, "dve"))
                for i in range(n + 4):
                    if i < n:
                        nk, sl = TT if st.units[i][1] < 2 else TX, i % NP
                        act.wait_ge(sem["negmax_ready"], st.at["negmax_ready"] + i + 1)
                        if i >= NP:
                            act.wait_ge(sem["pt_ready"], st.at["pt_ready"] + i - NP + 1)
                        for j in range(2):
                            ins = act.activation(p2_sb[:, sl, j, 0:nk],
                                                 PA[:, 2 * (i % 2) + j, 0:nk], ACT.Exp,
                                                 scale=HD ** -0.5, bias=nm[:, sl, j:j + 1],
                                                 accum_out=rs[:, sl, j:j + 1])
                        ins.then_inc(sem["p_ready"], 1)
                    if 2 <= i < n + 2:
                        j = i - 2
                        nk = TT if st.units[j][1] < 2 else TX
                        act.wait_ge(sem["pt_ready"], st.at["pt_ready"] + j + 1)
                        if j >= 2:
                            act.wait_ge(sem["o_ready"], st.at["o_ready"] + j - 1)
                        act.activation(pt_sb[:, j % 2, 0:nk], PB[:, 2 + j % 2, 0:nk], ACT.Copy)\
                           .then_inc(sem["pt_copied"], 1)
                    if i >= 4:
                        j = i - 4
                        act.wait_ge(sem["o_taken"], st.at["o_taken"] + j + 1)
                        if j >= 1:
                            act.wait_ge(sem["o_sq_ready"], st.at["o_sq_ready"] + j)
                        act.activation(osq[:, :], on[:, j, :], ACT.Square,
                                       accum_out=ssq[:, j:j + 1]).then_inc(sem["o_sq_ready"], 1)
                act.wait_ge(sem["o_sq_ready"], st.at["o_sq_ready"] + n)
                act.activation(sroot[:, :], ssq[:, :], ACT.Sqrt, scale=1.0 / P, bias=eps[:, 0:1])\
                   .then_inc(sem["o_sqrt_ready"], 1)
                for h in range(8):
                    act.wait_ge(sem["og_ready"], st.at["og_ready"] + h + 1)
                    act.activation(u_hi[:, h, :], og[:, h % 2, :], ACT.Copy)\
                       .then_inc(sem["y_hi_ready"], 1)

            st = plan[0]
            act.dma_start(cst[:, :], cst_in).then_inc(sem["consts_in"], 16)
            act.dma_start(vec[:, :], vec_in).then_inc(sem["consts_in"], 16)
            feed(0)
            feed(1)
            act.wait_ge(sem["setup_dve"], st.at["setup_dve"] + 2)
            act.activation(lam[:, 2:3], lam[:, 0:1], ACT.Exp).then_inc(sem["setup_act"], 1)
            act.activation(lam[:, 3:4], lam[:, 1:2], ACT.Exp).then_inc(sem["setup_act"], 1)
            act.wait_ge(sem["consts_in"], 32)
            act.wait_ge(sem["x_in"], 16)
            act.wait_ge(sem["mem_in"], 16)
            run = dict(norm=act_norm, proj=act_proj, ffn_in=act_ffn_in, ffn_out=act_ffn_out, proj_y=act_proj_y,
                       attn=act_attn, index=act_index, mix=act_mix, ada=act_ada, diff=act_diff)
            for st in plan[1:]:
                run[st.kind](st)

        @block.vector
        def _(dve):
            chain = Chain()

            def feed(s, i=0):
                if s >= ns:
                    return
                u, n = s % 2, sizes[s]
                dve.wait_ge(sem["w_hi_ready"], i + (s + 1))
                dve.tensor_tensor(wl[u][:, 0:n], raw[u][:, 0:n], wh[u][:, 0:n].bitcast(F32),
                                  ALU.subtract).then_inc(sem["w_split"], 1)

            def dve_norm(st):
                src = Y if st.apply == "resid" else X
                T, l, sub = st.T, st.l, st.sub
                nv, rows = T // TX, T // P * 32
                dve.wait_ge(*before(st, "pe"))
                dve.wait_ge(*before(st, "act"))
                dve.wait_ge(*before(st, "dve"))
                dve.wait_ge(sem["sqrt_ready"], st.at["sqrt_ready"] + 1)
                dve.reciprocal(rms[0:rows, :], rms_root[0:rows, :]).then_inc(sem["rms_ready"], 1)
                dve.wait_ge(sem["r_ready"], st.at["r_ready"] + 1)

                def gain(k, v):
                    if st.apply == "resid":
                        return gg[:, l, sub, k, v:v + 1]
                    if st.apply == "plain":
                        return vec[:, V_FG + k:V_FG + k + 1]
                    if st.mod:
                        return gs[:, l, sub, k, v:v + 1]
                    c = (V_NG, V_MG)[v] + l * KT + k
                    return vec[:, c:c + 1]

                def scale(k):
                    if k >= 2:
                        dve.wait_ge(sem["u_lo_ready" if st.apply == "split" else "x_ready"], st.at["u_lo_ready" if st.apply == "split" else "x_ready"] + k - 1)
                    for v in range(nv):
                        tok = slice(v * TX, v * TX + TX)
                        ins = dve.scalar_tensor_tensor(out=scaled[:, k % 2, tok],
                                                       in0=src[:, k, tok], scalar=gain(k, v),
                                                       in1=stat_bank(st)[:, tok], op0=ALU.mult,
                                                       op1=ALU.mult)
                    ins.then_inc(sem["scaled"], 1)

                def finish(k):
                    dve.wait_ge(sem["scaled"], st.at["scaled"] + k + 1)
                    if st.apply == "resid":
                        ins = dve.tensor_tensor(X[:, k, 0:T], X[:, k, 0:T], scaled[:, k % 2, 0:T],
                                                ALU.add)
                    elif st.apply == "plain":
                        ins = dve.tensor_copy(X[:, k, 0:T], scaled[:, k % 2, 0:T])
                    else:
                        dve.wait_ge(sem["u_hi_ready"], st.at["u_hi_ready"] + k + 1)
                        if not st.mod:
                            ins = dve.tensor_tensor(u_lo[:, k, 0:T], scaled[:, k % 2, 0:T],
                                                    u_hi[:, k, 0:T].bitcast(F32), ALU.subtract)
                        else:
                            for v in range(nv):
                                tok = slice(v * TX, v * TX + TX)
                                ins = dve.scalar_tensor_tensor(
                                    out=u_lo[:, k, tok], in0=scaled[:, k % 2, tok],
                                    scalar=mod[:, l, 3 * sub, k, v:v + 1],
                                    in1=u_hi[:, k, tok].bitcast(F32), op0=ALU.add,
                                    op1=ALU.subtract)
                        ins.then_inc(sem["u_lo_ready"], 1)
                        return
                    ins.then_inc(sem["x_ready"], 1)

                scale(0)
                for k in range(1, KT):
                    scale(k)
                    finish(k - 1)
                finish(KT - 1)

            def rope(src, dst, sh, table, mask, shape, taken):
                cos = cst[:, table:table + TX]
                sin = cst[:, table + TX:table + 2 * TX]
                if len(shape) == 3:
                    cos, sin = cos[:, None, :].broadcast_to(shape), sin[:, None, :].broadcast_to(shape)
                dve.stream_shuffle(sh, src, mask).then_inc(sem["chain"], chain.up())
                dve.tensor_tensor(dst, src, cos, ALU.mult).then_inc(taken, 1)
                dve.wait_ge(sem["chain"], chain.n)
                dve.tensor_tensor(sh, sh, sin, ALU.mult).then_inc(sem["chain"], chain.up())
                dve.wait_ge(sem["chain"], chain.n)
                return dve.tensor_tensor(dst, dst, sh, ALU.add)

            def dve_proj(st):
                dve.wait_ge(*before(st, "pe"))
                dve.wait_ge(*before(st, "act"))
                dve.wait_ge(*before(st, "dve"))
                if st.late:
                    feed(st.s0 + 1)
                mask1 = [(p + 8) % 16 if p < 16 else p for p in range(32)]
                mask2 = [(p + 16) % 32 for p in range(32)]
                done = 0
                for i, (how, to, tile, t0, T) in enumerate(st.steps):
                    s, ps = st.s0 + i, i % 2
                    feed(s + 2)
                    if how in ("copy", "silu", "scale", "nat"):
                        continue
                    dve.wait_ge(sem["slab_done"], st.at["slab_done"] + i + 1)
                    if done:
                        dve.wait_ge(sem["out_dve"], st.at["out_dve"] + done)
                    two = PA[:, 2 * ps:2 * ps + 2, 0:TX]
                    if how == "rope1":
                        ins = rope(two, dest[to][:, tile:tile + 2, :], shuf[:, :, :], C_R1, mask1,
                                   (P, 2, TX), sem["taken_dve"])
                    elif how == "rope2":
                        dve.tensor_copy(dest[to][:, tile:tile + 2, TX:TT],
                                                  PA[:, 2 * ps:2 * ps + 2, TX:TT]).then_inc(sem["chain"], chain.up())
                        ins = rope(PA[:, 2 * ps:2 * ps + 2, 0:TX], dest[to][:, tile:tile + 2, 0:TX],
                                   shuf[:, :, :], C_R2, mask2, (P, 2, TX), sem["taken_dve"])
                    elif how == "index":
                        dve.tensor_scalar(
                            wi[:, :, :], PA[:, 2 * ps, TX:TX + 2 * NH1]
                            .rearrange("p (t h) -> p t h", h=NH1), NH1 ** -0.5, None, ALU.mult).then_inc(sem["chain"], chain.up())
                        ins = rope(PA[:, 2 * ps, 0:TX], ik[:, :], shuf[:, 0, :], C_R1, mask1,
                                   (P, TX), sem["taken_dve"])
                    else:
                        x = X[:, tile:tile + 2, 0:TX]
                        dve.tensor_tensor(x, x, two, ALU.add).then_inc(sem["taken_dve"], 1)
                        continue
                    ins.then_inc(sem["out_dve"], 1)
                    done += 1

            def dve_ffn_in(st):
                T = st.T
                dve.wait_ge(*before(st, "pe"))
                dve.wait_ge(*before(st, "act"))
                dve.wait_ge(*before(st, "dve"))

                if st.late:
                    feed(st.s0 + 1)

                def step(i, p):
                    ps = p % 2
                    dve.wait_ge(sem["silu_ready"], st.at["silu_ready"] + (i + (p + 1)))
                    dve.tensor_tensor(h_f32[:, ps, 0:T], silu[:, ps, 0:T], PA[:, 2 * ps + 1, 0:T],
                                      ALU.mult).then_inc(sem["h_ready"], 1)
                    feed(st.s0 + p + 2, i)
                    dve.wait_ge(sem["g_hi_ready"], st.at["g_hi_ready"] + (i + (p + 1)))
                    at = p if isinstance(i, int) else bass.ds(i + p, 1)
                    dve.tensor_tensor(g_lo[:, at, 0:T], h_f32[:, ps, 0:T],
                                      g_hi[:, at, 0:T].bitcast(F32), ALU.subtract)\
                       .then_inc(sem["g_lo_ready"], 1)

                with dve.Fori(0, (FH - 3) // 2) as i:
                    step(i * 2, 0)
                    step(i * 2, 1)
                for p in range(FH - 3, FH):
                    step(0, p)

            def add_up(st, m):
                T = st.T
                dve.wait_ge(sem["sq_ready"], st.at["sq_ready"] + m + 1)
                dve.wait_ge(sem["sum_ready"], st.at["sum_ready"] + m - 1)
                dve.tensor_tensor(sqsum[:, 0:T], sqsum[:, 0:T], sq[:, m % NSQ, 0:T], ALU.add)\
                   .then_inc(sem["sum_ready"], 1)

            def dve_ffn_out(st):
                T = st.T
                dve.wait_ge(*before(st, "pe"))
                dve.wait_ge(*before(st, "act"))
                dve.wait_ge(*before(st, "dve"))
                if st.half == 0:
                    for p in range(4):
                        feed(st.s0 + p + 2)
                    return

                def add(m):
                    dve.wait_ge(sem[("tile_done", "slab_done")[m % 2]],
                                st.at[("tile_done", "slab_done")[m % 2]] + m // 2 + 1)
                    dve.tensor_tensor(Y[:, m, 0:T], Y[:, m, 0:T], PB[:, m % 4, 0:T], ALU.add)\
                       .then_inc(sem["y_ready"], 1)
                    if m >= 2:
                        add_up(st, m - 1)

                for p in range(4):
                    add(2 * p)
                    add(2 * p + 1)
                    if p < 3:
                        feed(st.s0 + p + 2)

            def dve_proj_y(st):
                dve.wait_ge(*before(st, "pe"))
                dve.wait_ge(*before(st, "act"))
                dve.wait_ge(*before(st, "dve"))
                for p in range(4):
                    if p < 3:
                        feed(st.s0 + p + 2)
                    for m in (2 * p, 2 * p + 1):
                        if m >= 2:
                            add_up(st, m - 1)

            def dve_attn(st):
                w, n = st.which, len(st.units)
                per = n // st.groups
                dve.wait_ge(*before(st, "pe"))
                dve.wait_ge(*before(st, "act"))
                dve.wait_ge(*before(st, "dve"))
                scale = dict(a=HD ** -0.5, b=HD ** -0.5, m=P ** -0.5, n=1.0)[w]

                def soft(i):
                    unit, sl, bank = st.units[i], i % NP, i % 4
                    dve.wait_ge(sem["s_ready"], st.at["s_ready"] + i + 1)
                    if i >= NP:
                        dve.wait_ge(sem["p_ready"], st.at["p_ready"] + i - NP + 1)
                    if w == "m":
                        dve.tensor_reduce(mx[:, sl, :], PA[:, bank, :]
                                          .rearrange("p (q k) -> p q k", k=TX), AX.X, ALU.max)\
                           .then_inc(sem["chain"], chain.up())
                    if w == "n":
                        dve.wait_ge(sem["bias_ready"], i + 1)
                        dve.wait_ge(sem["no_bias"], 1)
                    for e, (h, qt, off, nk) in enumerate(unit if w != "m" else ()):
                        extra = na_bias[:, i % 2, :] if w == "n" else \
                            sel_bias[:, qt, 0:nk] if w == "b" else \
                            cst[:, C_CM + TX - nk:C_CM + TX]
                        ins = dve.tensor_tensor_reduce(
                            s_sb[:, sl, off:off + nk], PA[:, bank, off:off + nk], extra,
                            1.0, 4 * NEG, ALU.add, ALU.max, mx[:, sl, e:e + 1])
                    if w != "m":
                        ins.then_inc(sem["chain"], chain.up())
                    dve.wait_ge(sem["chain"], chain.n)
                    ne = len(unit)
                    dve.tensor_scalar(nm[:, sl, 0:ne], mx[:, sl, 0:ne], -scale, None, ALU.mult)\
                       .then_inc(sem["negmax_ready"], 1)

                def normalise(j):
                    sl, ne = j % NP, len(st.units[j])
                    dve.wait_ge(sem["p_ready"], st.at["p_ready"] + j + 1)
                    dve.reciprocal(ri[:, sl, 0:ne], rs[:, sl, 0:ne])\
                       .then_inc(sem["chain"], chain.up())
                    dve.wait_ge(sem["chain"], chain.n)
                    for e, (_, _, off, nk) in enumerate(st.units[j]):
                        p_ = p_sb[:, sl, off:off + nk]
                        ins = dve.tensor_scalar(p_, p_, ri[:, sl, e:e + 1], None, ALU.mult)
                    ins.then_inc(sem["p_normed"], 1)

                def take(g):
                    dve.wait_ge(sem["o_ready"], st.at["o_ready"] + (per * (g + 1)))
                    o = PB[:, g % 2, 0:TX]
                    if w == "n":
                        ins = dve.tensor_copy(qn[:, g, :], o)
                    else:
                        ins = dve.tensor_tensor(q1[:, g, :], g1[:, g, :], o, ALU.mult)
                    ins.then_inc(sem["o_taken"], 1)

                for i in range(n + 4):
                    if i < n:
                        soft(i)
                    if 1 <= i <= n:
                        normalise(i - 1)
                    if i >= 4 and (i - 4) % per == per - 1:
                        take((i - 4) // per)
                dve.wait_ge(sem["y_hi_ready"], st.at["y_hi_ready"] + 1)
                if w == "n":
                    hi, lo, src = u_hi[:, :, 0:TX], u_lo[:, :, 0:TX], qn[:, :, :]
                else:
                    b = 4 * "abm".index(w)
                    hi, lo, src = y_hi[:, b:b + 4, :], y_lo[:, b:b + 4, :], q1[:, :, :]
                dve.tensor_tensor(lo, src, hi.bitcast(F32), ALU.subtract)\
                   .then_inc(sem["y_lo_ready"], 1)

            def dve_index(st):
                dve.wait_ge(*before(st, "pe"))
                dve.wait_ge(*before(st, "act"))
                dve.wait_ge(*before(st, "dve"))
                for j in range(16):
                    qt, h = j // 8, j % 8
                    nk = (qt + 1) * P
                    acc, r, wgt = idx_acc[:, qt, 0:nk], relu[:, j % 2, 0:nk], wi[:, qt, h:h + 1]
                    dve.wait_ge(sem["relu_ready"], st.at["relu_ready"] + j + 1)
                    if h == 0:
                        ins = dve.tensor_scalar(acc, r, wgt, 0.0, ALU.mult, ALU.add)
                    else:
                        dve.wait_ge(sem["acc_ready"], st.at["acc_ready"] + j)
                        ins = dve.scalar_tensor_tensor(out=acc, in0=r, scalar=wgt, in1=acc,
                                                       op0=ALU.mult, op1=ALU.add)
                    ins.then_inc(sem["acc_ready"], 1)
                for qt in range(2):
                    nk = (qt + 1) * P
                    acc = idx_acc[:, qt, 0:nk]
                    causal = cst[:, C_CM + (P if qt == 0 else 0):C_CM + 2 * P]
                    dve.wait_ge(sem["acc_ready"], st.at["acc_ready"] + (8 * (qt + 1)))
                    dve.tensor_tensor(acc, acc, causal, ALU.add).then_inc(sem["chain"], chain.up())
                    for _ in range(TOPK // 8):
                        dve.wait_ge(sem["chain"], chain.n)
                        dve.max(top8[:, :], acc).then_inc(sem["chain"], chain.up())
                        dve.wait_ge(sem["chain"], chain.n)
                        dve.match_replace(acc, top8[:, :], acc, TAKEN).then_inc(sem["chain"], chain.up())
                    dve.wait_ge(sem["chain"], chain.n)
                    sel = sel_bias[:, qt, 0:nk]
                    dve.tensor_scalar(sel, acc, TAKEN, NEG, ALU.is_gt, ALU.mult).then_inc(sem["chain"], chain.up())
                    dve.wait_ge(sem["chain"], chain.n)
                    dve.tensor_tensor(sel, sel, causal, ALU.add).then_inc(sem["topk_ready"], 1)

            def dve_mix(st):
                dve.wait_ge(*before(st, "pe"))
                dve.wait_ge(*before(st, "act"))
                dve.wait_ge(*before(st, "dve"))

                def step(b, i, p):
                    ps, n = p % 2, 8 * b + p
                    feed(st.s0 + n + 2, i)
                    dve.wait_ge(sem["gate_ready"], st.at["gate_ready"] + (i + (n + 1)))
                    at = p if isinstance(i, int) else bass.ds(i + p, 1)
                    if b == 0:
                        dve.tensor_tensor(upg[:, ps, :], sig[:, ps, :], PA[:, 2 * ps + 1, 0:TX],
                                          ALU.mult).then_inc(sem["up_taken"], 1)
                        dve.wait_ge(sem["up_taken"], st.at["up_taken"] + (i + (n + 1)))
                        dve.tensor_copy(merged[:, at, :], upg[:, ps, :]).then_inc(sem["merged"], 1)
                    else:
                        dve.tensor_tensor(upg[:, ps, :], sig[:, ps, :], PA[:, 2 * ps + 1, 0:TX],
                                          ALU.mult).then_inc(sem["up_taken"], 1)
                        dve.wait_ge(sem["up_taken"], st.at["up_taken"] + (i + (n + 1)))
                        dve.tensor_tensor(merged[:, at, :], merged[:, at, :], upg[:, ps, :],
                                          ALU.add).then_inc(sem["merged"], 1)

                for b in range(3):
                    with dve.Fori(0, 3) as i:
                        step(b, i * 2, 0)
                        step(b, i * 2, 1)
                    step(b, 0, 6)
                    step(b, 0, 7)
                dve.wait_ge(sem["m_hi_ready"], st.at["m_hi_ready"] + 1)
                dve.tensor_tensor(u_lo[:, :, 0:TX], merged[:, :, :], u_hi[:, :, 0:TX].bitcast(F32),
                                  ALU.subtract).then_inc(sem["m_lo_ready"], 1)

            def dve_ada(st):
                dve.wait_ge(*before(st, "pe"))
                dve.wait_ge(*before(st, "act"))
                dve.wait_ge(*before(st, "dve"))
                dve.memset(c_f32[:, :, :], 0.0).then_inc(sem["c_zero"], 1)
                dve.wait_ge(sem["c_hi_ready"], st.at["c_hi_ready"] + 1)
                dve.tensor_tensor(c_split[:, :, 66:68], c_f32[:, :, 64:66],
                                  c_split[:, :, 64:66].bitcast(F32), ALU.subtract)\
                   .then_inc(sem["mod_ready"], 1)
                flat = mod[:, :, :, :, :].rearrange("p l m k v -> p (l m k v)")

                def slabs(b, j0, j1):
                    for j in range(j0, j1):
                        dve.wait_ge(sem["ada_hi_ready"], b * AB + (j + 1))
                        dve.tensor_tensor(ada_lo[j % AR][:, :], ada_raw[j % AR][:, :],
                                          ada_hi[j % AH][:, :].bitcast(F32), ALU.subtract)\
                           .then_inc(sem["ada_split"], 1)

                def biased(b):
                    dve.wait_ge(sem["turned"], b + 1)
                    at = bass.ds(b * 4 * AB, 4 * AB)
                    dve.tensor_tensor(flat[:, at], PA[:, 3, 0:4 * AB],
                                      vec[:, bass.ds(b * 4 * AB + V_AB, 4 * AB)], ALU.add)\
                       .then_inc(sem["mod_ready"], 1)

                slabs(0, 0, AB)
                with dve.Fori(0, AN - 1) as i:
                    slabs(i + 1, 0, 10)
                    biased(i)
                    slabs(i + 1, 10, AB)
                biased(AN - 1)
                dve.wait_ge(sem["mod_ready"], AN + 1)
                m = mod[:, :, :, :, :].rearrange("p l (s m) k v -> p (l s) m (k v)", m=3)
                g = vec[:, V_G2:V_G2 + 12 * KT * 2 * DEPTH // 2]\
                    .rearrange("p (s e n) -> p s e n", e=2, n=2 * KT)
                flat_gs = gs[:, :, :, :, :].rearrange("p l s k v -> p (l s) (k v)")
                flat_gg = gg[:, :, :, :, :].rearrange("p l s k v -> p (l s) (k v)")
                dve.scalar_tensor_tensor(out=flat_gs, in0=m[:, :, 1, :], scalar=1.0,
                                         in1=g[:, :, 0, :], op0=ALU.add, op1=ALU.mult)\
                   .then_inc(sem["mod_ready"], 1)
                dve.scalar_tensor_tensor(out=flat_gg, in0=m[:, :, 2, :], scalar=0.5,
                                         in1=g[:, :, 1, :], op0=ALU.mult, op1=ALU.mult)\
                   .then_inc(sem["mod_ready"], 1)
                dve.wait_ge(sem["mod_ready"], AN + 3)
                dve.tensor_scalar(gg[:, :, 1, :, :], gg[:, :, 1, :, :], 2.0, None, ALU.mult)\
                   .then_inc(sem["mod_ready"], 1)
                dve.wait_ge(sem["ctx_in"], 16)

            def dve_diff(st):
                n = len(st.units)
                dve.wait_ge(*before(st, "pe"))
                dve.wait_ge(*before(st, "act"))
                dve.wait_ge(*before(st, "dve"))

                def soft(i):
                    nk, sl = (TT if st.units[i][1] < 2 else TX), i % NP
                    dve.wait_ge(sem["s_ready"], st.at["s_ready"] + i + 1)
                    if i >= NP:
                        dve.wait_ge(sem["p_ready"], st.at["p_ready"] + i - NP + 1)
                    b = 2 * (i % 2)
                    dve.tensor_reduce(mx[:, sl, :], PA[:, b:b + 2, 0:nk], AX.X, ALU.max)\
                       .then_inc(sem["chain"], chain.up())
                    dve.wait_ge(sem["chain"], chain.n)
                    dve.tensor_scalar(nm[:, sl, :], mx[:, sl, :], -HD ** -0.5, None, ALU.mult)\
                       .then_inc(sem["negmax_ready"], 1)

                def combine(j):
                    nk, sl = (TT if st.units[j][1] < 2 else TX), j % NP
                    p_1, p_2 = p2_sb[:, sl, 0, 0:nk], p2_sb[:, sl, 1, 0:nk]
                    dve.wait_ge(sem["p_ready"], st.at["p_ready"] + j + 1)
                    if j >= 4:
                        dve.wait_ge(sem["o_taken"], st.at["o_taken"] + j - 3)
                    dve.reciprocal(r2[:, sl:sl + 1], rs[:, sl, 1:2])\
                       .then_inc(sem["chain"], chain.up())
                    dve.reciprocal(ri[:, j % 4, 0:1], rs[:, sl, 0:1])\
                       .then_inc(sem["chain"], chain.up())
                    dve.wait_ge(sem["chain"], chain.n)
                    dve.scalar_tensor_tensor(out=rw[:, sl:sl + 1], in0=r2[:, sl:sl + 1],
                                             scalar=lam[:, 5:6], in1=rs[:, sl, 0:1],
                                             op0=ALU.mult, op1=ALU.mult)\
                       .then_inc(sem["chain"], chain.up())
                    dve.wait_ge(sem["chain"], chain.n)
                    dve.scalar_tensor_tensor(out=p_1, in0=p_2, scalar=rw[:, sl:sl + 1], in1=p_1,
                                             op0=ALU.mult, op1=ALU.add)\
                       .then_inc(sem["p_normed"], 1)

                for i in range(n + 4):
                    if i < n:
                        soft(i)
                    if 1 <= i <= n:
                        combine(i - 1)
                    if i >= 4:
                        j = i - 4
                        dve.wait_ge(sem["o_ready"], st.at["o_ready"] + j + 1)
                        dve.tensor_scalar(on[:, j, :], PB[:, j % 2, 0:P], ri[:, j % 4, 0:1], None,
                                          ALU.mult).then_inc(sem["o_taken"], 1)
                dve.wait_ge(sem["o_sqrt_ready"], st.at["o_sqrt_ready"] + 1)
                dve.reciprocal(srec[:, :], sroot[:, :]).then_inc(sem["chain"], chain.up())
                dve.wait_ge(sem["chain"], chain.n)
                for j in range(n):
                    dve.tensor_scalar(on[:, j, :], on[:, j, :], srec[:, j:j + 1], None, ALU.mult)\
                       .then_inc(sem["o_scaled"], 1)
                for h in range(8):
                    dve.wait_ge(sem["ot_ready"], st.at["ot_ready"] + h + 1)
                    dve.tensor_scalar(og[:, h % 2, :], PA[:, h % 4, :], sub_g[:, 0:1], None,
                                      ALU.mult).then_inc(sem["og_ready"], 1)
                    dve.wait_ge(sem["y_hi_ready"], st.at["y_hi_ready"] + h + 1)
                    dve.tensor_tensor(u_lo[:, h, :], og[:, h % 2, :], u_hi[:, h, :].bitcast(F32),
                                      ALU.subtract).then_inc(sem["y_lo_ready"], 1)

            st = plan[0]
            dve.memset(ones[:, :], 1.0 / D).then_inc(sem["ones_ready"], 1)
            dve.memset(eps[:, 0:1], EPS).then_inc(sem["ones_ready"], 1)
            dve.memset(eps[:, 1:2], EPS / D).then_inc(sem["ones_ready"], 1)
            dve.memset(spread[:, :, :], 0.0).then_inc(sem["ones_ready"], 1)
            dve.wait_ge(sem["ones_ready"], 4)
            for t in range(4):
                dve.memset(spread[32 * t:32 * t + 32, t, :], 1.0 / D)\
                   .then_inc(sem["ones_ready"], 1)
            dve.wait_ge(sem["consts_in"], 32)
            for e in range(2):
                a = V_LM + 2 * e * HD
                dve.tensor_tensor_reduce(lam_tmp[:, e, :], vec[:, a:a + HD],
                                         vec[:, a + HD:a + 2 * HD], 1.0, 0.0, ALU.mult, ALU.add,
                                         lam[:, e:e + 1]).then_inc(sem["setup_dve"], 1)
            feed(0)
            feed(1)
            dve.wait_ge(sem["setup_act"], st.at["setup_act"] + 2)
            dve.tensor_tensor(lam[:, 4:5], lam[:, 3:4], lam[:, 2:3], ALU.subtract)\
               .then_inc(sem["setup_dve"], 1)
            dve.tensor_scalar(sub_g[:, :], vec[:, V_SG:V_SG + 1], 1.0 - LAM_INIT, None, ALU.mult)
            dve.wait_ge(sem["setup_dve"], st.at["setup_dve"] + 3)
            dve.tensor_scalar(lam[:, 5:6], lam[:, 4:5], -LAM_INIT, None, ALU.add)\
               .then_inc(sem["setup_dve"], 1)
            dve.wait_ge(sem["x_in"], 16)
            dve.wait_ge(sem["mem_in"], 16)
            run = dict(norm=dve_norm, proj=dve_proj, ffn_in=dve_ffn_in, ffn_out=dve_ffn_out, proj_y=dve_proj_y,
                       attn=dve_attn, index=dve_index, mix=dve_mix, ada=dve_ada, diff=dve_diff)
            for st in plan[1:]:
                run[st.kind](st)

        @block.gpsimd
        def _(pool):
            st = [s for s in plan if s.kind == "attn" and s.which == "n"][0]
            pool.wait_ge(*before(st, "pe"))
            pool.wait_ge(*before(st, "act"))
            pool.wait_ge(*before(st, "dve"))
            pool.memset(na_bias[:, :, TX:TT], 0.0).then_inc(sem["no_bias"], 1)
            for i, [(h, qt, _, _)] in enumerate(st.units):
                if i >= 2:
                    pool.wait_ge(sem["negmax_ready"], st.at["negmax_ready"] + i - 1)
                pool.dma_start(na_bias[:, i % 2, 0:TX], bias_in[:, h, qt, :])\
                    .then_inc(sem[f"bias_in{i % 2}"], 16)
                pool.wait_ge(sem[f"bias_in{i % 2}"], 16 * (i // 2 + 1))
                rows = na_bias[:, i % 2, 0:TX].rearrange("p (r c) -> p r c", c=HD)
                window = cst[:, C_WM:C_WM + HD][:, None, :].broadcast_to((P, 4, HD))
                pool.tensor_tensor(rows, rows, window, ALU.add).then_inc(sem["bias_ready"], 1)


def pack(w, nk=KT):
    n = w.shape[1] // 256
    return w.reshape(nk, P, n, 256).transpose(2, 1, 0, 3).reshape(n, P, nk * 256)


def pack_ffn_in(w):
    n = D_FF // P
    return w.reshape(KT, P, 2, n, P).transpose(3, 1, 0, 2, 4).reshape(n, P, SLAB)


def pack_mix(w_mix, w_up):
    a = w_mix.reshape(KT, P, KT, P).transpose(2, 1, 0, 3)
    b = w_up.reshape(4, P, KT, P).transpose(2, 1, 0, 3)
    return np.concatenate([a, b], axis=2).reshape(KT, P, SLAB_MIX)


def lay_out(a):
    s16, s22, s12 = [], [], []
    for l in range(DEPTH):
        w = a["w_in"][l]
        col = lambda i, n=1: w[:, i * BW:(i + n) * BW]
        s16 += [pack(col(0)), pack(col(1)), pack(col(2)), pack(col(3)), pack(col(8))]
        small = np.zeros((D, 256), np.float32)
        o = 9 * BW
        small[:, 0:HD] = w[:, o:o + HD]
        small[:, HD:P] = w[:, o:o + HD]
        small[:, P:P + NH1] = w[:, o + HD:o + HD + NH1]
        s16.append(pack(small))
        s16 += [pack(col(4)), pack(col(5)), pack(col(6)), pack(col(7))]
        o += HD + NH1
        s16 += [pack(a["w_mem_kv"][l]), pack(w[:, o:o + 2 * BW])]
        o += 2 * BW
        for b in range(3):
            s12.append(pack_mix(w[:, o + b * D:o + (b + 1) * D], a["w_branch"][l, b]))
        s16.append(pack(a["w_out"][l]))
    for l in range(DEPTH):
        for f in range(2):
            s16.append(pack_ffn_in(a["ffn_w_in_2"][l, f]))
            w = a["ffn_w_out_2"][l, f]
            s22 += [pack(w[0:FH * P], FH), pack(w[FH * P:], FH)]
            if f == 0:
                m = ("da", "na")[l]
                s16 += [pack(a[f"{m}_w_in_2"][0]), pack(a[f"{m}_w_out_2"][0])]
    cols = lambda v: v.reshape(-1, P).T
    two = lambda v: np.repeat(cols(v), 2, axis=1)
    vec = np.concatenate([
        cols(a["norm_g"]), cols(a["mem_norm_g"]), cols(a["final_g"]), two(a["norm_g_2"]),
        two(a["ada_b_2"]), cols(a["da_subln_g_2"]),
        np.stack([cols(a["c_2"]), cols(a["c_ctx_2"])], axis=2).reshape(P, 2 * KT),
        np.broadcast_to(a["da_lambda_2"].reshape(1, -1), (P, 4 * HD))], axis=1)
    rpb = np.zeros((16, 15, 127), np.float32)
    rpb[:, :, 48:79] = a["na_rpb_2"][0]
    bias = np.empty((P, 16, 2, 4, HD), np.float32)
    for p in range(P):
        for i in range(2):
            r, c = 2 * i + p // HD, p % HD
            bias[p, :, i] = rpb[:, 7 - r:11 - r, 63 - c:127 - c]
    tr = lambda t: t.reshape(TX, KT, P).transpose(2, 1, 0)
    return dict(x=tr(a["x"]), mem=tr(a["mem"]), ctx=tr(a["ctx_2"]), vec=vec, cst=constants(),
                bias=bias.reshape(P, 16, 2, TX), w16=np.concatenate(s16), w22=np.concatenate(s22),
                w12=np.concatenate(s12),
                ada=np.concatenate([pack(w) for w in a["ada_w_2"]]))


def constants():
    t = np.arange(TX, dtype=np.float32)
    c = np.zeros((P, NC), np.float32)
    c[:, C_ID:C_ID + P] = np.eye(P)
    f1 = (np.float32(500000.0) ** (-np.arange(8, dtype=np.float32) / np.float32(8)))
    f1 = f1.astype(np.float32)
    f2 = (np.float32(10000.0) ** (-np.arange(16, dtype=np.float32) / np.float32(16)))
    f2 = f2.astype(np.float32)
    for p in range(P):
        d = p % HD
        cos, sin = np.ones(TX), np.zeros(TX)
        if d < 16:
            ang = (t * f1[d % 8]).astype(np.float32)
            cos, sin = np.cos(ang), np.sin(ang) * (-1 if d < 8 else 1)
        c[p, C_R1:C_R1 + TX], c[p, C_R1 + TX:C_R1 + 2 * TX] = cos, sin
        pos = (np.arange(TX) // 64 if d < 32 else np.arange(TX) % 64).astype(np.float32)
        ang = (pos * f2[d % 16]).astype(np.float32)
        c[p, C_R2:C_R2 + TX] = np.cos(ang)
        c[p, C_R2 + TX:C_R2 + 2 * TX] = np.sin(ang) * (-1 if d % 32 < 16 else 1)
        c[p, C_CM + P:C_CM + 2 * P] = np.where(np.arange(P) <= p, 0.0, NEG)
        start = min(max(d - 8, 0), HD - 16)
        k = np.arange(HD)
        c[p, C_WM:C_WM + HD] = np.where((k >= start) & (k < start + 16), 0.0, -1e9)
    for e in range(3):
        for v in range(4):
            for g in range(4):
                for n in range(2):
                    c[32 * e + 8 * v + 2 * g + n, C_TU + 2 * (6 * g + 2 * e + n) + v % 2] = 1.0
    return c


def kernel(**inputs):
    import concourse.bacc as bacc
    from concourse.bass_utils import run_bass_kernel_spmd

    a = {k: np.asarray(v) for k, v in inputs.items() if not k.startswith("rw_")}
    laid = {k: np.ascontiguousarray(v) for k, v in lay_out(a).items()}
    nc = bacc.Bacc("TRN2", target_bir_lowering=False, num_devices=1)
    args = {k: nc.dram_tensor(f"in_{k}", v.shape, F32, kind="ExternalInput").ap()
            for k, v in laid.items()}
    out = nc.dram_tensor("out", (P, KT, TX), F32, kind="ExternalOutput").ap()
    build(nc, args["x"], args["mem"], args["ctx"], args["vec"], args["cst"], args["bias"],
          args["w16"], args["w22"], args["w12"], args["ada"], out)
    r = run_bass_kernel_spmd(nc, [{f"in_{k}": v for k, v in laid.items()}], core_ids=[0])
    got = r.results[0]["out"]
    return np.ascontiguousarray(got.transpose(2, 1, 0)).reshape(1, TX, D)
```

```python
import math
from contextlib import ExitStack

import numpy as np
import concourse.bass as bass
from concourse import mybir

F32 = mybir.dt.float32
F32R = mybir.dt.float32r
ACT = mybir.ActivationFunctionType
ALU = mybir.AluOpType
AX = mybir.AxisListType

P = 128
D = 1024
KT = D // P
TX = 256
TT = 2 * TX
DEPTH = 2
BW = 512
NH1 = 8
HD = 64
TOPK = 64
D_FF = 2816
FH = D_FF // P // 2
EPS = 1e-6
NP = 3
NSQ = 4
NEG = -1e30
TAKEN = -3e38
SLAB = KT * 256
SLAB_OUT = FH * 256
SLAB_MIX = (KT + 4) * P
INDEX_AT = (0, 3, 6, 8, 10, 12, 14, 16, 16)
TOPK_AT = (0, 1, 2, 3, 4, 7, 10, 13, 16)
LAM_INIT = 0.8 - 0.6 * math.exp(-0.3 * 0)

V_NG = 0
V_MG = V_NG + DEPTH * KT
V_FG = V_MG + DEPTH * KT
V_G2 = V_FG + KT
V_AB = V_G2 + DEPTH * 6 * KT * 2
V_SG = V_AB + DEPTH * 9 * KT * 2
V_C = V_SG + 1
V_LM = V_C + 2 * KT
NV = V_LM + 4 * HD
C_ID = 0
C_R1 = C_ID + P
C_R2 = C_R1 + 2 * TX
C_CM = C_R2 + 2 * TX
C_WM = C_CM + 2 * P
C_TU = C_WM + HD
NC = C_TU + 4 * 12
AB = 12
AN = 3 * DEPTH
AR = 6
AH = 4


class Stage:

    def __init__(self, kind, counts, last, slabs=(), T=TT, apply=None, l=0, sub=0,
                 mod=False, steps=(), which=None, units=(), groups=1, half=0, stat=None,
                 more=False, topk=False, index=False):
        self.kind, self.counts, self.last, self.slabs = kind, counts, last, slabs
        self.T, self.apply, self.l, self.sub, self.mod = T, apply, l, sub, mod
        self.steps, self.which, self.units, self.groups = steps, which, units, groups
        self.topk, self.index = topk, index
        self.half, self.stat, self.more, self.late = half, stat, more, False


def norm(apply, T, stat, more=True, **par):
    counts = dict(sqrt_ready=1, rms_ready=1, r_ready=1, scaled=KT)
    last = dict(pe="r_ready", act="sqrt_ready", dve="rms_ready")
    if stat == "own":
        counts |= dict(sq_ready=KT, stat_used=KT)
    if apply == "split":
        counts |= dict(u_hi_ready=KT, u_lo_ready=KT)
        last |= dict(act="u_hi_ready", dve="u_lo_ready")
    else:
        counts |= dict(x_ready=KT)
        last |= dict(dve="x_ready")
    if apply == "resid":
        counts |= dict(sq_ready=KT * more, stat_used=1 + KT * more, xg_ready=KT * more,
                       yg_ready=int(stat == "PA3"))
        if more:
            last |= dict(pe="stat_used", act="xg_ready")
    return Stage("norm", counts, last, T=T, apply=apply, stat=stat, more=more, **par)


def out_y(kind, T, slabs, **par):
    counts = dict(slab_done=4, tile_done=4, sq_ready=KT, sum_ready=KT - 2,
                  yg_ready=KT - (kind == "ffn_out"))
    if kind == "ffn_out":
        counts |= dict(y_ready=KT)
    return Stage(kind, counts, dict(pe="slab_done", act="sq_ready", dve="sum_ready"), slabs,
                 T=T, **par)


def proj(steps, index=False, topk=False):
    act = sum(s[0] in ("copy", "silu", "scale", "nat") for s in steps)
    rope = sum(s[0] in ("rope1", "rope2", "index") for s in steps)
    counts = dict(slab_done=len(steps), taken_act=act, taken_dve=len(steps) - act, out_dve=rope)
    last = dict(pe="slab_done")
    if act:
        last["act"] = "taken_act"
    if act < len(steps):
        last["dve"] = "out_dve" if rope else "taken_dve"
    if topk:
        counts |= dict(topk_ready=2)
    if index:
        counts |= dict(is_ready=2 * NH1, relu_ready=2 * NH1, acc_ready=2 * NH1)
        last = dict(pe="is_ready", act="relu_ready", dve="acc_ready")
    return Stage("proj", counts, last, [SLAB] * len(steps), steps=steps, topk=topk,
                 index=index)


def attn(which, heads):
    if which in "ab":
        units = [[(h, 0, 0, P), (h, 1, P, TX)] for h in range(heads)]
    elif which == "m":
        units = [[(h, 0, 0, TX), (h, 1, TX, TX)] for h in range(heads)]
    else:
        units = [[(h, i, 0, TT)] for h in range(heads) for i in range(2)]
    ny = heads // 2 if which == "n" else 1
    n, groups = len(units), heads if which == "m" else heads // 2
    counts = dict(s_ready=n, negmax_ready=n, p_ready=n, p_normed=n, pt_ready=n, pt_copied=n,
                  o_ready=n, o_taken=groups, y_hi_ready=ny, y_lo_ready=ny)
    return Stage("attn", counts, dict(pe="o_ready", act="y_hi_ready", dve="y_lo_ready"),
                 which=which, units=units, groups=groups)


def ffn(l, sub, T, stat, more=True):
    out = [norm("split", T, stat, l=l, sub=sub, mod=True)]
    for half in range(2):
        out.append(Stage("ffn_in", dict(slab_done=FH, silu_ready=FH, h_ready=FH, g_hi_ready=FH,
                                        g_lo_ready=FH),
                         dict(pe="slab_done", act="g_hi_ready", dve="g_lo_ready"),
                         [SLAB] * FH, T=T, half=half))
        if half == 0:
            out.append(Stage("ffn_out", dict(slab_done=4, tile_done=4, taken_act=4),
                             dict(pe="slab_done", act="taken_act"), [SLAB_OUT] * 4, T=T, half=0))
        else:
            out.append(out_y("ffn_out", T, [SLAB_OUT] * 4, half=1, l=l, sub=sub))
    out.append(norm("resid", T, "PA3", more=more, l=l, sub=sub))
    return out


def make_plan():
    plan = []
    for l in range(DEPTH):
        plan.append(norm("split", TT, "own", l=l))
        qkvg = [("rope1", "q", 2 * i, 0, TX) for i in range(2)]
        qkvg += [("rope1", "k", 2 * i, 0, TX) for i in range(2)]
        qkvg += [("nat", "v", i, 0, TX) for i in range(2)]
        qkvg += [("silu", "g", 2 * i, 0, TX) for i in range(2)]
        plan.append(proj([("rope1", "iq", 0, 0, TX), ("rope1", "iq", 2, 0, TX),
                          ("index", "ik", 0, 0, TX)]))
        plan.append(proj(qkvg, index=True))
        plan.append(attn("a", NH1))
        plan.append(proj(qkvg, topk=True))
        plan.append(attn("b", NH1))
        plan.append(proj([("copy", "k", 0, TX, TX), ("copy", "k", 2, TX, TX),
                          ("nat", "v", 0, TX, TX), ("nat", "v", 1, TX, TX),
                          ("copy", "q", 0, 0, TX), ("copy", "q", 2, 0, TX),
                          ("silu", "g", 0, 0, TX), ("silu", "g", 2, 0, TX)]))
        plan.append(attn("m", 4))
        plan.append(Stage("mix", dict(slab_done=24, gate_ready=24, up_taken=24, merged=24,
                                      m_hi_ready=KT, m_lo_ready=KT),
                          dict(pe="slab_done", act="m_hi_ready", dve="m_lo_ready"),
                          [SLAB_MIX] * 24))
        plan.append(proj([("add_x", "X", 2 * i, 0, TX) for i in range(4)]))
    plan.append(norm("plain", TX, "own"))
    plan.append(Stage("ada", dict(ada_hi_ready=AB * AN, ada_split=AB * AN, ada_used=AB * AN,
                                  rows_copied=AN, rows_moved=48 * AN, turned=AN,
                                  mod_ready=AN + 4, lam_act=2, lam_dve=4, c_ready=1, c_hi_ready=1),
                      dict(pe="turned", act="rows_copied", dve="mod_ready")))
    for l in range(DEPTH):
        plan += ffn(l, 0, TT, "own" if l == 0 else "PB2")
        plan.append(norm("split", TT, "PB2", l=l, sub=1, mod=True))
        T = TT if l == 0 else TX
        q = "rope2" if l == 0 else "scale"
        k = "rope2" if l == 0 else "copy"
        plan.append(proj([(q, "Q", 2 * i, 0, T) for i in range(4)] +
                         [(k, "K", 2 * i, 0, TT) for i in range(4)] +
                         [("nat", "V", i, 0, TT) for i in range(4)]))
        if l == 0:
            n = 32
            plan.append(Stage("diff", dict(s_ready=n, negmax_ready=n, p_ready=n, p_normed=n,
                                           pt_ready=n, pt_copied=n, o_ready=n, o_taken=n,
                                           o_sq_ready=n, o_sqrt_ready=1, o_scaled=n, ot_ready=8,
                                           og_ready=8, y_hi_ready=8, y_lo_ready=8),
                              dict(pe="ot_ready", act="y_hi_ready", dve="y_lo_ready"),
                              units=[(h, t) for h in range(8) for t in range(4)]))
        else:
            plan.append(attn("n", 16))
        plan.append(out_y("proj_y", T, [SLAB] * 4, l=l, sub=1))
        plan.append(norm("resid", T, "PB3", l=l, sub=1))
        plan += ffn(l, 2, T, "PB2", more=l + 1 < DEPTH)
    plan[1].late = True
    for n, st in enumerate(plan):
        if st.apply == "resid" and st.more:
            plan[n + 2].late = True
    at, last, sizes = {}, {}, []
    for n, st in enumerate(plan):
        st.at, st.before, st.s0 = dict(at), dict(last), len(sizes)
        sizes += st.slabs
        for name, count in st.counts.items():
            at[name] = at.get(name, 0) + count
        for name in st.counts:
            st.at.setdefault(name, 0)
        for engine, name in st.last.items():
            last[engine] = (name, at[name])
    return plan, at, last, sizes


def build(nc, x_in, mem_in, ctx_in, vec_in, cst_in, bias_in, w16, w22, w12, w_ada, out):
    plan, totals, finals, sizes = make_plan()
    ns = len(sizes)

    with ExitStack() as ctx:
        base = 16512

        def sb(name, shape, dt, at):
            return nc.alloc_sbuf_tensor_at(name, [P] + shape, dt, offset=base + at)

        kb = 1024
        raw = [sb(f"raw{u}", [SLAB_OUT], F32, 11 * kb * u) for u in range(2)]
        wh = [sb(f"w_hi{u}", [SLAB_OUT], F32R, 22 * kb + 11 * kb * u) for u in range(2)]
        wl = [sb(f"w_lo{u}", [SLAB_OUT], F32R, 44 * kb + 11 * kb * u) for u in range(2)]
        u_hi = sb("u_hi", [KT, TT], F32R, 66 * kb)
        u_lo = sb("u_lo", [KT, TT], F32R, 82 * kb)
        X = sb("X", [KT, TT], F32, 98 * kb)
        YO = 114 * kb
        Y = sb("Y", [KT, TT], F32, YO)
        q1, k1, g1 = [sb(f"{n}1", [4, TX], F32, YO + 4 * kb * i) for i, n in enumerate("qkg")]
        v1 = sb("v1", [2, BW], F32, YO + 12 * kb)
        merged = sb("merged", [KT, TX], F32, YO)
        Q = sb("Q", [KT, TT], F32, YO)
        qn = sb("qn", [KT, TX], F32, YO)
        on = sb("on", [32, P], F32, YO)
        GO = 130 * kb
        g_hi = sb("g_hi", [FH, TT], F32R, GO)
        g_lo = sb("g_lo", [FH, TT], F32R, GO + 22 * kb)
        y_hi = sb("y_hi", [12, TX], F32R, GO)
        y_lo = sb("y_lo", [12, TX], F32R, GO + 22 * kb)
        mg_hi = sb("mg_hi", [KT, TX], F32R, GO + 12 * kb)
        mg_lo = sb("mg_lo", [KT, TX], F32R, GO + 34 * kb)
        iq = sb("iq", [4, TX], F32, GO + 12 * kb)
        ik = sb("ik", [TX], F32, GO + 16 * kb)
        sel_bias = sb("sel_bias", [2, TX], F32, GO + 17 * kb)
        idx_acc = sb("idx_acc", [2, TX], F32, GO + 19 * kb)
        K = sb("K", [KT, TT], F32, GO)
        V = sb("V", [4, D], F32, GO + 16 * kb)
        na_bias = sb("na_bias", [4, TT], F32, GO + 32 * kb)
        ro = [66 * kb + 8 * kb * u for u in range(4)] + [GO, GO + 20 * kb]
        ho = [YO, YO + 8 * kb, GO + 8 * kb, GO + 28 * kb]
        ada_raw = [sb(f"ada_raw{u}", [SLAB], F32, ro[u]) for u in range(AR)]
        ada_lo = [sb(f"ada_lo{u}", [SLAB], F32R, ro[u]) for u in range(AR)]
        ada_hi = [sb(f"ada_hi{u}", [SLAB], F32R, ho[u]) for u in range(AH)]
        ada_rows = sb("ada_rows", [4 * 256], F32, GO + 36 * kb)
        ada_turn = sb("ada_turn", [P], F32, GO + 40 * kb)
        c_f32 = sb("c_f32", [KT, 160], F32, 174 * kb)
        c_split = sb("c_split", [KT, 160], F32R, 182 * kb)
        SO = 174 * kb
        sq = sb("sq", [NSQ, TT], F32, SO)
        sqsum = sb("sqsum", [TT], F32, SO + 8 * kb)
        rms_root = sb("rms_root", [P], F32, SO + 10 * kb)
        rms = sb("rms", [P], F32, SO + 10 * kb + 512)
        silu = sb("silu", [2, TT], F32, SO)
        h_f32 = sb("h_f32", [2, TT], F32, SO + 4 * kb)
        shuf = sb("shuf", [2, TX], F32, SO)
        sig = sb("sig", [2, TX], F32, SO)
        upg = sb("upg", [2, TX], F32, SO + 2 * kb)
        relu = sb("relu", [2, TX], F32, SO + 4 * kb)
        s_sb = sb("s_sb", [NP, TT], F32, SO)
        p_sb = sb("p_sb", [NP, TT], F32, SO + 6 * kb)
        pt_sb = sb("pt_sb", [2, TT], F32, SO + 12 * kb)
        p2_sb = sb("p2_sb", [NP, 2, TT], F32, SO)
        og = sb("og", [2, TT], F32, SO)
        CO = 190 * kb
        cst = sb("cst", [NC], F32, CO)
        CO += 4 * NC
        vec = sb("vec", [NV], F32, CO)
        CO += -(-4 * NV // 32) * 32
        ones = sb("ones", [P], F32, CO)
        spread = sb("spread", [4, P], F32, CO + 512)
        CO += 2048
        mod = sb("mod", [DEPTH, 9, KT, 2], F32, CO + 512)
        CO += 512 + 4 * DEPTH * 9 * KT * 2
        gs = sb("gs", [DEPTH, 3, KT, 2], F32, CO)
        gg = sb("gg", [DEPTH, 3, KT, 2], F32, CO + 4 * DEPTH * 3 * KT * 2)
        CO += 8 * DEPTH * 3 * KT * 2
        wi = sb("wi", [2, NH1], F32, CO)
        top8 = sb("top8", [8], F32, CO + 64)
        eps = sb("eps", [2], F32, CO + 96)
        lam = sb("lam", [8], F32, CO + 128)
        mx = sb("mx", [NP, 2], F32, CO + 160)
        nm = sb("nm", [NP, 2], F32, CO + 192)
        rs = sb("rs", [NP, 2], F32, CO + 224)
        ri = sb("ri", [4, 2], F32, CO + 256)
        rw = sb("rw", [NP], F32, CO + 288)
        sub_g = sb("sub_g", [1], F32, CO + 320)
        ssq = sb("ssq", [32], F32, CO + 352)
        sroot = sb("sroot", [32], F32, CO + 480)
        srec = sb("srec", [32], F32, CO + 608)
        lam_tmp = sb("lam_tmp", [2, HD], F32, CO + 736)
        junk = sb("junk", [1], F32, CO + 736 + 1024)
        osq = sb("osq", [P], F32, CO + 736 + 512)
        CO += 736 + 1024 + 32
        assert base + CO <= 229368, CO

        PA = ctx.enter_context(nc.psum_tensor("PA", [P, 4, 512], F32))
        PB = ctx.enter_context(nc.psum_tensor("PB", [P, 4, 512], F32))

        ident = cst[:, C_ID:C_ID + P]
        dest = dict(q=q1, k=k1, g=g1, v=v1, iq=iq, ik=ik, Q=Q, K=K, V=V, Y=Y, X=X)

        names = set(totals) | {"raw_full0", "raw_full1", "w_hi_ready", "w_split", "chain",
                               "ones_ready", "consts_in", "x_in", "mem_in", "ctx_in", "no_bias",
                               "c_zero", "stored", "bias_ready"}
        names |= {f"bias_in{u}" for u in range(4)}
        names |= {f"ada_full{u}" for u in range(AR)}
        sem = {n: ctx.enter_context(nc.semaphore(n)) for n in sorted(names)}
        raw_full = [sem["raw_full0"], sem["raw_full1"]]
        block = ctx.enter_context(nc.Block())

        def before(st, engine):
            name, value = st.before.get(engine, ("ones_ready", 8))
            return sem[name], value

        def stat_bank(st):
            return PB[:, 2, :] if st.stat in ("own", "PB2") else \
                PA[:, 3, :] if st.stat == "PA3" else PB[:, 3, :]

        def width(unit):
            return sum(nk for _, _, _, nk in unit)

        class Chain:

            n = 0

            def up(self):
                self.n += 1
                return 1

        @block.sync
        def _(sp):
            sp.dma_start(X[:, :, 0:TX], x_in).then_inc(sem["x_in"], 16)
            sp.dma_start(X[:, :, TX:TT], mem_in).then_inc(sem["mem_in"], 16)
            sp.wait_ge(sem["x_in"], 16)
            sp.wait_ge(sem["mem_in"], 16)
            src = {SLAB: w16, SLAB_OUT: w22, SLAB_MIX: w12}
            used = {SLAB: 0, SLAB_OUT: 0, SLAB_MIX: 0}
            ada = [st for st in plan if st.kind == "ada"][0]
            out_proj = plan[plan.index(ada) - 2]

            def load_ada():
                for engine in ("pe", "act", "dve"):
                    sp.wait_ge(*before(out_proj, engine))
                for j in range(AR):
                    sp.dma_start(ada_raw[j][:, :], w_ada[j, :, :])\
                      .then_inc(sem[f"ada_full{j}"], 16)
                with sp.Fori(0, AB * AN // AR - 1) as i:
                    for u in range(AR):
                        sp.wait_ge(sem["ada_used"], i * AR + (u + 1))
                        sp.dma_start(ada_raw[u][:, :], w_ada[bass.ds(i * AR + (AR + u), 1), :, :]
                                     .rearrange("a p n -> p (a n)"))\
                          .then_inc(sem[f"ada_full{u}"], 16)

            near = [st for st in plan if st.kind == "attn" and st.which == "n"][0]

            def load_bias():
                for engine in ("pe", "act", "dve"):
                    sp.wait_ge(*before(near, engine))
                for i, unit in enumerate(near.units):
                    h, qt, _, _ = unit[0]
                    if i >= 4:
                        sp.wait_ge(sem["negmax_ready"], near.at["negmax_ready"] + i - 3)
                    sp.dma_start(na_bias[:, i % 4, 0:TX], bias_in[:, h, qt, :])\
                      .then_inc(sem[f"bias_in{i % 4}"], 16)

            s = 0
            while s < ns:
                if s == ada.s0 + 2:
                    load_ada()
                if s == near.s0 + 2:
                    load_bias()
                size, n = sizes[s], 1
                while (s + n < ns and sizes[s + n] == size
                       and s + n not in (ada.s0 + 2, near.s0 + 2)):
                    n += 1
                pairs = (n - 2) // 2 if s == 0 else n // 2

                def load(s, half, index):
                    if not isinstance(s, int) or s >= 2:
                        sp.wait_ge(sem["w_split"], s - 1)
                    sp.dma_start(raw[half][:, 0:size],
                                 src[size][bass.ds(index, 1), :, :].rearrange("a p n -> p (a n)"))\
                      .then_inc(raw_full[half], 16)

                first = used[size]
                done = 0
                if s == 0:
                    load(0, 0, first)
                    load(1, 1, first + 1)
                    done = 2
                if pairs > 1:
                    with sp.Fori(0, pairs) as i:
                        for p in range(2):
                            load(i * 2 + (s + done + p), (s + done + p) % 2,
                                 i * 2 + (first + done + p))
                    done += 2 * pairs
                for p in range(done, n):
                    load(s + p, (s + p) % 2, first + p)
                used[size] += n
                s += n
            name, value = finals["dve"]
            sp.wait_ge(sem[name], value)
            sp.dma_start(out, X[:, :, 0:TX]).then_inc(sem["stored"], 16)
            sp.wait_ge(sem["stored"], 16)

        @block.tensor
        def _(pe):
            def mm3(psum, u, wcol, hi, lo, first, last):
                whi, wlo = wh[u][:, wcol:wcol + P], wl[u][:, wcol:wcol + P]
                pe.matmul(psum, whi, hi, start=first, stop=False)
                pe.matmul(psum, whi, lo, start=False, stop=False)
                return pe.matmul(psum, wlo, hi, start=False, stop=last)

            def nat3(psum, u, c0, c1, k, hi, lo, first, last):
                whi, wlo = wh[u][:, k * 256 + c0:k * 256 + c1], wl[u][:, k * 256 + c0:k * 256 + c1]
                pe.matmul(psum, hi, whi, start=first, stop=False)
                pe.matmul(psum, lo, whi, start=False, stop=False)
                return pe.matmul(psum, hi, wlo, start=False, stop=last)

            def add_squares(bank, tile, T, first, last):
                for t in range(T // P):
                    mm = pe.matmul(bank[32 * t:32 * t + 32, 0:P], ones[:, 0:32],
                                   tile[:, t * P:t * P + P], start=first, stop=last)
                return mm

            def pe_norm(st):
                T = st.T
                bank = stat_bank(st)
                pe.wait_ge(*before(st, "act"))
                pe.wait_ge(*before(st, "dve"))
                if st.stat == "own":
                    for k in range(KT):
                        pe.wait_ge(sem["sq_ready"], st.at["sq_ready"] + k + 1)
                        add_squares(bank, sq[:, k % NSQ, :], T, k == 0, k == KT - 1)\
                            .then_inc(sem["stat_used"], 1)
                if st.apply == "resid":
                    pe.wait_ge(sem["sum_ready"], st.at["sum_ready"])
                    add_squares(bank, sqsum, T, True, False)
                    pe.wait_ge(sem["sq_ready"], st.at["sq_ready"])
                    add_squares(bank, sq[:, (KT - 1) % NSQ, :], T, False, True)\
                        .then_inc(sem["stat_used"], 1)
                pe.wait_ge(sem["rms_ready"], st.at["rms_ready"] + 1)
                for t in range(T // P):
                    mm = pe.matmul(bank[:, t * P:t * P + P], spread[0:T // 4, t, :],
                                   rms[0:T // 4, :], start=True, stop=True)
                mm.then_inc(sem["r_ready"], 1)
                if st.apply == "resid" and st.more:
                    for k in range(KT):
                        pe.wait_ge(sem["sq_ready"], st.at["sq_ready"] + k + 1)
                        add_squares(PB[:, 2, :], sq[:, k % NSQ, :], T, k == 0, k == KT - 1)\
                            .then_inc(sem["stat_used"], 1)

            def operand(st):
                prev = plan[plan.index(st) - 1]
                if prev.kind == "norm":
                    return "u_lo_ready"
                if prev.kind == "mix":
                    pe.wait_ge(sem["up_taken"], st.at["up_taken"])
                    return "m_lo_ready"
                if prev.kind == "diff":
                    pe.wait_ge(sem["og_ready"], st.at["og_ready"] - 2)
                    return "y_lo_ready"
                if prev.kind == "proj":
                    pe.wait_ge(sem["taken_dve"], st.at["taken_dve"])
                    pe.wait_ge(sem["taken_act"], st.at["taken_act"])
                elif prev.kind == "ffn_out":
                    pe.wait_ge(sem["h_ready"], st.at["h_ready"])
                elif prev.kind == "attn" and prev.which == "n":
                    pe.wait_ge(sem["p_ready"], st.at["p_ready"])
                    return "y_lo_ready"
                elif prev.kind == "attn":
                    pe.wait_ge(sem["o_taken"], st.at["o_taken"])
                    pe.wait_ge(sem["p_ready"], st.at["p_ready"])
                    pe.wait_ge(sem["pt_copied"], st.at["pt_copied"])
                else:
                    pe.wait_ge(*before(st, "act"))
                    pe.wait_ge(*before(st, "dve"))
                return None

            def first_slab(st, ready, out, hi, lo, t0, T):
                pe.wait_ge(sem["w_split"], st.s0 + 1)
                for k in range(KT):
                    pe.wait_ge(sem[ready], st.at[ready] - KT + k + 1)
                    for c in range(2):
                        mm = mm3(out[c], st.s0 % 2, k * 256 + c * P, hi[:, k, t0:t0 + T],
                                 lo[:, k, t0:t0 + T], k == 0, k == KT - 1)
                mm.then_inc(sem["slab_done"], 1)

            def index_scores(st, j):
                qt, h = j // NH1, j % NH1
                p0, nk = HD * (h % 2), (qt + 1) * P
                if j == 0:
                    pe.wait_ge(sem["out_dve"], st.at["out_dve"])
                if j >= 4:
                    pe.wait_ge(sem["relu_ready"], st.at["relu_ready"] + j - 3)
                pe.matmul(PB[:, j % 4, 0:nk], iq[p0:p0 + HD, h // 2, qt * P:qt * P + P],
                          ik[p0:p0 + HD, 0:nk], start=True, stop=True)\
                  .then_inc(sem["is_ready"], 1)

            def pe_proj(st):
                by_tile = operand(st)
                hi, lo = (mg_hi, mg_lo) if st.steps[0][0] == "add_x" else (u_hi, u_lo)
                act = dve = 0
                taken = []
                for i, (how, to, tile, t0, T) in enumerate(st.steps):
                    s = st.s0 + i
                    u, ps = s % 2, i % 2
                    if i == 0 and by_tile:
                        first_slab(st, by_tile, [PA[:, c, 0:T] for c in range(2)], hi, lo, t0, T)
                        taken.append(("taken_act", 1) if how == "scale" else ("taken_dve", 1))
                        act, dve = (1, 0) if how == "scale" else (0, 1)
                        continue
                    if i >= 2:
                        name, count = taken[i - 2]
                        pe.wait_ge(sem[name], st.at[name] + count)
                    pe.wait_ge(sem["w_split"], s + 1)
                    if how == "nat":
                        for t in range(T // P):
                            po = PA[:, 2 * ps + t // 2, (t % 2) * 256:(t % 2) * 256 + 256]
                            tok = slice(t0 + t * P, t0 + t * P + P)
                            for k in range(KT):
                                mm = nat3(po, u, 0, 256, k, u_hi[:, k, tok], u_lo[:, k, tok],
                                          k == 0, k == KT - 1)
                    elif how == "index":
                        for k in range(KT):
                            mm3(PA[:, 2 * ps, 0:TX], u, k * 256, u_hi[:, k, 0:TX],
                                u_lo[:, k, 0:TX], k == 0, k == KT - 1)
                        for t in range(2):
                            po = PA[:, 2 * ps, TX + 8 * t:TX + 8 * t + 8]
                            tok = slice(t * P, t * P + P)
                            for k in range(KT):
                                mm = nat3(po, u, P, P + NH1, k, u_hi[:, k, tok],
                                          u_lo[:, k, tok], k == 0, k == KT - 1)
                    else:
                        for c in range(2):
                            po = PA[:, 2 * ps + c, 0:T]
                            for k in range(KT):
                                mm = mm3(po, u, k * 256 + c * P, hi[:, k, t0:t0 + T],
                                         lo[:, k, t0:t0 + T], k == 0, k == KT - 1)
                    mm.then_inc(sem["slab_done"], 1)
                    if st.index:
                        for j in range(INDEX_AT[i], INDEX_AT[i + 1]):
                            index_scores(st, j)
                    if how in ("copy", "silu", "scale", "nat"):
                        act += 1
                        taken.append(("taken_act", act))
                    else:
                        dve += 1
                        taken.append(("taken_dve", dve))

            def pe_ffn_in(st):
                T = st.T
                by_tile = operand(st)

                def step(i, p):
                    s = st.s0 + p
                    u, ps = s % 2, p % 2
                    if not isinstance(i, int) or i + p >= 2:
                        pe.wait_ge(sem["h_ready"], st.at["h_ready"] + (i + (p - 1)))
                    pe.wait_ge(sem["w_split"], i + (s + 1))
                    for c in range(2):
                        for k in range(KT):
                            mm = mm3(PA[:, 2 * ps + c, 0:T], u, k * 256 + c * P, u_hi[:, k, 0:T],
                                     u_lo[:, k, 0:T], k == 0, k == KT - 1)
                    mm.then_inc(sem["slab_done"], 1)

                if by_tile:
                    first_slab(st, by_tile, [PA[:, c, 0:T] for c in range(2)], u_hi, u_lo, 0, T)
                else:
                    step(0, 0)
                step(0, 1)
                with pe.Fori(0, (FH - 3) // 2) as i:
                    step(i * 2, 2)
                    step(i * 2, 3)
                step(0, FH - 1)

            def pe_out(st):
                T = st.T
                ffn = st.kind == "ffn_out"
                if ffn:
                    pe.wait_ge(sem["taken_act"], st.at["taken_act"])
                    pe.wait_ge(sem["g_lo_ready"], st.at["g_lo_ready"] - 1)
                else:
                    ready = operand(st)
                nk, hi, lo, bank = (FH, g_hi, g_lo, PB) if ffn else (KT, u_hi, u_lo, PA)
                for p in range(4):
                    s = st.s0 + p
                    u, ps = s % 2, p % 2
                    if p >= 2:
                        if not ffn:
                            pe.wait_ge(sem["sq_ready"], st.at["sq_ready"] + 2 * (p - 1))
                        elif st.half == 0:
                            pe.wait_ge(sem["taken_act"], st.at["taken_act"] + p - 1)
                        else:
                            pe.wait_ge(sem["y_ready"], st.at["y_ready"] + 2 * (p - 1))
                    pe.wait_ge(sem["w_split"], s + 1)
                    if p == 0 and not ffn and ready:
                        for k in range(KT):
                            pe.wait_ge(sem[ready], st.at[ready] - KT + k + 1)
                            for c in range(2):
                                mm = mm3(PA[:, c, 0:T], u, k * 256 + c * P, u_hi[:, k, 0:T],
                                         u_lo[:, k, 0:T], k == 0, k == KT - 1)
                                if k == KT - 1:
                                    mm.then_inc(sem[("tile_done", "slab_done")[c]], 1)
                        continue
                    for c in range(2):
                        for k in range(nk):
                            if ffn and (p, c, k) == (0, 0, nk - 1):
                                pe.wait_ge(sem["g_lo_ready"], st.at["g_lo_ready"])
                            mm = mm3(bank[:, 2 * ps + c, 0:T], u, k * 256 + c * P, hi[:, k, 0:T],
                                     lo[:, k, 0:T], k == 0, k == nk - 1)
                        mm.then_inc(sem[("tile_done", "slab_done")[c]], 1)

            def started(st, unit):
                left = 1 if unit == 0 else 0
                pe.wait_ge(sem["taken_act"], st.at["taken_act"] - left)
                pe.wait_ge(sem["out_dve"], st.at["out_dve"])

            def pe_attn(st):
                n, w = len(st.units), st.which
                per = n // st.groups
                for i in range(n + 3):
                    if i < n:
                        if i in (0, 2):
                            started(st, i)
                        if i >= 4:
                            pe.wait_ge(sem["p_ready"], st.at["p_ready"] + i - 3)
                        for h, qt, off, nk in st.units[i]:
                            mm = scores(w, h, qt, PA[:, i % 4, off:off + nk], nk)
                        mm.then_inc(sem["s_ready"], 1)
                    if 2 <= i < n + 2:
                        j = i - 2
                        pe.wait_ge(sem["p_normed"], st.at["p_normed"] + j + 1)
                        if j >= 2:
                            pe.wait_ge(sem["pt_copied"], st.at["pt_copied"] + j - 1)
                        for b in range(width(st.units[j]) // P):
                            mm = pe.transpose(PB[:, 2 + j % 2, b * P:b * P + P],
                                              p_sb[:, j % NP, b * P:b * P + P], ident)
                        mm.then_inc(sem["pt_ready"], 1)
                    if i >= 3:
                        j = i - 3
                        g = j // per
                        if g >= 2 and j % per == 0:
                            pe.wait_ge(sem["o_taken"], st.at["o_taken"] + g - 1)
                        pe.wait_ge(sem["pt_copied"], st.at["pt_copied"] + j + 1)
                        for h, qt, off, nk in st.units[j]:
                            m = P if w == "m" else HD
                            p0 = 0 if w == "m" else HD * (h % 2)
                            values = V if w == "n" else v1
                            for b in range(nk // P):
                                mm = pe.matmul(PB[p0:p0 + m, g % 2, qt * P:qt * P + P],
                                               values[:, b, h * m:h * m + m],
                                               pt_sb[:, j % 2, off + b * P:off + b * P + P],
                                               start=(b == 0), stop=(b == nk // P - 1))
                        mm.then_inc(sem["o_ready"], 1)

            def scores(w, h, qt, bank, nk):
                if w == "m":
                    return pe.matmul(bank, q1[:, h, qt * P:qt * P + P], k1[:, h, 0:nk],
                                     start=True, stop=True)
                p0 = HD * (h % 2)
                q_, k_ = (q1, k1) if w in "ab" else (qn, K)
                return pe.matmul(bank, q_[p0:p0 + HD, h // 2, qt * P:qt * P + P],
                                 k_[p0:p0 + HD, h // 2, 0:nk], start=True, stop=True)

            def pe_mix(st):
                pe.wait_ge(sem["o_taken"], st.at["o_taken"])
                pe.wait_ge(sem["p_ready"], st.at["p_ready"])
                pe.wait_ge(sem["pt_copied"], st.at["pt_copied"])
                pe.wait_ge(sem["y_lo_ready"], st.at["y_lo_ready"] - 1)

                def step(b, i, p):
                    s = st.s0 + 8 * b + p
                    u, ps = s % 2, p % 2
                    if b or p >= 2:
                        pe.wait_ge(sem["up_taken"], st.at["up_taken"] + (i + (8 * b + p - 1)))
                    pe.wait_ge(sem["w_split"], i + (s + 1))
                    for k in range(KT):
                        mm3(PA[:, 2 * ps, 0:TX], u, k * P, u_hi[:, k, 0:TX], u_lo[:, k, 0:TX],
                            k == 0, k == KT - 1)
                    for k in range(4):
                        mm = mm3(PA[:, 2 * ps + 1, 0:TX], u, (KT + k) * P, y_hi[:, 4 * b + k, :],
                                 y_lo[:, 4 * b + k, :], k == 0, k == 3)
                    mm.then_inc(sem["slab_done"], 1)

                for b in range(3):
                    if b == 2:
                        pe.wait_ge(sem["y_lo_ready"], st.at["y_lo_ready"])
                    step(b, 0, 0)
                    step(b, 0, 1)
                    with pe.Fori(0, 3) as i:
                        step(b, i * 2, 2)
                        step(b, i * 2, 3)

            def pe_ada(st):
                pe.wait_ge(*before(st, "act"))
                pe.wait_ge(*before(st, "dve"))
                pe.wait_ge(sem["mod_ready"], 1)

                def slabs(i, j0, j1):
                    for j in range(j0, j1):
                        g, e = j // 3, j % 3
                        po = PA[0:96, g // 2, 256 * (g % 2):256 * (g % 2) + 256]
                        pe.wait_ge(sem["ada_split"], i + (j + 1))
                        for k in range(KT):
                            w = slice(k * 256, k * 256 + 256)
                            c = c_split[:, k, 64 - 32 * e:160 - 32 * e]
                            pe.matmul(po, c, ada_hi[j % AH][:, w],
                                      start=(e == 0 and k == 0), stop=False)
                            mm = pe.matmul(po, c, ada_lo[j % AR][:, w], start=False,
                                           stop=(e == 2 and k == KT - 1))
                        mm.then_inc(sem["ada_used"], 1)

                def turn(i):
                    pe.wait_ge(sem["rows_moved"], i * 48 + 48)
                    pe.wait_ge(sem["mod_ready"], i + 1)
                    pe.matmul(PA[:, 3, 0:4 * AB], ada_turn[0:8 * AB, :],
                              cst[0:8 * AB, C_TU:C_TU + 4 * AB], start=True, stop=True)\
                      .then_inc(sem["turned"], 1)

                slabs(0, 0, AB)
                with pe.Fori(0, AN - 1) as i:
                    pe.wait_ge(sem["rows_copied"], i + 1)
                    slabs(i * AB + AB, 0, 8)
                    turn(i)
                    slabs(i * AB + AB, 8, AB)
                turn(AN - 1)

            def pe_diff(st):
                n = len(st.units)
                for i in range(n + 3):
                    if i < n:
                        h, t = st.units[i]
                        k0 = 0 if t < 2 else TX
                        if i in (0, 1):
                            started(st, i)
                        if i >= 2:
                            pe.wait_ge(sem["p_ready"], st.at["p_ready"] + i - 1)
                        for j in range(2):
                            p0 = HD * j
                            mm = pe.matmul(PA[:, 2 * (i % 2) + j, 0:TT - k0],
                                           Q[p0:p0 + HD, h, t * P:t * P + P],
                                           K[p0:p0 + HD, h, k0:TT], start=True, stop=True)
                        mm.then_inc(sem["s_ready"], 1)
                    if 2 <= i < n + 2:
                        j = i - 2
                        pe.wait_ge(sem["p_normed"], st.at["p_normed"] + j + 1)
                        if j >= 2:
                            pe.wait_ge(sem["pt_copied"], st.at["pt_copied"] + j - 1)
                        for b in range(4 if st.units[j][1] < 2 else 2):
                            mm = pe.transpose(PB[:, 2 + j % 2, b * P:b * P + P],
                                              p2_sb[:, j % NP, 0, b * P:b * P + P], ident)
                        mm.then_inc(sem["pt_ready"], 1)
                    if i >= 3:
                        j = i - 3
                        h, t = st.units[j]
                        if j >= 2:
                            pe.wait_ge(sem["o_taken"], st.at["o_taken"] + j - 1)
                        pe.wait_ge(sem["pt_copied"], st.at["pt_copied"] + j + 1)
                        nb, b0 = (4, 0) if t < 2 else (2, 2)
                        for b in range(nb):
                            mm = pe.matmul(PB[:, j % 2, 0:P], pt_sb[:, j % 2, b * P:b * P + P],
                                           V[:, b0 + b, h * P:h * P + P],
                                           start=(b == 0), stop=(b == nb - 1))
                        mm.then_inc(sem["o_ready"], 1)
                for h in range(8):
                    pe.wait_ge(sem["o_scaled"], st.at["o_scaled"] + (4 * h + 4))
                    if h >= 4:
                        pe.wait_ge(sem["og_ready"], st.at["og_ready"] + h - 3)
                    for t in range(4):
                        mm = pe.transpose(PA[:, h % 4, t * P:t * P + P], on[:, 4 * h + t, :],
                                          ident)
                    mm.then_inc(sem["ot_ready"], 1)

            run = dict(norm=pe_norm, proj=pe_proj, ffn_in=pe_ffn_in, ffn_out=pe_out, proj_y=pe_out,
                       attn=pe_attn, mix=pe_mix, ada=pe_ada, diff=pe_diff)
            pe.wait_ge(sem["consts_in"], 32)
            for st in plan:
                if st.kind in run:
                    run[st.kind](st)

        @block.scalar
        def _(act):
            def feed(s, i=0):
                if s >= ns:
                    return
                u = s % 2
                half = i if isinstance(i, int) else None
                act.wait_ge(raw_full[u], (feed_pair * 16 if half is None else 0) +
                            16 * (s // 2 + 1))
                if s >= 2:
                    act.wait_ge(sem["slab_done"], i + (s - 1))
                act.activation(wh[u][:, 0:sizes[s]], raw[u][:, 0:sizes[s]], ACT.Copy)\
                   .then_inc(sem["w_hi_ready"], 1)

            feed_pair = 0

            def sqrt_table():
                act.activation(junk[:, :], eps[:, 0:1], ACT.Sqrt)

            def times_gain(st, to, src, gain, k):
                for v in range(st.T // TX):
                    tok = slice(v * TX, v * TX + TX)
                    ins = act.activation(to[:, k, tok], src[:, tok], ACT.Copy,
                                         scale=gain[:, st.l, st.sub, k, v:v + 1])
                return ins

            def act_norm(st):
                T = st.T
                act.wait_ge(*before(st, "pe"))
                act.wait_ge(*before(st, "act"))
                act.wait_ge(*before(st, "dve"))
                if st.stat == "own":
                    for k in range(KT):
                        if k >= NSQ:
                            act.wait_ge(sem["stat_used"], st.at["stat_used"] + k - NSQ + 1)
                        act.activation(sq[:, k % NSQ, 0:T], X[:, k, 0:T], ACT.Square)\
                           .then_inc(sem["sq_ready"], 1)
                    if st is plan[0]:
                        feed(0)
                    else:
                        sqrt_table()
                rows = T // P * 32
                stat = KT if st.stat == "own" else 1 if st.apply == "resid" else 0
                act.wait_ge(sem["stat_used"], st.at["stat_used"] + stat)
                act.activation(rms_root[0:rows, :], stat_bank(st)[0:rows, 0:P], ACT.Sqrt,
                               scale=1.0 / D, bias=eps[0:rows, 1:2])\
                   .then_inc(sem["sqrt_ready"], 1)
                if st.stat == "PA3":
                    times_gain(st, Y, Y[:, KT - 1, :], gg, KT - 1).then_inc(sem["yg_ready"], 1)
                if st.apply == "resid" and st.more:
                    for k in range(KT):
                        act.wait_ge(sem["x_ready"], st.at["x_ready"] + k + 1)
                        if k >= NSQ:
                            act.wait_ge(sem["stat_used"], st.at["stat_used"] + k - NSQ + 2)
                        act.activation(sq[:, k % NSQ, 0:T], X[:, k, 0:T], ACT.Square)\
                           .then_inc(sem["sq_ready"], 1)
                        times_gain(plan[plan.index(st) + 1], Y, X[:, k, :], gs, k)\
                            .then_inc(sem["xg_ready"], 1)
                if st.apply == "split":
                    for k in range(KT):
                        act.wait_ge(sem["scaled"], st.at["scaled"] + k + 1)
                        for v in range(T // TX):
                            tok = slice(v * TX, v * TX + TX)
                            if st.mod:
                                ins = act.activation(u_hi[:, k, tok], Y[:, k, tok],
                                                     ACT.Identity,
                                                     bias=mod[:, st.l, 3 * st.sub, k, v:v + 1])
                            else:
                                ins = act.activation(u_hi[:, k, tok], Y[:, k, tok],
                                                     ACT.Copy)
                        ins.then_inc(sem["u_hi_ready"], 1)

            def index_relu(st, j):
                nk = (j // NH1 + 1) * P
                act.wait_ge(sem["is_ready"], st.at["is_ready"] + j + 1)
                if j >= 2:
                    act.wait_ge(sem["acc_ready"], st.at["acc_ready"] + j - 1)
                act.activation(relu[:, j % 2, 0:nk], PB[:, j % 4, 0:nk], ACT.Relu,
                               scale=HD ** -0.5).then_inc(sem["relu_ready"], 1)

            def act_proj(st):
                act.wait_ge(*before(st, "pe"))
                act.wait_ge(*before(st, "act"))
                act.wait_ge(*before(st, "dve"))
                if st.late:
                    feed(st.s0 + 1)
                def take(i):
                    how, to, tile, t0, T = st.steps[i]
                    ps = i % 2
                    act.wait_ge(sem["slab_done"], st.at["slab_done"] + i + 1)
                    if how == "nat":
                        nt = T // P
                        src = PA[:, 2 * ps:2 * ps + nt // 2, :]\
                            .rearrange("p b (t c) -> p (b t) c", c=256)
                        dst = dest[to][:, 0:nt, tile * 256:tile * 256 + 256]
                    elif T == TX:
                        src = PA[:, 2 * ps:2 * ps + 2, 0:TX]
                        full = qn if to == "Q" else dest[to]
                        dst = full[:, tile:tile + 2, 0:TX]
                    else:
                        src = PA[:, 2 * ps:2 * ps + 2, :]
                        dst = dest[to][:, tile:tile + 2, 0:TT]
                    if how == "silu":
                        ins = act.activation(dst, src, ACT.Silu)
                    elif how == "scale":
                        ins = act.activation(dst, src, ACT.Copy, scale=HD ** -0.5)
                    else:
                        ins = act.activation(dst, src, ACT.Copy)
                    ins.then_inc(sem["taken_act"], 1)

                for i, (how, to, tile, t0, T) in enumerate(st.steps):
                    s = st.s0 + i
                    if st.index and i:
                        for m in range(INDEX_AT[i - 1], INDEX_AT[i]):
                            index_relu(st, m)
                    if how in ("copy", "silu", "scale", "nat"):
                        take(i)
                    feed(s + 2)

            def act_ffn_in(st):
                nonlocal feed_pair
                T = st.T
                act.wait_ge(*before(st, "pe"))
                act.wait_ge(*before(st, "act"))
                act.wait_ge(*before(st, "dve"))

                if st.late:
                    feed(st.s0 + 1)

                def step(i, p):
                    ps = p % 2
                    act.wait_ge(sem["slab_done"], st.at["slab_done"] + (i + (p + 1)))
                    act.activation(silu[:, ps, 0:T], PA[:, 2 * ps, 0:T], ACT.Silu)\
                       .then_inc(sem["silu_ready"], 1)
                    if p < FH - 1:
                        feed(st.s0 + p + 2, i)
                    act.wait_ge(sem["h_ready"], st.at["h_ready"] + (i + (p + 1)))
                    act.activation(g_hi[:, p if isinstance(i, int) else bass.ds(i + p, 1), 0:T],
                                   h_f32[:, ps, 0:T], ACT.Copy).then_inc(sem["g_hi_ready"], 1)

                with act.Fori(0, (FH - 3) // 2) as i:
                    feed_pair = i
                    step(i * 2, 0)
                    step(i * 2, 1)
                for p in range(FH - 3, FH):
                    step(0, p)
                feed(st.s0 + FH + 1)

            def act_ffn_out(st):
                T = st.T
                act.wait_ge(*before(st, "pe"))
                act.wait_ge(*before(st, "act"))
                act.wait_ge(*before(st, "dve"))
                if st.half == 0:
                    for p in range(4):
                        ps = p % 2
                        feed(st.s0 + p + 2)
                        act.wait_ge(sem["slab_done"], st.at["slab_done"] + p + 1)
                        act.activation(Y[:, 2 * p:2 * p + 2, 0:T], PB[:, 2 * ps:2 * ps + 2, 0:T],
                                       ACT.Copy).then_inc(sem["taken_act"], 1)
                    return

                def square(m):
                    act.wait_ge(sem["y_ready"], st.at["y_ready"] + m + 1)
                    if m > NSQ:
                        act.wait_ge(sem["sum_ready"], st.at["sum_ready"] + m - NSQ)
                    to = sqsum[:, 0:T] if m == 0 else sq[:, m % NSQ, 0:T]
                    act.activation(to, Y[:, m, 0:T], ACT.Square).then_inc(sem["sq_ready"], 1)
                    if m < KT - 1:
                        act.wait_ge(sem["sq_ready"], st.at["sq_ready"] + m + 1)
                        times_gain(st, Y, Y[:, m, :], gg, m).then_inc(sem["yg_ready"], 1)
                    if m == KT - 3:
                        sqrt_table()

                for p in range(4):
                    square(2 * p)
                    if p < 3:
                        feed(st.s0 + p + 2)
                    square(2 * p + 1)

            def act_proj_y(st):
                T = st.T
                act.wait_ge(*before(st, "pe"))
                act.wait_ge(*before(st, "act"))
                act.wait_ge(*before(st, "dve"))

                def take(m):
                    bank = PA[:, m % 4, 0:T]
                    act.wait_ge(sem[("tile_done", "slab_done")[m % 2]],
                                st.at[("tile_done", "slab_done")[m % 2]] + m // 2 + 1)
                    if m > NSQ:
                        act.wait_ge(sem["sum_ready"], st.at["sum_ready"] + m - NSQ)
                    to = sqsum[:, 0:T] if m == 0 else sq[:, m % NSQ, 0:T]
                    times_gain(st, Y, PA[:, m % 4, :], gg, m).then_inc(sem["yg_ready"], 1)
                    act.activation(to, bank, ACT.Square).then_inc(sem["sq_ready"], 1)
                    if m == KT - 3:
                        sqrt_table()

                for p in range(4):
                    take(2 * p)
                    if p < 3:
                        feed(st.s0 + p + 2)
                    take(2 * p + 1)

            def act_attn(st):
                w, n = st.which, len(st.units)
                scale = dict(a=HD ** -0.5, b=HD ** -0.5, m=P ** -0.5, n=1.0)[w]
                act.wait_ge(*before(st, "pe"))
                act.wait_ge(*before(st, "act"))
                act.wait_ge(*before(st, "dve"))

                def out_hi(g):
                    act.wait_ge(sem["o_taken"], st.at["o_taken"] + g + 1)
                    act.activation(u_hi[:, g, 0:TX], qn[:, g, :], ACT.Copy)\
                       .then_inc(sem["y_hi_ready"], 1)

                for i in range(n + 2):
                    if i < n:
                        act.wait_ge(sem["negmax_ready"], st.at["negmax_ready"] + i + 1)
                        if i >= NP:
                            act.wait_ge(sem["pt_ready"], st.at["pt_ready"] + i - NP + 1)
                        for e, (_, _, off, nk) in enumerate(st.units[i]):
                            src = PA[:, i % 4, off:off + nk] if w == "m" else \
                                s_sb[:, i % NP, off:off + nk]
                            ins = act.activation(p_sb[:, i % NP, off:off + nk], src, ACT.Exp,
                                                 scale=scale, bias=nm[:, i % NP, e:e + 1],
                                                 accum_out=rs[:, i % NP, e:e + 1])
                        ins.then_inc(sem["p_ready"], 1)
                    if i >= 2:
                        j = i - 2
                        nk = width(st.units[j])
                        act.wait_ge(sem["pt_ready"], st.at["pt_ready"] + j + 1)
                        if j >= 2:
                            act.wait_ge(sem["o_ready"], st.at["o_ready"] + j - 1)
                        act.activation(pt_sb[:, j % 2, 0:nk], PB[:, 2 + j % 2, 0:nk], ACT.Copy)\
                           .then_inc(sem["pt_copied"], 1)
                    if w == "n" and i >= 5 and (i - 5) % 4 == 3:
                        out_hi((i - 5) // 4)
                act.wait_ge(sem["o_taken"], st.at["o_taken"] + st.groups)
                if w == "n":
                    out_hi(st.groups - 1)
                else:
                    b = 4 * "abm".index(w)
                    act.activation(y_hi[:, b:b + 4, :], q1[:, :, :], ACT.Copy)\
                       .then_inc(sem["y_hi_ready"], 1)

            def act_mix(st):
                nonlocal feed_pair
                act.wait_ge(*before(st, "pe"))
                act.wait_ge(*before(st, "act"))
                act.wait_ge(*before(st, "dve"))

                def step(i, p):
                    ps = p % 2
                    if p < 16:
                        feed(st.s0 + p + 2, i)
                    act.wait_ge(sem["slab_done"], st.at["slab_done"] + (i + (p + 1)))
                    if not isinstance(i, int) or p >= 2:
                        act.wait_ge(sem["up_taken"], st.at["up_taken"] + (i + (p - 1)))
                    act.activation(sig[:, ps, :], PA[:, 2 * ps, 0:TX], ACT.Sigmoid)\
                       .then_inc(sem["gate_ready"], 1)

                def merged_hi(i, m):
                    act.wait_ge(sem["merged"], st.at["merged"] + (i + (16 + m + 1)))
                    at = m if isinstance(i, int) else bass.ds(i + m, 1)
                    act.activation(mg_hi[:, at, :], merged[:, at, :], ACT.Copy)\
                       .then_inc(sem["m_hi_ready"], 1)

                step(0, 0)
                step(0, 1)
                with act.Fori(0, 7) as i:
                    feed_pair = i
                    step(i * 2, 2)
                    step(i * 2, 3)
                with act.Fori(0, 3) as i:
                    feed_pair = i
                    for p in range(2):
                        step(i * 2, 16 + p)
                        feed(st.s0 + 18 + p, i * 2)
                        merged_hi(i * 2, p)
                for p in (6, 7):
                    step(0, 16 + p)
                    feed(st.s0 + 18 + p)
                    merged_hi(0, p)


            def act_ada(st):
                act.wait_ge(*before(st, "pe"))
                act.wait_ge(*before(st, "act"))
                act.wait_ge(*before(st, "dve"))
                act.dma_start(X[:, :, TX:TT], ctx_in).then_inc(sem["ctx_in"], 16)
                act.wait_ge(sem["lam_dve"], 2)
                act.activation(lam[:, 2:3], lam[:, 0:1], ACT.Exp).then_inc(sem["lam_act"], 1)
                act.activation(lam[:, 3:4], lam[:, 1:2], ACT.Exp).then_inc(sem["lam_act"], 1)
                act.wait_ge(sem["c_zero"], 1)
                act.activation(c_f32[:, :, 64:66], vec[:, V_C:V_C + 2 * KT]
                               .rearrange("p (k v) -> p k v", v=2), ACT.Silu)\
                   .then_inc(sem["c_ready"], 1)
                act.wait_ge(sem["c_ready"], st.at["c_ready"] + 1)
                act.activation(c_split[:, :, :], c_f32[:, :, :], ACT.Copy)\
                   .then_inc(sem["c_hi_ready"], 1)

                def slabs(b, j0, j1, first):
                    for j in range(j0, j1):
                        act.wait_ge(sem[f"ada_full{j % AR}"], b * 32 + 16 * (j // AR + 1))
                        if not first or j >= AH:
                            act.wait_ge(sem["ada_used"], b * AB + (j + 1 - AH))
                        act.activation(ada_hi[j % AH][:, :], ada_raw[j % AR][:, :], ACT.Copy)\
                           .then_inc(sem["ada_hi_ready"], 1)

                def rows(b):
                    act.wait_ge(sem["ada_used"], b * AB + AB)
                    act.wait_ge(sem["mod_ready"], b + 1)
                    act.activation(ada_rows[0:96, :], PA[0:96, 0:2, :]
                                   .rearrange("p b c -> p (b c)"), ACT.Copy)\
                       .then_inc(sem["rows_copied"], 1)
                    act.wait_ge(sem["rows_copied"], b + 1)
                    for e in range(3):
                        act.dma_start(ada_turn[32 * e:32 * e + 32, :],
                                      ada_rows[32 * e:32 * e + 4, :])\
                           .then_inc(sem["rows_moved"], 16)

                slabs(0, 0, AB, True)
                with act.Fori(0, AN - 1) as i:
                    slabs(i + 1, 0, 2, False)
                    rows(i)
                    slabs(i + 1, 2, AB, False)
                rows(AN - 1)
                act.wait_ge(sem["ctx_in"], 16)

            def act_diff(st):
                n = len(st.units)
                act.wait_ge(*before(st, "pe"))
                act.wait_ge(*before(st, "act"))
                act.wait_ge(*before(st, "dve"))
                for i in range(n + 4):
                    if i < n:
                        nk, sl = TT if st.units[i][1] < 2 else TX, i % NP
                        act.wait_ge(sem["negmax_ready"], st.at["negmax_ready"] + i + 1)
                        if i >= NP:
                            act.wait_ge(sem["pt_ready"], st.at["pt_ready"] + i - NP + 1)
                        for j in range(2):
                            ins = act.activation(p2_sb[:, sl, j, 0:nk],
                                                 PA[:, 2 * (i % 2) + j, 0:nk], ACT.Exp,
                                                 scale=HD ** -0.5, bias=nm[:, sl, j:j + 1],
                                                 accum_out=rs[:, sl, j:j + 1])
                        ins.then_inc(sem["p_ready"], 1)
                    if 2 <= i < n + 2:
                        j = i - 2
                        nk = TT if st.units[j][1] < 2 else TX
                        act.wait_ge(sem["pt_ready"], st.at["pt_ready"] + j + 1)
                        if j >= 2:
                            act.wait_ge(sem["o_ready"], st.at["o_ready"] + j - 1)
                        act.activation(pt_sb[:, j % 2, 0:nk], PB[:, 2 + j % 2, 0:nk], ACT.Copy)\
                           .then_inc(sem["pt_copied"], 1)
                    if i >= 4:
                        j = i - 4
                        act.wait_ge(sem["o_taken"], st.at["o_taken"] + j + 1)
                        if j >= 1:
                            act.wait_ge(sem["o_sq_ready"], st.at["o_sq_ready"] + j)
                        act.activation(osq[:, :], on[:, j, :], ACT.Square,
                                       accum_out=ssq[:, j:j + 1]).then_inc(sem["o_sq_ready"], 1)
                act.wait_ge(sem["o_sq_ready"], st.at["o_sq_ready"] + n)
                act.activation(sroot[:, :], ssq[:, :], ACT.Sqrt, scale=1.0 / P, bias=eps[:, 0:1])\
                   .then_inc(sem["o_sqrt_ready"], 1)
                for h in range(8):
                    act.wait_ge(sem["og_ready"], st.at["og_ready"] + h + 1)
                    act.activation(u_hi[:, h, :], og[:, h % 2, :], ACT.Copy)\
                       .then_inc(sem["y_hi_ready"], 1)

            act.dma_start(cst[:, :], cst_in).then_inc(sem["consts_in"], 16)
            act.dma_start(vec[:, :], vec_in).then_inc(sem["consts_in"], 16)
            act.wait_ge(sem["ones_ready"], 8)
            sqrt_table()
            act.wait_ge(sem["consts_in"], 32)
            act.wait_ge(sem["x_in"], 16)
            act.wait_ge(sem["mem_in"], 16)
            run = dict(norm=act_norm, proj=act_proj, ffn_in=act_ffn_in, ffn_out=act_ffn_out,
                       proj_y=act_proj_y,
                       attn=act_attn, mix=act_mix, ada=act_ada, diff=act_diff)
            for st in plan:
                run[st.kind](st)

        @block.vector
        def _(dve):
            chain = Chain()

            def feed(s, i=0):
                if s >= ns:
                    return
                u, n = s % 2, sizes[s]
                dve.wait_ge(sem["w_hi_ready"], i + (s + 1))
                dve.tensor_tensor(wl[u][:, 0:n], raw[u][:, 0:n], wh[u][:, 0:n].bitcast(F32),
                                  ALU.subtract).then_inc(sem["w_split"], 1)

            def dve_norm(st):
                T, l, sub = st.T, st.l, st.sub
                nv, rows = T // TX, T // P * 32
                dve.wait_ge(*before(st, "pe"))
                dve.wait_ge(*before(st, "act"))
                dve.wait_ge(*before(st, "dve"))
                if st is plan[0]:
                    feed(0)
                dve.wait_ge(sem["sqrt_ready"], st.at["sqrt_ready"] + 1)
                dve.reciprocal(rms[0:rows, :], rms_root[0:rows, :]).then_inc(sem["rms_ready"], 1)
                dve.wait_ge(sem["r_ready"], st.at["r_ready"] + 1)

                def gain(k, v):
                    if st.apply == "plain":
                        return vec[:, V_FG + k:V_FG + k + 1]
                    if st.mod:
                        return gs[:, l, sub, k, v:v + 1]
                    c = (V_NG, V_MG)[v] + l * KT + k
                    return vec[:, c:c + 1]

                def scale(k):
                    if st.apply == "resid" or st.stat == "PB2":
                        if st.apply == "resid":
                            done = KT - (st.stat == "PA3")
                            dve.wait_ge(sem["yg_ready"], st.at["yg_ready"] - done + k + 1)
                        ins = dve.tensor_tensor(Y[:, k, 0:T], Y[:, k, 0:T],
                                                stat_bank(st)[:, 0:T], ALU.mult)
                    else:
                        for v in range(nv):
                            tok = slice(v * TX, v * TX + TX)
                            ins = dve.scalar_tensor_tensor(
                                out=Y[:, k, tok], in0=X[:, k, tok], scalar=gain(k, v),
                                in1=stat_bank(st)[:, tok], op0=ALU.mult, op1=ALU.mult)
                    ins.then_inc(sem["scaled"], 1)

                def finish(k):
                    dve.wait_ge(sem["scaled"], st.at["scaled"] + k + 1)
                    if st.apply == "resid":
                        ins = dve.tensor_tensor(X[:, k, 0:T], X[:, k, 0:T], Y[:, k, 0:T],
                                                ALU.add)
                    elif st.apply == "plain":
                        ins = dve.tensor_copy(X[:, k, 0:T], Y[:, k, 0:T])
                    else:
                        dve.wait_ge(sem["u_hi_ready"], st.at["u_hi_ready"] + k + 1)
                        if not st.mod:
                            ins = dve.tensor_tensor(u_lo[:, k, 0:T], Y[:, k, 0:T],
                                                    u_hi[:, k, 0:T].bitcast(F32), ALU.subtract)
                        else:
                            for v in range(nv):
                                tok = slice(v * TX, v * TX + TX)
                                ins = dve.scalar_tensor_tensor(
                                    out=u_lo[:, k, tok], in0=Y[:, k, tok],
                                    scalar=mod[:, l, 3 * sub, k, v:v + 1],
                                    in1=u_hi[:, k, tok].bitcast(F32), op0=ALU.add,
                                    op1=ALU.subtract)
                        ins.then_inc(sem["u_lo_ready"], 1)
                        return
                    ins.then_inc(sem["x_ready"], 1)

                scale(0)
                for k in range(1, KT):
                    scale(k)
                    finish(k - 1)
                finish(KT - 1)

            def rope(src, dst, sh, table, mask, shape, taken):
                cos = cst[:, table:table + TX]
                sin = cst[:, table + TX:table + 2 * TX]
                if len(shape) == 3:
                    cos = cos[:, None, :].broadcast_to(shape)
                    sin = sin[:, None, :].broadcast_to(shape)
                dve.stream_shuffle(sh, src, mask).then_inc(sem["chain"], chain.up())
                dve.tensor_tensor(dst, src, cos, ALU.mult).then_inc(taken, 1)
                dve.wait_ge(sem["chain"], chain.n)
                dve.tensor_tensor(sh, sh, sin, ALU.mult).then_inc(sem["chain"], chain.up())
                dve.wait_ge(sem["chain"], chain.n)
                return dve.tensor_tensor(dst, dst, sh, ALU.add)

            def index_add(st, j):
                qt, h = j // NH1, j % NH1
                nk = (qt + 1) * P
                acc, r, wgt = idx_acc[:, qt, 0:nk], relu[:, j % 2, 0:nk], wi[:, qt, h:h + 1]
                dve.wait_ge(sem["relu_ready"], st.at["relu_ready"] + j + 1)
                if h == 0:
                    ins = dve.tensor_scalar(acc, r, wgt, 0.0, ALU.mult, ALU.add)
                else:
                    dve.wait_ge(sem["acc_ready"], st.at["acc_ready"] + j)
                    ins = dve.scalar_tensor_tensor(out=acc, in0=r, scalar=wgt, in1=acc,
                                                   op0=ALU.mult, op1=ALU.add)
                ins.then_inc(sem["acc_ready"], 1)

            def topk_round(st, r):
                qt = r // 8
                nk = (qt + 1) * P
                acc = idx_acc[:, qt, 0:nk]
                causal = cst[:, C_CM + (P if qt == 0 else 0):C_CM + 2 * P]
                if r % 8 == 0:
                    dve.wait_ge(sem["acc_ready"], st.at["acc_ready"] - 8 + 8 * qt)
                    dve.tensor_tensor(acc, acc, causal, ALU.add)\
                       .then_inc(sem["chain"], chain.up())
                dve.wait_ge(sem["chain"], chain.n)
                dve.max(top8[:, :], acc).then_inc(sem["chain"], chain.up())
                dve.wait_ge(sem["chain"], chain.n)
                dve.match_replace(acc, top8[:, :], acc, TAKEN).then_inc(sem["chain"], chain.up())
                if r % 8 == TOPK // 8 - 1:
                    sel = sel_bias[:, qt, 0:nk]
                    dve.wait_ge(sem["chain"], chain.n)
                    dve.tensor_scalar(sel, acc, TAKEN, NEG, ALU.is_gt, ALU.mult)\
                       .then_inc(sem["chain"], chain.up())
                    dve.wait_ge(sem["chain"], chain.n)
                    dve.tensor_tensor(sel, sel, causal, ALU.add).then_inc(sem["topk_ready"], 1)

            def dve_proj(st):
                dve.wait_ge(*before(st, "pe"))
                dve.wait_ge(*before(st, "act"))
                dve.wait_ge(*before(st, "dve"))
                if st.late:
                    feed(st.s0 + 1)
                mask1 = [(p + 8) % 16 if p < 16 else p for p in range(32)]
                mask2 = [(p + 16) % 32 for p in range(32)]
                done = 0
                def take(i):
                    nonlocal done
                    how, to, tile, t0, T = st.steps[i]
                    ps = i % 2
                    dve.wait_ge(sem["slab_done"], st.at["slab_done"] + i + 1)
                    if done:
                        dve.wait_ge(sem["out_dve"], st.at["out_dve"] + done)
                    two = PA[:, 2 * ps:2 * ps + 2, 0:TX]
                    if how == "rope1":
                        ins = rope(two, dest[to][:, tile:tile + 2, :], shuf[:, :, :], C_R1, mask1,
                                   (P, 2, TX), sem["taken_dve"])
                    elif how == "rope2":
                        dve.tensor_copy(dest[to][:, tile:tile + 2, TX:TT],
                                        PA[:, 2 * ps:2 * ps + 2, TX:TT])\
                           .then_inc(sem["chain"], chain.up())
                        ins = rope(two, dest[to][:, tile:tile + 2, 0:TX],
                                   shuf[:, :, :], C_R2, mask2, (P, 2, TX), sem["taken_dve"])
                    elif how == "index":
                        dve.tensor_scalar(
                            wi[:, :, :], PA[:, 2 * ps, TX:TX + 2 * NH1]
                            .rearrange("p (t h) -> p t h", h=NH1), NH1 ** -0.5, None,
                            ALU.mult).then_inc(sem["chain"], chain.up())
                        ins = rope(PA[:, 2 * ps, 0:TX], ik[:, :], shuf[:, 0, :], C_R1, mask1,
                                   (P, TX), sem["taken_dve"])
                    else:
                        x = X[:, tile:tile + 2, 0:TX]
                        dve.tensor_tensor(x, x, two, ALU.add).then_inc(sem["taken_dve"], 1)
                        return
                    ins.then_inc(sem["out_dve"], 1)
                    done += 1

                for i, (how, to, tile, t0, T) in enumerate(st.steps):
                    s = st.s0 + i
                    if st.index and i:
                        for m in range(INDEX_AT[i - 1], INDEX_AT[i]):
                            index_add(st, m)
                    if st.topk:
                        for r in range(TOPK_AT[i], TOPK_AT[i + 1]):
                            topk_round(st, r)
                    if how not in ("copy", "silu", "scale", "nat"):
                        take(i)
                    feed(s + 2)

            def dve_ffn_in(st):
                T = st.T
                dve.wait_ge(*before(st, "pe"))
                dve.wait_ge(*before(st, "act"))
                dve.wait_ge(*before(st, "dve"))

                if st.late:
                    feed(st.s0 + 1)

                def step(i, p):
                    ps = p % 2
                    dve.wait_ge(sem["silu_ready"], st.at["silu_ready"] + (i + (p + 1)))
                    dve.tensor_tensor(h_f32[:, ps, 0:T], silu[:, ps, 0:T], PA[:, 2 * ps + 1, 0:T],
                                      ALU.mult).then_inc(sem["h_ready"], 1)
                    if p < FH - 1:
                        feed(st.s0 + p + 2, i)
                    dve.wait_ge(sem["g_hi_ready"], st.at["g_hi_ready"] + (i + (p + 1)))
                    at = p if isinstance(i, int) else bass.ds(i + p, 1)
                    dve.tensor_tensor(g_lo[:, at, 0:T], h_f32[:, ps, 0:T],
                                      g_hi[:, at, 0:T].bitcast(F32), ALU.subtract)\
                       .then_inc(sem["g_lo_ready"], 1)

                with dve.Fori(0, (FH - 3) // 2) as i:
                    step(i * 2, 0)
                    step(i * 2, 1)
                for p in range(FH - 3, FH):
                    step(0, p)
                feed(st.s0 + FH + 1)

            def add_up(st, m):
                T = st.T
                dve.wait_ge(sem["sq_ready"], st.at["sq_ready"] + m + 1)
                dve.wait_ge(sem["sum_ready"], st.at["sum_ready"] + m - 1)
                dve.tensor_tensor(sqsum[:, 0:T], sqsum[:, 0:T], sq[:, m % NSQ, 0:T], ALU.add)\
                   .then_inc(sem["sum_ready"], 1)

            def dve_ffn_out(st):
                T = st.T
                dve.wait_ge(*before(st, "pe"))
                dve.wait_ge(*before(st, "act"))
                dve.wait_ge(*before(st, "dve"))
                if st.half == 0:
                    for p in range(4):
                        feed(st.s0 + p + 2)
                    return

                def add(m):
                    dve.wait_ge(sem[("tile_done", "slab_done")[m % 2]],
                                st.at[("tile_done", "slab_done")[m % 2]] + m // 2 + 1)
                    dve.tensor_tensor(Y[:, m, 0:T], Y[:, m, 0:T], PB[:, m % 4, 0:T], ALU.add)\
                       .then_inc(sem["y_ready"], 1)
                    if m >= 2:
                        add_up(st, m - 1)

                for p in range(4):
                    add(2 * p)
                    add(2 * p + 1)
                    if p < 3:
                        feed(st.s0 + p + 2)

            def dve_proj_y(st):
                dve.wait_ge(*before(st, "pe"))
                dve.wait_ge(*before(st, "act"))
                dve.wait_ge(*before(st, "dve"))
                for p in range(4):
                    if p < 3:
                        feed(st.s0 + p + 2)
                    for m in (2 * p, 2 * p + 1):
                        if m >= 2:
                            add_up(st, m - 1)

            def dve_attn(st):
                w, n = st.which, len(st.units)
                per = n // st.groups
                dve.wait_ge(*before(st, "pe"))
                dve.wait_ge(*before(st, "dve"))
                if w == "b":
                    dve.wait_ge(sem["topk_ready"], st.at["topk_ready"])
                scale = dict(a=HD ** -0.5, b=HD ** -0.5, m=P ** -0.5, n=1.0)[w]

                def soft(i):
                    unit, sl, bank = st.units[i], i % NP, i % 4
                    dve.wait_ge(sem["s_ready"], st.at["s_ready"] + i + 1)
                    if i >= NP:
                        dve.wait_ge(sem["p_ready"], st.at["p_ready"] + i - NP + 1)
                    if w == "m":
                        dve.tensor_reduce(mx[:, sl, :], PA[:, bank, :]
                                          .rearrange("p (q k) -> p q k", k=TX), AX.X, ALU.max)\
                           .then_inc(sem["chain"], chain.up())
                    if w == "n":
                        dve.wait_ge(sem["bias_ready"], i + 1)
                        dve.wait_ge(sem["no_bias"], 1)
                    for e, (h, qt, off, nk) in enumerate(unit if w != "m" else ()):
                        extra = na_bias[:, i % 4, :] if w == "n" else \
                            sel_bias[:, qt, 0:nk] if w == "b" else \
                            cst[:, C_CM + TX - nk:C_CM + TX]
                        ins = dve.tensor_tensor_reduce(
                            s_sb[:, sl, off:off + nk], PA[:, bank, off:off + nk], extra,
                            1.0, 4 * NEG, ALU.add, ALU.max, mx[:, sl, e:e + 1])
                    if w != "m":
                        ins.then_inc(sem["chain"], chain.up())
                    dve.wait_ge(sem["chain"], chain.n)
                    ne = len(unit)
                    dve.tensor_scalar(nm[:, sl, 0:ne], mx[:, sl, 0:ne], -scale, None, ALU.mult)\
                       .then_inc(sem["negmax_ready"], 1)

                def normalise(j):
                    sl, ne = j % NP, len(st.units[j])
                    dve.wait_ge(sem["p_ready"], st.at["p_ready"] + j + 1)
                    dve.reciprocal(ri[:, sl, 0:ne], rs[:, sl, 0:ne])\
                       .then_inc(sem["chain"], chain.up())
                    dve.wait_ge(sem["chain"], chain.n)
                    for e, (_, _, off, nk) in enumerate(st.units[j]):
                        p_ = p_sb[:, sl, off:off + nk]
                        ins = dve.tensor_scalar(p_, p_, ri[:, sl, e:e + 1], None, ALU.mult)
                    ins.then_inc(sem["p_normed"], 1)

                def take(g):
                    if g == 0:
                        dve.wait_ge(*before(st, "act"))
                    dve.wait_ge(sem["o_ready"], st.at["o_ready"] + (per * (g + 1)))
                    o = PB[:, g % 2, 0:TX]
                    if w == "n":
                        ins = dve.tensor_copy(qn[:, g, :], o)
                    else:
                        ins = dve.tensor_tensor(q1[:, g, :], g1[:, g, :], o, ALU.mult)
                    ins.then_inc(sem["o_taken"], 1)

                def out_lo(g):
                    dve.wait_ge(sem["y_hi_ready"], st.at["y_hi_ready"] + g + 1)
                    dve.tensor_tensor(u_lo[:, g, 0:TX], qn[:, g, :],
                                      u_hi[:, g, 0:TX].bitcast(F32), ALU.subtract)\
                       .then_inc(sem["y_lo_ready"], 1)

                for i in range(n + 4):
                    if i < n:
                        soft(i)
                    if 1 <= i <= n:
                        normalise(i - 1)
                    if i >= 4 and (i - 4) % per == per - 1:
                        take((i - 4) // per)
                    if w == "n" and i >= 6 and (i - 6) % per == per - 1:
                        out_lo((i - 6) // per)
                if w == "n":
                    out_lo(st.groups - 1)
                    return
                dve.wait_ge(sem["y_hi_ready"], st.at["y_hi_ready"] + 1)
                b = 4 * "abm".index(w)
                dve.tensor_tensor(y_lo[:, b:b + 4, :], q1[:, :, :],
                                  y_hi[:, b:b + 4, :].bitcast(F32), ALU.subtract)\
                   .then_inc(sem["y_lo_ready"], 1)

            def dve_mix(st):
                dve.wait_ge(*before(st, "pe"))
                dve.wait_ge(*before(st, "act"))
                dve.wait_ge(*before(st, "dve"))

                def step(b, i, p):
                    ps, n = p % 2, 8 * b + p
                    if b < 2:
                        feed(st.s0 + n + 2, i)
                    dve.wait_ge(sem["gate_ready"], st.at["gate_ready"] + (i + (n + 1)))
                    at = p if isinstance(i, int) else bass.ds(i + p, 1)
                    if b == 0:
                        dve.tensor_tensor(upg[:, ps, :], sig[:, ps, :], PA[:, 2 * ps + 1, 0:TX],
                                          ALU.mult).then_inc(sem["up_taken"], 1)
                        dve.wait_ge(sem["up_taken"], st.at["up_taken"] + (i + (n + 1)))
                        dve.tensor_copy(merged[:, at, :], upg[:, ps, :]).then_inc(sem["merged"], 1)
                    else:
                        dve.tensor_tensor(upg[:, ps, :], sig[:, ps, :], PA[:, 2 * ps + 1, 0:TX],
                                          ALU.mult).then_inc(sem["up_taken"], 1)
                        dve.wait_ge(sem["up_taken"], st.at["up_taken"] + (i + (n + 1)))
                        dve.tensor_tensor(merged[:, at, :], merged[:, at, :], upg[:, ps, :],
                                          ALU.add).then_inc(sem["merged"], 1)

                def merged_lo(i, m):
                    dve.wait_ge(sem["m_hi_ready"], st.at["m_hi_ready"] + (i + (m + 1)))
                    at = m if isinstance(i, int) else bass.ds(i + m, 1)
                    dve.tensor_tensor(mg_lo[:, at, :], merged[:, at, :],
                                      mg_hi[:, at, :].bitcast(F32), ALU.subtract)\
                       .then_inc(sem["m_lo_ready"], 1)

                for b in range(3):
                    with dve.Fori(0, 3) as i:
                        for p in range(2):
                            step(b, i * 2, p)
                            if b == 2:
                                feed(st.s0 + 18 + p, i * 2)
                                merged_lo(i * 2, p)
                    for p in (6, 7):
                        step(b, 0, p)
                        if b == 2:
                            feed(st.s0 + 18 + p)
                            merged_lo(0, p)


            def dve_ada(st):
                dve.wait_ge(*before(st, "pe"))
                dve.wait_ge(*before(st, "act"))
                dve.wait_ge(*before(st, "dve"))
                for e in range(2):
                    a = V_LM + 2 * e * HD
                    dve.tensor_tensor_reduce(lam_tmp[:, e, :], vec[:, a:a + HD],
                                             vec[:, a + HD:a + 2 * HD], 1.0, 0.0, ALU.mult,
                                             ALU.add, lam[:, e:e + 1])\
                       .then_inc(sem["lam_dve"], 1)
                dve.tensor_scalar(sub_g[:, :], vec[:, V_SG:V_SG + 1], 1.0 - LAM_INIT, None,
                                  ALU.mult)
                dve.memset(c_f32[:, :, :], 0.0).then_inc(sem["c_zero"], 1)
                dve.wait_ge(sem["c_hi_ready"], st.at["c_hi_ready"] + 1)
                dve.tensor_tensor(c_split[:, :, 66:68], c_f32[:, :, 64:66],
                                  c_split[:, :, 64:66].bitcast(F32), ALU.subtract)\
                   .then_inc(sem["mod_ready"], 1)
                flat = mod[:, :, :, :, :].rearrange("p l m k v -> p (l m k v)")

                def slabs(b, j0, j1):
                    for j in range(j0, j1):
                        dve.wait_ge(sem["ada_hi_ready"], b * AB + (j + 1))
                        dve.tensor_tensor(ada_lo[j % AR][:, :], ada_raw[j % AR][:, :],
                                          ada_hi[j % AH][:, :].bitcast(F32), ALU.subtract)\
                           .then_inc(sem["ada_split"], 1)

                def biased(b):
                    dve.wait_ge(sem["turned"], b + 1)
                    at = bass.ds(b * 4 * AB, 4 * AB)
                    dve.tensor_tensor(flat[:, at], PA[:, 3, 0:4 * AB],
                                      vec[:, bass.ds(b * 4 * AB + V_AB, 4 * AB)], ALU.add)\
                       .then_inc(sem["mod_ready"], 1)

                slabs(0, 0, AB)
                with dve.Fori(0, AN - 1) as i:
                    slabs(i + 1, 0, 10)
                    biased(i)
                    slabs(i + 1, 10, AB)
                dve.wait_ge(sem["lam_act"], 2)
                dve.tensor_tensor(lam[:, 4:5], lam[:, 3:4], lam[:, 2:3], ALU.subtract)\
                   .then_inc(sem["lam_dve"], 1)
                dve.wait_ge(sem["lam_dve"], 3)
                dve.tensor_scalar(lam[:, 5:6], lam[:, 4:5], -LAM_INIT, None, ALU.add)\
                   .then_inc(sem["lam_dve"], 1)
                biased(AN - 1)
                dve.wait_ge(sem["mod_ready"], AN + 1)
                m = mod[:, :, :, :, :].rearrange("p l (s m) k v -> p (l s) m (k v)", m=3)
                g = vec[:, V_G2:V_G2 + 12 * KT * 2 * DEPTH // 2]\
                    .rearrange("p (s e n) -> p s e n", e=2, n=2 * KT)
                flat_gs = gs[:, :, :, :, :].rearrange("p l s k v -> p (l s) (k v)")
                flat_gg = gg[:, :, :, :, :].rearrange("p l s k v -> p (l s) (k v)")
                dve.scalar_tensor_tensor(out=flat_gs, in0=m[:, :, 1, :], scalar=1.0,
                                         in1=g[:, :, 0, :], op0=ALU.add, op1=ALU.mult)\
                   .then_inc(sem["mod_ready"], 1)
                dve.scalar_tensor_tensor(out=flat_gg, in0=m[:, :, 2, :], scalar=0.5,
                                         in1=g[:, :, 1, :], op0=ALU.mult, op1=ALU.mult)\
                   .then_inc(sem["mod_ready"], 1)
                dve.wait_ge(sem["mod_ready"], AN + 3)
                dve.tensor_scalar(gg[:, :, 1, :, :], gg[:, :, 1, :, :], 2.0, None, ALU.mult)\
                   .then_inc(sem["mod_ready"], 1)
                dve.wait_ge(sem["ctx_in"], 16)

            def dve_diff(st):
                n = len(st.units)
                dve.wait_ge(*before(st, "pe"))
                dve.wait_ge(*before(st, "act"))
                dve.wait_ge(*before(st, "dve"))

                def soft(i):
                    nk, sl = (TT if st.units[i][1] < 2 else TX), i % NP
                    dve.wait_ge(sem["s_ready"], st.at["s_ready"] + i + 1)
                    if i >= NP:
                        dve.wait_ge(sem["p_ready"], st.at["p_ready"] + i - NP + 1)
                    b = 2 * (i % 2)
                    dve.tensor_reduce(mx[:, sl, :], PA[:, b:b + 2, 0:nk], AX.X, ALU.max)\
                       .then_inc(sem["chain"], chain.up())
                    dve.wait_ge(sem["chain"], chain.n)
                    dve.tensor_scalar(nm[:, sl, :], mx[:, sl, :], -HD ** -0.5, None, ALU.mult)\
                       .then_inc(sem["negmax_ready"], 1)

                def combine(j):
                    nk, sl = (TT if st.units[j][1] < 2 else TX), j % NP
                    p_1, p_2 = p2_sb[:, sl, 0, 0:nk], p2_sb[:, sl, 1, 0:nk]
                    dve.wait_ge(sem["p_ready"], st.at["p_ready"] + j + 1)
                    if j >= 4:
                        dve.wait_ge(sem["o_taken"], st.at["o_taken"] + j - 3)
                    dve.reciprocal(ri[:, j % 4, :], rs[:, sl, :])\
                       .then_inc(sem["chain"], chain.up())
                    dve.wait_ge(sem["chain"], chain.n)
                    dve.scalar_tensor_tensor(out=rw[:, sl:sl + 1], in0=ri[:, j % 4, 1:2],
                                             scalar=lam[:, 5:6], in1=rs[:, sl, 0:1],
                                             op0=ALU.mult, op1=ALU.mult)\
                       .then_inc(sem["chain"], chain.up())
                    dve.wait_ge(sem["chain"], chain.n)
                    dve.scalar_tensor_tensor(out=p_1, in0=p_2, scalar=rw[:, sl:sl + 1], in1=p_1,
                                             op0=ALU.mult, op1=ALU.add)\
                       .then_inc(sem["p_normed"], 1)

                for i in range(n + 4):
                    if i < n:
                        soft(i)
                    if 1 <= i <= n:
                        combine(i - 1)
                    if i >= 4:
                        j = i - 4
                        dve.wait_ge(sem["o_ready"], st.at["o_ready"] + j + 1)
                        dve.tensor_scalar(on[:, j, :], PB[:, j % 2, 0:P], ri[:, j % 4, 0:1], None,
                                          ALU.mult).then_inc(sem["o_taken"], 1)
                dve.wait_ge(sem["o_sqrt_ready"], st.at["o_sqrt_ready"] + 1)
                dve.reciprocal(srec[:, :], sroot[:, :]).then_inc(sem["chain"], chain.up())
                dve.wait_ge(sem["chain"], chain.n)
                for j in range(n):
                    dve.tensor_scalar(on[:, j, :], on[:, j, :], srec[:, j:j + 1], None, ALU.mult)\
                       .then_inc(sem["o_scaled"], 1)
                for h in range(8):
                    dve.wait_ge(sem["ot_ready"], st.at["ot_ready"] + h + 1)
                    dve.tensor_scalar(og[:, h % 2, :], PA[:, h % 4, :], sub_g[:, 0:1], None,
                                      ALU.mult).then_inc(sem["og_ready"], 1)
                    dve.wait_ge(sem["y_hi_ready"], st.at["y_hi_ready"] + h + 1)
                    dve.tensor_tensor(u_lo[:, h, :], og[:, h % 2, :], u_hi[:, h, :].bitcast(F32),
                                      ALU.subtract).then_inc(sem["y_lo_ready"], 1)

            dve.memset(ones[:, :], 1.0 / D).then_inc(sem["ones_ready"], 1)
            dve.memset(eps[:, 0:1], EPS).then_inc(sem["ones_ready"], 1)
            dve.memset(eps[:, 1:2], EPS / D).then_inc(sem["ones_ready"], 1)
            dve.memset(spread[:, :, :], 0.0).then_inc(sem["ones_ready"], 1)
            dve.wait_ge(sem["ones_ready"], 4)
            for t in range(4):
                dve.memset(spread[32 * t:32 * t + 32, t, :], 1.0 / D)\
                   .then_inc(sem["ones_ready"], 1)
            dve.wait_ge(sem["consts_in"], 32)
            dve.wait_ge(sem["x_in"], 16)
            dve.wait_ge(sem["mem_in"], 16)
            run = dict(norm=dve_norm, proj=dve_proj, ffn_in=dve_ffn_in, ffn_out=dve_ffn_out,
                       proj_y=dve_proj_y,
                       attn=dve_attn, mix=dve_mix, ada=dve_ada, diff=dve_diff)
            for st in plan:
                run[st.kind](st)

        @block.gpsimd
        def _(pool):
            st = [s for s in plan if s.kind == "attn" and s.which == "n"][0]
            pool.wait_ge(*before(st, "pe"))
            pool.wait_ge(*before(st, "act"))
            pool.wait_ge(*before(st, "dve"))
            pool.memset(na_bias[:, :, TX:TT], 0.0).then_inc(sem["no_bias"], 1)

            for i in range(len(st.units)):
                pool.wait_ge(sem[f"bias_in{i % 4}"], 16 * (i // 4 + 1))
                rows = na_bias[:, i % 4, 0:TX].rearrange("p (r c) -> p r c", c=HD)
                window = cst[:, C_WM:C_WM + HD][:, None, :].broadcast_to((P, 4, HD))
                pool.tensor_tensor(rows, rows, window, ALU.add).then_inc(sem["bias_ready"], 1)


def pack(w, nk=KT):
    n = w.shape[1] // 256
    return w.reshape(nk, P, n, 256).transpose(2, 1, 0, 3).reshape(n, P, nk * 256)


def pack_ffn_in(w):
    n = D_FF // P
    return w.reshape(KT, P, 2, n, P).transpose(3, 1, 0, 2, 4).reshape(n, P, SLAB)


def pack_mix(w_mix, w_up):
    a = w_mix.reshape(KT, P, KT, P).transpose(2, 1, 0, 3)
    b = w_up.reshape(4, P, KT, P).transpose(2, 1, 0, 3)
    return np.concatenate([a, b], axis=2).reshape(KT, P, SLAB_MIX)


def lay_out(a):
    s16, s22, s12 = [], [], []
    for l in range(DEPTH):
        w = a["w_in"][l]
        col = lambda i, n=1: w[:, i * BW:(i + n) * BW]
        s16.append(pack(col(8)))
        small = np.zeros((D, 256), np.float32)
        o = 9 * BW
        small[:, 0:HD] = w[:, o:o + HD]
        small[:, HD:P] = w[:, o:o + HD]
        small[:, P:P + NH1] = w[:, o + HD:o + HD + NH1]
        s16.append(pack(small))
        s16 += [pack(col(i)) for i in range(8)]
        o += HD + NH1
        s16 += [pack(a["w_mem_kv"][l]), pack(w[:, o:o + 2 * BW])]
        o += 2 * BW
        for b in range(3):
            s12.append(pack_mix(w[:, o + b * D:o + (b + 1) * D], a["w_branch"][l, b]))
        s16.append(pack(a["w_out"][l]))
    for l in range(DEPTH):
        for f in range(2):
            s16.append(pack_ffn_in(a["ffn_w_in_2"][l, f]))
            w = a["ffn_w_out_2"][l, f]
            s22 += [pack(w[0:FH * P], FH), pack(w[FH * P:], FH)]
            if f == 0:
                m = ("da", "na")[l]
                s16 += [pack(a[f"{m}_w_in_2"][0]), pack(a[f"{m}_w_out_2"][0])]
    cols = lambda v: v.reshape(-1, P).T
    two = lambda v: np.repeat(cols(v), 2, axis=1)
    vec = np.concatenate([
        cols(a["norm_g"]), cols(a["mem_norm_g"]), cols(a["final_g"]), two(a["norm_g_2"]),
        two(a["ada_b_2"]), cols(a["da_subln_g_2"]),
        np.stack([cols(a["c_2"]), cols(a["c_ctx_2"])], axis=2).reshape(P, 2 * KT),
        np.broadcast_to(a["da_lambda_2"].reshape(1, -1), (P, 4 * HD))], axis=1)
    rpb = np.zeros((16, 15, 127), np.float32)
    rpb[:, :, 48:79] = a["na_rpb_2"][0]
    bias = np.empty((P, 16, 2, 4, HD), np.float32)
    for p in range(P):
        for i in range(2):
            r, c = 2 * i + p // HD, p % HD
            bias[p, :, i] = rpb[:, 7 - r:11 - r, 63 - c:127 - c]
    tr = lambda t: t.reshape(TX, KT, P).transpose(2, 1, 0)
    return dict(x=tr(a["x"]), mem=tr(a["mem"]), ctx=tr(a["ctx_2"]), vec=vec, cst=constants(),
                bias=bias.reshape(P, 16, 2, TX), w16=np.concatenate(s16), w22=np.concatenate(s22),
                w12=np.concatenate(s12),
                ada=np.concatenate([pack(w) for w in a["ada_w_2"]]))


def constants():
    t = np.arange(TX, dtype=np.float32)
    c = np.zeros((P, NC), np.float32)
    c[:, C_ID:C_ID + P] = np.eye(P)
    f1 = (np.float32(500000.0) ** (-np.arange(8, dtype=np.float32) / np.float32(8)))
    f1 = f1.astype(np.float32)
    f2 = (np.float32(10000.0) ** (-np.arange(16, dtype=np.float32) / np.float32(16)))
    f2 = f2.astype(np.float32)
    for p in range(P):
        d = p % HD
        cos, sin = np.ones(TX), np.zeros(TX)
        if d < 16:
            ang = (t * f1[d % 8]).astype(np.float32)
            cos, sin = np.cos(ang), np.sin(ang) * (-1 if d < 8 else 1)
        c[p, C_R1:C_R1 + TX], c[p, C_R1 + TX:C_R1 + 2 * TX] = cos, sin
        pos = (np.arange(TX) // 64 if d < 32 else np.arange(TX) % 64).astype(np.float32)
        ang = (pos * f2[d % 16]).astype(np.float32)
        c[p, C_R2:C_R2 + TX] = np.cos(ang)
        c[p, C_R2 + TX:C_R2 + 2 * TX] = np.sin(ang) * (-1 if d % 32 < 16 else 1)
        c[p, C_CM + P:C_CM + 2 * P] = np.where(np.arange(P) <= p, 0.0, NEG)
        start = min(max(d - 8, 0), HD - 16)
        k = np.arange(HD)
        c[p, C_WM:C_WM + HD] = np.where((k >= start) & (k < start + 16), 0.0, -1e9)
    for e in range(3):
        for v in range(4):
            for g in range(4):
                for n in range(2):
                    c[32 * e + 8 * v + 2 * g + n, C_TU + 2 * (6 * g + 2 * e + n) + v % 2] = 1.0
    return c


def kernel(**inputs):
    import concourse.bacc as bacc
    from concourse.bass_utils import run_bass_kernel_spmd

    a = {k: np.asarray(v) for k, v in inputs.items() if not k.startswith("rw_")}
    laid = {k: np.ascontiguousarray(v) for k, v in lay_out(a).items()}
    nc = bacc.Bacc("TRN2", target_bir_lowering=False, num_devices=1)
    args = {k: nc.dram_tensor(f"in_{k}", v.shape, F32, kind="ExternalInput").ap()
            for k, v in laid.items()}
    out = nc.dram_tensor("out", (P, KT, TX), F32, kind="ExternalOutput").ap()
    build(nc, args["x"], args["mem"], args["ctx"], args["vec"], args["cst"], args["bias"],
          args["w16"], args["w22"], args["w12"], args["ada"], out)
    r = run_bass_kernel_spmd(nc, [{f"in_{k}": v for k, v in laid.items()}], core_ids=[0])
    got = r.results[0]["out"]
    return np.ascontiguousarray(got.transpose(2, 1, 0)).reshape(1, TX, D)
```
